# Optimizing a Trainium2 kernel written in Bass

```python
import numpy as np
import jax
import jax.numpy as jnp
from jax import lax
import math
import jax, jax.numpy as jnp

D_MODEL = 1024
BATCH = 1
SEQ = 256
DEPTH = 1

NSA_HEADS = 8
NSA_KV_GROUPS = 2
NSA_GROUP = NSA_HEADS // NSA_KV_GROUPS
NSA_HEAD_DIM = 64
ROPE_DIM = NSA_HEAD_DIM // 4
ROPE_THETA = 500000.0
CMP_BLOCK = 32
CMP_STRIDE = 16
CMP_HIDDEN = 256
SLC_BLOCK = 64
SLC_TOPK = 16
WINDOW = 512
Q_BLOCK = 128

RET_HEADS = 4
RET_QK_DIM = 128
RET_V_DIM = 256
RET_CHUNK = 128
RET_ROPE_THETA = 10000.0

D_FF = 2816
CONV_WIDTH = 3

EPS = 1e-6
NEG = -1e30

NSA_Q_W = NSA_HEADS * NSA_HEAD_DIM
NSA_KV_W = NSA_KV_GROUPS * NSA_HEAD_DIM
RET_QK_W = RET_HEADS * RET_QK_DIM
RET_V_W = RET_HEADS * RET_V_DIM
IN_SPLITS = (NSA_Q_W, 6 * NSA_KV_W, 3 * NSA_HEADS, RET_QK_W, RET_QK_W, RET_V_W, RET_V_W, 2 * D_MODEL)
IN_PROJ_W = sum(IN_SPLITS)


def rms_norm(x, w):
    xf = x.astype(jnp.float32)
    y = xf * lax.rsqrt(jnp.mean(xf * xf, axis=-1, keepdims=True) + EPS)
    return (y * w.astype(jnp.float32)).astype(x.dtype)

def rope(x, rot_dim, theta):
    S = x.shape[1]
    half = rot_dim // 2
    inv = jnp.power(jnp.float32(theta), -jnp.arange(half, dtype=jnp.float32) / half)
    ang = jnp.arange(S, dtype=jnp.float32)[:, None] * inv[None, :]
    cos = jnp.cos(ang)[None, :, None, :]
    sin = jnp.sin(ang)[None, :, None, :]
    xr = x[..., :rot_dim].astype(jnp.float32)
    x1, x2 = xr[..., :half], xr[..., half:]
    rot = jnp.concatenate([x1 * cos - x2 * sin, x1 * sin + x2 * cos], axis=-1).astype(x.dtype)
    return jnp.concatenate([rot, x[..., rot_dim:]], axis=-1)

def masked_softmax(s, mask):
    p = jax.nn.softmax(jnp.where(mask, s, NEG), axis=-1)
    return jnp.where(mask, p, 0.0)

def nsa_attention(q, k_cmp, v_cmp, k_slc, v_slc, k_win, v_win, gates,
                  pe_k, w1_k, w2_k, pe_v, w1_v, w2_v):
    B, S = q.shape[0], q.shape[1]
    H, G, dh = NSA_KV_GROUPS, NSA_GROUP, NSA_HEAD_DIM
    scale = dh ** -0.5
    pos = jnp.arange(S)
    qg = q.reshape(B, S, H, G, dh)

    n_cmp = (S - CMP_BLOCK) // CMP_STRIDE + 1
    cmp_start = np.arange(n_cmp) * CMP_STRIDE
    cmp_idx = cmp_start[:, None] + np.arange(CMP_BLOCK)[None, :]

    def compress(t, pe, w1, w2):
        blk = t[:, cmp_idx] + pe[:, None, :]
        blk = jnp.swapaxes(blk, 2, 3).reshape(B, n_cmp, H, CMP_BLOCK * dh)
        return jax.nn.gelu(blk @ w1) @ w2

    kc = compress(k_cmp, pe_k, w1_k, w2_k)
    vc = compress(v_cmp, pe_v, w1_v, w2_v)
    s_cmp = jnp.einsum('bshgd,bchd->bhgsc', qg, kc).astype(jnp.float32) * scale
    mask_cmp = jnp.asarray(cmp_start + CMP_BLOCK - 1)[None, :] <= pos[:, None]
    p_cmp = masked_softmax(s_cmp, mask_cmp)
    o_cmp = jnp.einsum('bhgsc,bchd->bshgd', p_cmp.astype(vc.dtype), vc)

    n_slc = S // SLC_BLOCK
    slc_start = np.arange(n_slc) * SLC_BLOCK
    overlap = np.clip(np.minimum(cmp_start[:, None] + CMP_BLOCK, slc_start[None, :] + SLC_BLOCK)
                      - np.maximum(cmp_start[:, None], slc_start[None, :]), 0, None) / CMP_BLOCK
    imp = jnp.einsum('bhgsc,cj->bhsj', p_cmp, jnp.asarray(overlap, dtype=jnp.float32))
    cur = (pos // SLC_BLOCK)[:, None]
    jb = jnp.arange(n_slc)[None, :]
    forced = (jb == 0) | (jb == cur) | (jb == cur - 1)
    valid = jb <= cur
    imp = jnp.where(forced, jnp.inf, jnp.where(valid, imp, -jnp.inf))
    top_n = min(SLC_TOPK, n_slc)
    _, sel = lax.top_k(imp, top_n)

    k_blocks = jnp.swapaxes(k_slc.reshape(B, n_slc, SLC_BLOCK, H, dh), 1, 3)
    k_blocks = jnp.swapaxes(k_blocks, 2, 3)
    v_blocks = jnp.swapaxes(jnp.swapaxes(v_slc.reshape(B, n_slc, SLC_BLOCK, H, dh), 1, 3), 2, 3)
    n_q = S // Q_BLOCK
    q_chunks = jnp.moveaxis(qg.reshape(B, n_q, Q_BLOCK, H, G, dh), 1, 0)
    sel_chunks = jnp.moveaxis(sel.reshape(B, H, n_q, Q_BLOCK, top_n), 2, 0)
    pos_chunks = pos.reshape(n_q, Q_BLOCK)
    gather = jax.vmap(jax.vmap(lambda blocks, ix: blocks[ix]))

    def selected_block(args):
        qb, ib, tb = args
        kg = gather(k_blocks, ib)
        vg = gather(v_blocks, ib)
        s = jnp.einsum('bqhgd,bhqnkd->bhgqnk', qb, kg).astype(jnp.float32) * scale
        kpos = ib[..., None] * SLC_BLOCK + jnp.arange(SLC_BLOCK)
        mask = (kpos <= tb[None, None, :, None, None]).reshape(B, H, 1, Q_BLOCK, top_n * SLC_BLOCK)
        p = masked_softmax(s.reshape(B, H, G, Q_BLOCK, top_n * SLC_BLOCK), mask)
        return jnp.einsum('bhgqm,bhqmd->bqhgd', p.astype(vg.dtype),
                          vg.reshape(B, H, Q_BLOCK, top_n * SLC_BLOCK, dh))

    o_slc = lax.map(selected_block, (q_chunks, sel_chunks, pos_chunks))
    o_slc = jnp.moveaxis(o_slc, 0, 1).reshape(B, S, H, G, dh)

    kw = jnp.pad(k_win, ((0, 0), (WINDOW, 0), (0, 0), (0, 0)))
    vw = jnp.pad(v_win, ((0, 0), (WINDOW, 0), (0, 0), (0, 0)))
    band_len = Q_BLOCK + WINDOW
    band = np.arange(n_q)[:, None] * Q_BLOCK + np.arange(band_len)[None, :]
    kb = kw[:, band]
    vb = vw[:, band]
    qb = qg.reshape(B, n_q, Q_BLOCK, H, G, dh)
    s_win = jnp.einsum('bnqhgd,bnkhd->bnhgqk', qb, kb).astype(jnp.float32) * scale
    qi = np.arange(Q_BLOCK)[:, None]
    ki = np.arange(band_len)[None, :]
    k_abs = np.arange(n_q)[:, None, None] * Q_BLOCK + ki[None] - WINDOW
    win_mask = ((ki > qi) & (ki <= qi + WINDOW))[None] & (k_abs >= 0)
    p_win = masked_softmax(s_win, jnp.asarray(win_mask)[None, :, None, None])
    o_win = jnp.einsum('bnhgqk,bnkhd->bnqhgd', p_win.astype(vb.dtype), vb).reshape(B, S, H, G, dh)

    g = gates.reshape(B, S, H, G, 3)
    o = g[..., 0:1] * o_cmp + g[..., 1:2] * o_slc + g[..., 2:3] * o_win
    return o.reshape(B, S, NSA_HEADS * dh)

def retention(q, k, v):
    B, S, H, dk = q.shape
    dv = v.shape[-1]
    C = RET_CHUNK
    n = S // C
    f32 = jnp.float32
    q = rope(q, dk, RET_ROPE_THETA).astype(f32)
    k = rope(k, dk, RET_ROPE_THETA).astype(f32) * (dk ** -0.5)
    v = v.astype(f32)
    log_gamma = jnp.log1p(-jnp.exp2(-5.0 - jnp.arange(H, dtype=f32)))
    idx = jnp.arange(C, dtype=f32)
    diff = idx[:, None] - idx[None, :]
    decay_in = jnp.where(diff >= 0, jnp.exp(log_gamma[:, None, None] * jnp.maximum(diff, 0.0)), 0.0)
    q_decay = jnp.exp(log_gamma[None, :] * (idx[:, None] + 1.0))
    k_decay = jnp.exp(log_gamma[None, :] * (C - 1.0 - idx[:, None]))
    chunk_decay = jnp.exp(log_gamma * C)
    qc = q.reshape(B, n, C, H, dk)
    kc = k.reshape(B, n, C, H, dk)
    vc = v.reshape(B, n, C, H, dv)
    scores = jnp.einsum('bnihd,bnjhd->bnhij', qc, kc) * decay_in
    o_inner = jnp.einsum('bnhij,bnjhe->bnihe', scores, vc)

    def step(state, xs):
        qn, kn, vn = xs
        cross = jnp.einsum('bihd,bhde->bihe', qn, state) * q_decay[None, :, :, None]
        state = state * chunk_decay[None, :, None, None] + jnp.einsum(
            'bjhd,bjhe->bhde', kn * k_decay[None, :, :, None], vn)
        return state, cross

    state0 = jnp.zeros((B, H, dk, dv), f32)
    _, o_cross = lax.scan(step, state0, (jnp.moveaxis(qc, 1, 0), jnp.moveaxis(kc, 1, 0), jnp.moveaxis(vc, 1, 0)))
    o = o_inner + jnp.moveaxis(o_cross, 0, 1)
    return o.reshape(B, S, H, dv)

def head_group_norm(o, w):
    mean = jnp.mean(o, axis=-1, keepdims=True)
    var = jnp.mean(jnp.square(o - mean), axis=-1, keepdims=True)
    return (o - mean) * lax.rsqrt(var + EPS) * w.astype(jnp.float32)

def causal_dwconv(u, w, b):
    S = u.shape[1]
    up = jnp.pad(u, ((0, 0), (CONV_WIDTH - 1, 0), (0, 0)))
    y = b
    for j in range(CONV_WIDTH):
        y = y + w[j] * up[:, j:j + S]
    return y

def first_inputs(seed: int = 0) -> dict:
    key = jax.random.key(seed)
    ks = jax.random.split(key, 20)
    f32 = jnp.float32
    L = DEPTH

    def nrm(k, shape, fan_in):
        return jax.random.normal(k, shape, f32) * (fan_in ** -0.5)

    def gain(k, shape):
        return 1.0 + 0.02 * jax.random.normal(k, shape, f32)

    return {
        'x': jax.random.normal(ks[0], (BATCH, SEQ, D_MODEL), f32),
        'norm_mix_w': gain(ks[1], (L, D_MODEL)),
        'w_in': nrm(ks[2], (L, D_MODEL, IN_PROJ_W), D_MODEL),
        'cmp_pe_k': 0.02 * jax.random.normal(ks[3], (L, CMP_BLOCK, NSA_HEAD_DIM), f32),
        'cmp_w1_k': nrm(ks[4], (L, CMP_BLOCK * NSA_HEAD_DIM, CMP_HIDDEN), CMP_BLOCK * NSA_HEAD_DIM),
        'cmp_w2_k': nrm(ks[5], (L, CMP_HIDDEN, NSA_HEAD_DIM), CMP_HIDDEN),
        'cmp_pe_v': 0.02 * jax.random.normal(ks[6], (L, CMP_BLOCK, NSA_HEAD_DIM), f32),
        'cmp_w1_v': nrm(ks[7], (L, CMP_BLOCK * NSA_HEAD_DIM, CMP_HIDDEN), CMP_BLOCK * NSA_HEAD_DIM),
        'cmp_w2_v': nrm(ks[8], (L, CMP_HIDDEN, NSA_HEAD_DIM), CMP_HIDDEN),
        'w_nsa_branch': nrm(ks[9], (L, NSA_Q_W, D_MODEL), NSA_Q_W),
        'ret_gn_w': gain(ks[10], (L, RET_HEADS, RET_V_DIM)),
        'w_ret_branch': nrm(ks[11], (L, RET_V_W, D_MODEL), RET_V_W),
        'w_mix_out': nrm(ks[12], (L, D_MODEL, D_MODEL), D_MODEL),
        'norm_ffn_w': gain(ks[13], (L, D_MODEL)),
        'w_ffn_up': nrm(ks[14], (L, D_MODEL, 2 * D_FF), D_MODEL),
        'ffn_conv_w': nrm(ks[15], (L, CONV_WIDTH, 2 * D_FF), CONV_WIDTH),
        'ffn_conv_b': 0.01 * jax.random.normal(ks[16], (L, 2 * D_FF), f32),
        'w_ffn_down': nrm(ks[17], (L, D_FF, D_MODEL), D_FF),
        'norm_final_w': gain(ks[18], (D_MODEL,)),
    }

def first_block(x, norm_mix_w, w_in, cmp_pe_k, cmp_w1_k, cmp_w2_k, cmp_pe_v, cmp_w1_v, cmp_w2_v,
              w_nsa_branch, ret_gn_w, w_ret_branch, w_mix_out, norm_ffn_w, w_ffn_up, ffn_conv_w,
              ffn_conv_b, w_ffn_down, norm_final_w):
    B, S, _ = x.shape
    split_at = [int(v) for v in np.cumsum(IN_SPLITS)[:-1]]
    for layer in range(DEPTH):
        h = rms_norm(x, norm_mix_w[layer])
        proj = h @ w_in[layer]
        q_nsa, kv_nsa, g_nsa, q_ret, k_ret, v_ret, g_ret, g_merge = jnp.split(proj, split_at, axis=-1)

        q_nsa = rope(q_nsa.reshape(B, S, NSA_HEADS, NSA_HEAD_DIM), ROPE_DIM, ROPE_THETA)
        kv = kv_nsa.reshape(B, S, 6, NSA_KV_GROUPS, NSA_HEAD_DIM)
        k_cmp, v_cmp = kv[:, :, 0], kv[:, :, 1]
        k_slc = rope(kv[:, :, 2], ROPE_DIM, ROPE_THETA)
        v_slc = kv[:, :, 3]
        k_win = rope(kv[:, :, 4], ROPE_DIM, ROPE_THETA)
        v_win = kv[:, :, 5]
        nsa_gates = jax.nn.sigmoid(g_nsa.reshape(B, S, NSA_HEADS, 3))
        o_a = nsa_attention(q_nsa, k_cmp, v_cmp, k_slc, v_slc, k_win, v_win, nsa_gates,
                            cmp_pe_k[layer], cmp_w1_k[layer], cmp_w2_k[layer],
                            cmp_pe_v[layer], cmp_w1_v[layer], cmp_w2_v[layer])
        y_a = o_a @ w_nsa_branch[layer]

        o_r = retention(q_ret.reshape(B, S, RET_HEADS, RET_QK_DIM),
                        k_ret.reshape(B, S, RET_HEADS, RET_QK_DIM),
                        v_ret.reshape(B, S, RET_HEADS, RET_V_DIM))
        o_r = head_group_norm(o_r, ret_gn_w[layer]) * jax.nn.silu(
            g_ret.reshape(B, S, RET_HEADS, RET_V_DIM).astype(jnp.float32))
        y_b = o_r.astype(x.dtype).reshape(B, S, RET_V_W) @ w_ret_branch[layer]

        gate_a, gate_b = jnp.split(jax.nn.sigmoid(g_merge), 2, axis=-1)
        x = x + (gate_a * y_a + gate_b * y_b) @ w_mix_out[layer]

        h = rms_norm(x, norm_ffn_w[layer])
        u = causal_dwconv(h @ w_ffn_up[layer], ffn_conv_w[layer], ffn_conv_b[layer])
        u_gate, u_val = jnp.split(u, 2, axis=-1)
        x = x + (jax.nn.silu(u_gate) * u_val) @ w_ffn_down[layer]
    return rms_norm(x, norm_final_w)


DEPTH_2 = 2

N_HEADS_A = 8
D_COMP_A = 32
D_V_A = 2 * D_COMP_A
WIDTH_A = N_HEADS_A * D_V_A
ROPE_DIMS = D_COMP_A // 4
WIDTH_B = 512
CONV_WIDTH_2 = 31
N_GROUPS_C = 4
GROUP_C = 128
WIDTH_C = N_GROUPS_C * GROUP_C
N_BRANCH = 3
IN_WIDTH = 3 * WIDTH_A + 2 * WIDTH_B + WIDTH_C
D_FF_2 = -(-8 * D_MODEL // (3 * 256)) * 256


def rmsnorm(x, g):
    xf = x.astype(jnp.float32)
    y = xf * lax.rsqrt(jnp.mean(xf * xf, axis=-1, keepdims=True) + EPS)
    return (y * g.astype(jnp.float32)).astype(x.dtype)

def layernorm(x, g, b):
    xf = x.astype(jnp.float32)
    mu = jnp.mean(xf, axis=-1, keepdims=True)
    var = jnp.mean(jnp.square(xf - mu), axis=-1, keepdims=True)
    y = (xf - mu) * lax.rsqrt(var + EPS)
    return (y * g.astype(jnp.float32) + b.astype(jnp.float32)).astype(x.dtype)

def rope_tables(seq):
    pos = jnp.arange(seq, dtype=jnp.float32)
    inv = 1.0 / (ROPE_THETA ** (jnp.arange(0, ROPE_DIMS, 2, dtype=jnp.float32) / ROPE_DIMS))
    ang = pos[:, None] * inv[None, :]
    return jnp.cos(ang), jnp.sin(ang)

def apply_partial_rope(t, cos, sin):
    half = ROPE_DIMS // 2
    c = cos[None, :, None, None, :].astype(t.dtype)
    s = sin[None, :, None, None, :].astype(t.dtype)
    r1 = t[..., :half]
    r2 = t[..., half:ROPE_DIMS]
    rest = t[..., ROPE_DIMS:]
    return jnp.concatenate([r1 * c - r2 * s, r2 * c + r1 * s, rest], axis=-1)

def diff_attention(q, k, v, lam):
    b, s = q.shape[0], q.shape[1]
    nb = s // Q_BLOCK
    qb = q.reshape(b, nb, Q_BLOCK, N_HEADS_A, 2, D_COMP_A).transpose(1, 0, 2, 3, 4, 5)
    vf = v.astype(jnp.float32)
    scale = D_COMP_A ** -0.5

    def block(qi):
        sc = jnp.einsum('bqhcd,bkhcd->bhcqk', qi, k,
                        preferred_element_type=jnp.float32) * scale
        p = jax.nn.softmax(sc, axis=-1)
        w = p[:, :, 0] - lam * p[:, :, 1]
        return jnp.einsum('bhqk,bkhe->bqhe', w, vf)

    out = lax.map(block, qb)
    return out.transpose(1, 0, 2, 3, 4).reshape(b, s, N_HEADS_A, D_V_A).astype(v.dtype)

def second_inputs(seed: int = 0) -> dict:
    key = jax.random.key(seed)
    ks = jax.random.split(key, 24)
    f32 = jnp.float32
    L, D = DEPTH_2, D_MODEL

    def nrm(k, shape, scale):
        return jax.random.normal(k, shape, f32) * scale

    return {
        'x': nrm(ks[0], (BATCH, SEQ, D), 1.0),
        'norm1_g': 1.0 + nrm(ks[1], (L, D), 0.02),
        'w_in': nrm(ks[2], (L, D, IN_WIDTH), D ** -0.5),
        'qnorm_g': 1.0 + nrm(ks[3], (L, D_COMP_A), 0.02),
        'knorm_g': 1.0 + nrm(ks[4], (L, D_COMP_A), 0.02),
        'lambda_q1': nrm(ks[5], (L, D_COMP_A), 0.1),
        'lambda_k1': nrm(ks[6], (L, D_COMP_A), 0.1),
        'lambda_q2': nrm(ks[7], (L, D_COMP_A), 0.1),
        'lambda_k2': nrm(ks[8], (L, D_COMP_A), 0.1),
        'subln_g': 1.0 + nrm(ks[9], (L, D_V_A), 0.02),
        'w_proj_a': nrm(ks[10], (L, WIDTH_A, D), WIDTH_A ** -0.5),
        'conv_w': nrm(ks[11], (L, CONV_WIDTH_2, WIDTH_B), CONV_WIDTH_2 ** -0.5),
        'conv_b': nrm(ks[12], (L, WIDTH_B), 0.02),
        'conv_ln_g': 1.0 + nrm(ks[13], (L, WIDTH_B), 0.02),
        'conv_ln_b': nrm(ks[14], (L, WIDTH_B), 0.02),
        'w_proj_b': nrm(ks[15], (L, WIDTH_B, D), WIDTH_B ** -0.5),
        'w_proj_c': nrm(ks[16], (L, WIDTH_C, D), WIDTH_C ** -0.5),
        'w_gate': nrm(ks[17], (L, D, N_BRANCH * D), D ** -0.5),
        'b_gate': nrm(ks[18], (L, N_BRANCH * D), 0.02),
        'w_out': nrm(ks[19], (L, D, D), D ** -0.5),
        'norm2_g': 1.0 + nrm(ks[20], (L, D), 0.02),
        'w_ffn_in': nrm(ks[21], (L, D, 2 * D_FF_2), D ** -0.5),
        'w_ffn_out': nrm(ks[22], (L, D_FF_2, D), D_FF_2 ** -0.5),
    }

def second_block(x, norm1_g, w_in, qnorm_g, knorm_g, lambda_q1, lambda_k1, lambda_q2, lambda_k2,
              subln_g, w_proj_a, conv_w, conv_b, conv_ln_g, conv_ln_b, w_proj_b, w_proj_c,
              w_gate, b_gate, w_out, norm2_g, w_ffn_in, w_ffn_out):
    b, s, d = x.shape
    cos, sin = rope_tables(s)
    for l in range(DEPTH_2):
        h = rmsnorm(x, norm1_g[l])
        u = h @ w_in[l]
        o = 0
        q = u[..., o:o + WIDTH_A].reshape(b, s, N_HEADS_A, 2, D_COMP_A); o += WIDTH_A
        k = u[..., o:o + WIDTH_A].reshape(b, s, N_HEADS_A, 2, D_COMP_A); o += WIDTH_A
        v = u[..., o:o + WIDTH_A].reshape(b, s, N_HEADS_A, D_V_A); o += WIDTH_A
        glu_in = u[..., o:o + 2 * WIDTH_B]; o += 2 * WIDTH_B
        four_in = u[..., o:o + WIDTH_C]

        q = apply_partial_rope(rmsnorm(q, qnorm_g[l]), cos, sin)
        k = apply_partial_rope(rmsnorm(k, knorm_g[l]), cos, sin)
        lam_init = 0.8 - 0.6 * math.exp(-0.3 * l)
        lam = (jnp.exp(jnp.sum(lambda_q1[l].astype(jnp.float32) * lambda_k1[l].astype(jnp.float32)))
               - jnp.exp(jnp.sum(lambda_q2[l].astype(jnp.float32) * lambda_k2[l].astype(jnp.float32)))
               + lam_init)
        att = diff_attention(q, k, v, lam)
        att = rmsnorm(att, subln_g[l]) * (1.0 - lam_init)
        y_a = att.reshape(b, s, WIDTH_A) @ w_proj_a[l]

        ga, gb = jnp.split(glu_in, 2, axis=-1)
        g = ga * jax.nn.sigmoid(gb)
        cv = lax.conv_general_dilated(
            g, conv_w[l].reshape(CONV_WIDTH_2, 1, WIDTH_B), window_strides=(1,),
            padding=[((CONV_WIDTH_2 - 1) // 2, (CONV_WIDTH_2 - 1) // 2)],
            dimension_numbers=('NWC', 'WIO', 'NWC'), feature_group_count=WIDTH_B)
        cv = layernorm(cv + conv_b[l], conv_ln_g[l], conv_ln_b[l])
        y_b = jax.nn.silu(cv) @ w_proj_b[l]

        fc = four_in.astype(jnp.float32).reshape(b, s, N_GROUPS_C, GROUP_C)
        fr = jnp.fft.fft2(fc, axes=(1, 3), norm='ortho').real.astype(x.dtype)
        y_c = fr.reshape(b, s, WIDTH_C) @ w_proj_c[l]

        gates = jax.nn.sigmoid(h @ w_gate[l] + b_gate[l]).reshape(b, s, N_BRANCH, d)
        merged = gates[:, :, 0] * y_a + gates[:, :, 1] * y_b + gates[:, :, 2] * y_c
        x = x + merged @ w_out[l]

        h2 = rmsnorm(x, norm2_g[l])
        f_gate, f_up = jnp.split(h2 @ w_ffn_in[l], 2, axis=-1)
        x = x + (jax.nn.silu(f_gate) * f_up) @ w_ffn_out[l]
    return x


def setup_inputs(seed=0):
    out = dict(first_inputs(seed))
    for name, value in second_inputs(seed + 1).items():
        if name != "x":
            out[name + "_2"] = value
    return out


def reference(
    x, norm_mix_w, w_in, cmp_pe_k, cmp_w1_k, cmp_w2_k, cmp_pe_v, cmp_w1_v, cmp_w2_v,
    w_nsa_branch, ret_gn_w, w_ret_branch, w_mix_out, norm_ffn_w, w_ffn_up, ffn_conv_w,
    ffn_conv_b, w_ffn_down, norm_final_w, norm1_g_2, w_in_2, qnorm_g_2, knorm_g_2, lambda_q1_2,
    lambda_k1_2, lambda_q2_2, lambda_k2_2, subln_g_2, w_proj_a_2, conv_w_2, conv_b_2,
    conv_ln_g_2, conv_ln_b_2, w_proj_b_2, w_proj_c_2, w_gate_2, b_gate_2, w_out_2, norm2_g_2,
    w_ffn_in_2, w_ffn_out_2,
):
    x = first_block(
        x, norm_mix_w, w_in, cmp_pe_k, cmp_w1_k, cmp_w2_k, cmp_pe_v, cmp_w1_v, cmp_w2_v,
        w_nsa_branch, ret_gn_w, w_ret_branch, w_mix_out, norm_ffn_w, w_ffn_up, ffn_conv_w,
        ffn_conv_b, w_ffn_down, norm_final_w,
    )
    return second_block(
        x, norm1_g_2, w_in_2, qnorm_g_2, knorm_g_2, lambda_q1_2, lambda_k1_2, lambda_q2_2,
        lambda_k2_2, subln_g_2, w_proj_a_2, conv_w_2, conv_b_2, conv_ln_g_2, conv_ln_b_2,
        w_proj_b_2, w_proj_c_2, w_gate_2, b_gate_2, w_out_2, norm2_g_2, w_ffn_in_2, w_ffn_out_2,
    )


_drawn_inputs = setup_inputs


def setup_inputs(seed=0):
    import zlib

    import numpy as np

    out = dict(_drawn_inputs(seed))
    spreads = {}
    factors = {'cmp_pe_k': 8.0,
     'cmp_pe_v': 8.0,
     'ret_gn_w': 6.322,
     'norm_ffn_w': 2.777,
     'ffn_conv_b': 4.691,
     'qnorm_g_2': 5.899,
     'knorm_g_2': 6.627,
     'lambda_q1_2': 8.0,
     'lambda_q2_2': 5.48,
     'subln_g_2': 6.386,
     'conv_b_2': 3.434,
     'conv_ln_g_2': 5.611,
     'conv_ln_b_2': 6.351,
     'b_gate_2': 8.0,
     'norm2_g_2': 3.185}
    for name, (base, spread) in spreads.items():
        noise = np.random.default_rng([zlib.crc32(name.encode()), seed]).standard_normal(out[name].shape)
        drawn = base * np.exp(spread * noise) if base else spread * noise
        out[name] = jnp.asarray(drawn.astype(out[name].dtype))
    for name, factor in factors.items():
        out[name] = (out[name] * factor).astype(out[name].dtype)
    return out
```

```python
import math
from contextlib import ExitStack

import numpy as np

import concourse.bass as bass
from concourse import mybir

F32 = mybir.dt.float32
R32 = mybir.dt.float32r
BF16 = mybir.dt.bfloat16
ALU = mybir.AluOpType
ACT = mybir.ActivationFunctionType
AXX = mybir.AxisListType.X

D = 1024
S = 256
EPS = 1e-6
NEG = -1e30
FF = 2816
NFT = FF // 128
CW = 2048
NRAW, NHL, AHEAD = 4, 3, 2


def cols(*spans):
    return [c for a, n in spans for c in range(a, a + n)]


def chunk_plan():
    plan = []

    def wide(name, layer, cs, nk, per, split=True):
        for k in range(0, nk, per):
            plan.append((name, layer, cs, k, per, split))

    def in1(a, n):
        wide("w_in", 0, cols((a, n)), 8, 4)

    wide("w_in", 0, cols(*[(64 * h, 64) for h in (0, 4, 1, 5, 2, 6, 3, 7)]), 8, 4)
    in1(512, 512)
    in1(1024, 280)
    wide("cmp_w1_k", 0, cols((0, 256)), 16, 8, False)
    wide("cmp_w1_v", 0, cols((0, 256)), 16, 8, False)
    for a in range(1304, 4376, 512):
        in1(a, 512)
    for f in range(8):
        wide("w_in", 0, cols((4376 + 256 * f, 256)), 8, 8)
    for f in range(2):
        wide("w_nsa_branch", 0, cols((512 * f, 512)), 4, 4)
    for f in range(4):
        wide("w_ret_branch", 0, cols((256 * f, 256)), 8, 8)
    for f in range(2):
        wide("w_mix_out", 0, cols((512 * f, 512)), 8, 4)
    for f in range(NFT):
        wide("w_ffn_up", 0, cols((128 * f, 128), (FF + 128 * f, 128)), 8, 8)
    wide("w_ffn_down", 0, cols((0, 1024)), NFT, 2)
    for l in range(2):
        qk = [64 * h + 32 * c + d for c in range(2) for h in range(8) for d in range(32)]
        wide("w_in_2", l, qk, 8, 4)
        wide("w_in_2", l, [512 + c for c in qk], 8, 4)
        wide("w_in_2", l, cols((1024, 512)), 8, 4)
        for f in range(4):
            wide("w_in_2", l, cols((1536 + 128 * f, 128), (2048 + 128 * f, 128)), 8, 8)
        wide("w_in_2", l, cols((2560, 512)), 8, 4)
        for f in range(12):
            wide("w_gate_2", l, cols((256 * f, 256)), 8, 8)
        for n in "abc":
            for f in range(2):
                wide(f"w_proj_{n}_2", l, cols((512 * f, 512)), 4, 4)
        for f in range(2):
            wide("w_out_2", l, cols((512 * f, 512)), 8, 4)
        for f in range(NFT):
            wide("w_ffn_in_2", l, cols((128 * f, 128), (FF + 128 * f, 128)), 8, 8)
        wide("w_ffn_out_2", l, cols((0, 1024)), NFT, 2)
    return plan


SMALL = [
    ("ident", 128), ("ones", 128), ("ropen", 64), ("madd", 32), ("m01", 32), ("bm", 8),
    ("w2k", 128), ("w2v", 128), ("pe", 32), ("fconv", 4 * 2 * NFT),
    ("lam", 256), ("qkg", 128), ("subg", 128), ("cw", 248), ("cvec", 24), ("bg", 48), ("rope4", 32),
    ("mhalf", 16),
]
SOFF, _n = {}, 0
for _name, _w in SMALL:
    SOFF[_name] = (_n, _w)
    _n += _w
NSMALL = _n


class Token:

    def __init__(self, sem, count):
        self.sem, self.count = sem, count


class Queue:

    def __init__(self, engine, sem, linked=False):
        self.linked = linked
        self.engine, self.sem, self.count, self.waited, self.prev = engine, sem, 0, {}, None

    def wait(self, tokens):
        for t in tokens:
            if t is not None and self.waited.get(t.sem.num, 0) < t.count:
                self.waited[t.sem.num] = t.count
                self.engine.wait_ge(t.sem, t.count)

    def do(self, after, make):
        if self.linked:
            self.wait([self.last()])
        self.quiet(after, make)
        return self.mark()

    def quiet(self, after, make):
        self.wait(after)
        self.prev = make(self.engine)

    def mark(self):
        self.prev.then_inc(self.sem, 1)
        self.count += 1
        return self.last()

    def dma(self, after, sem, count, make):
        self.wait(after)
        make(self.engine).then_inc(sem, 16)
        return Token(sem, count)

    def last(self):
        return Token(self.sem, self.count)


def program(nc, wts, small, tabs, rows, x_in, out):
    ctx = ExitStack()
    with ctx:
        base = 16640
        used = [0]

        def at(name, kb, shape, dt=F32):
            n = int(np.prod(shape[1:])) * (2 if dt == BF16 else 4)
            assert base + int(kb * 1024) + n <= 229344, name
            return nc.alloc_sbuf_tensor_at(name, shape, dt, offset=base + int(kb * 1024))

        def sem(name):
            return ctx.enter_context(nc.semaphore(name))

        raw = [at(f"raw{i}", 8 * i, [128, CW]) for i in range(NRAW)]
        whi = [at(f"whi{i}", 32 + 8 * i, [128, CW], R32) for i in range(NHL)]
        wlo = [at(f"wlo{i}", 56 + 8 * i, [128, CW], R32) for i in range(NHL)]
        x = at("x", 80, [128, 2, D])
        hhi = at("hhi", 88, [128, 8, S], R32)
        hlo = at("hlo", 96, [128, 8, S], R32)
        gain = at("gain", 104, [128, D])
        sm = at("sm", 108, [128, NSMALL])
        P0 = 108 + (NSMALL * 4 + 1023) // 1024
        idb = at("idb", P0, [128, 128], BF16)
        mkb = at("mkb", P0 + 0.25, [128, 128], BF16)
        st = at("st", P0 + 0.5, [128, 512])
        P = P0 + 2.5
        assert P <= 119, P

        def smv(name):
            a, n = SOFF[name]
            return sm[:, a:a + n]

        ident, ones = smv("ident"), smv("ones")

        PS = [ctx.enter_context(nc.psum_tensor(f"ps{i}", [128, 512], F32)) for i in range(8)]
        PB = PS[0:4]
        SC, TP, OB = PS[4:6], PS[6], PS[7]

        pe, act, dve, pool, sp = (Queue(e, sem(n), n in ("s_act", "s_dve", "s_pool")) for e, n in (
            (nc.tensor, "s_pe"), (nc.scalar, "s_act"), (nc.vector, "s_dve"), (nc.gpsimd, "s_pool"),
            (nc.sync, "s_sp")))

        def everything():
            return [pe.last(), act.last(), dve.last(), pool.last()]

        def load(name, dst, src, after=()):
            s = sem(name)
            return sp.dma(after, s, 16, lambda e: e.dma_start(dst, src))

        t_x = [load(f"d_x{t}", x[:, t, :], x_in[t * 128:(t + 1) * 128, :]) for t in range(2)]
        t_sm = load("d_sm", sm[:, :], small)
        gain_sem = sem("d_gain")
        gain_n = [0]

        def load_gain(i, after):
            gain_n[0] += 1
            src = rows[i:i + 1, :].partition_broadcast(128) if False else rows[i:i + 1, :].to_broadcast([128, D])
            return sp.dma(after, gain_sem, 16 * gain_n[0], lambda e: e.dma_start(gain[:, :], src))

        t_gain = load_gain(0, [])

        plan = chunk_plan()
        offs, n = [], 0
        for _, _, cs, _, kk, _ in plan:
            offs.append(n)
            n += 128 * kk * len(cs)
        raw_sem = [sem(f"d_w{i}") for i in range(NRAW)]
        raw_free = {}
        landed, split, hl_free = {}, {}, {}
        nxt = {"dma": 0, "split": 0, "use": 0}

        def run_dmas():
            while nxt["dma"] < len(plan):
                i = nxt["dma"]
                if i >= NRAW and i - NRAW not in raw_free:
                    return
                w = plan[i][4] * len(plan[i][2])
                src = wts[offs[i]:offs[i] + 128 * w].rearrange("(p n) -> p n", p=128)
                dst = raw[i % NRAW][:, 0:w]
                landed[i] = sp.dma(raw_free.get(i - NRAW, []), raw_sem[i % NRAW], 16 * (i // NRAW + 1),
                                   lambda e, dst=dst, src=src: e.dma_start(dst, src))
                nxt["dma"] += 1

        def run_splits(upto):
            while nxt["split"] <= min(upto, len(plan) - 1):
                run_dmas()
                i = nxt["split"]
                nxt["split"] += 1
                if not plan[i][5]:
                    continue
                w = plan[i][4] * len(plan[i][2])
                r, h, l = raw[i % NRAW][:, 0:w], whi[i % NHL][:, 0:w], wlo[i % NHL][:, 0:w]
                free = hl_free.get(i - NHL, [])
                t1 = act.do([landed[i], *free], lambda e: e.activation(h, r, ACT.Copy))
                t2 = dve.do([landed[i], t1, *free],
                            lambda e: e.tensor_tensor(l, r, h.bitcast(F32), ALU.subtract))
                split[i] = [t1, t2]
                raw_free[i] = [t1, t2]
                run_dmas()

        def take():
            i = nxt["use"]
            nxt["use"] += 1
            run_splits(i + AHEAD)
            kk, ncol = plan[i][4], len(plan[i][2])
            v = [t[:, 0:kk * ncol].rearrange("p (k n) -> p k n", k=kk)
                 for t in (raw[i % NRAW], whi[i % NHL], wlo[i % NHL])]
            return i, v

        def taken(i, token):
            hl_free[i] = [token]
            if not plan[i][5]:
                raw_free[i] = [token]
                run_dmas()

        bank_free = {}
        turn = [0]

        def bank():
            b = turn[0] % 4
            turn[0] += 1
            return b

        def mm3(out, sh, sl, mh, ml, start, stop, after=()):
            pe.quiet(after, lambda e: e.matmul(out, sh, mh, start=start, stop=False, skip_group_check=True))
            pe.quiet([], lambda e: e.matmul(out, sh, ml, start=False, stop=False, skip_group_check=True))
            make = lambda e: e.matmul(out, sl, mh, start=False, stop=stop, skip_group_check=True)
            if stop:
                return pe.do([], make)
            pe.quiet([], make)

        def rows_out(hi, lo, ready, evac):
            b = [bank(), bank()]
            for c in range(2):
                i, (_, wh, wl) = take()
                kk, ncol = plan[i][4], len(plan[i][2])
                for k in range(kk):
                    kg = c * kk + k
                    toks = []
                    for tt in range(2):
                        o = PB[b[tt]][:, 0:ncol]
                        sl = slice(tt * 128, tt * 128 + 128)
                        after = list(split[i]) + (ready if kg == 0 else [])
                        if kg == 0:
                            after += bank_free.get(b[tt], [])
                        toks.append(mm3(o, hi[:, kg, sl], lo[:, kg, sl], wh[:, k, :], wl[:, k, :],
                                        kg == 0, kg == 7, after))
                    if k == kk - 1:
                        tk = toks[1] if kg == 7 else pe_mark()
                        taken(i, tk)
                    if kg == 7:
                        for tt in range(2):
                            bank_free[b[tt]] = evac(tt, PB[b[tt]][:, 0:ncol], toks[tt])
                    yield

        def pe_mark():
            return pe.mark()

        def feats_out(hi, lo, nk, ready, evac):
            i, (_, wh, wl) = take()
            npair = len(plan[i][2]) // 256
            for p in range(npair):
                b = bank()
                toks = None
                for k in range(nk):
                    for f in range(2):
                        o = PB[b][:, f * S:f * S + S]
                        c = p * 256 + f * 128
                        first = k == 0 and f == 0
                        after = list(split[i]) + (ready if first else [])
                        if first:
                            after += bank_free.get(b, [])
                        wsh, wsl = wh[:, k, c:c + 128], wl[:, k, c:c + 128]
                        pe.quiet(after, lambda e, o=o, a=wsh, m=hi[:, k, :], s=first: e.matmul(
                            o, a, m, start=s, stop=False, skip_group_check=True))
                        pe.quiet([], lambda e, o=o, a=wsh, m=lo[:, k, :]: e.matmul(
                            o, a, m, start=False, stop=False, skip_group_check=True))
                        pe.quiet([], lambda e, o=o, a=wsl, m=hi[:, k, :], s=(k == nk - 1): e.matmul(
                            o, a, m, start=False, stop=s, skip_group_check=True))
                    if k == nk - 1:
                        toks = pe_mark()
                        if p == npair - 1:
                            taken(i, toks)
                        bank_free[b] = evac(p, PB[b][:, :].rearrange("p (f s) -> p f s", f=2), toks)
                    yield

        def run(g):
            for _ in g:
                pass

        def chain(*gs):
            for g in gs:
                yield from g

        def weave(front, back, n):
            for _ in front:
                for _ in range(n):
                    next(back, None)
            run(back)

        def halves(dst_hi, dst_lo, src, after):
            a = act.do(after, lambda e: e.activation(dst_hi, src, ACT.Copy))
            b = dve.do([a, *after], lambda e: e.tensor_tensor(dst_lo, src, dst_hi.bitcast(F32), ALU.subtract))
            return [a, b]

        def mul(q, after, o, a, b):
            return q.do(after, lambda e: e.tensor_tensor(o, a, b, ALU.mult))

        def add(q, after, o, a, b):
            return q.do(after, lambda e: e.tensor_tensor(o, a, b, ALU.add))

        def scal(q, after, o, a, s1, s2, op0, op1):
            return q.do(after, lambda e: e.tensor_scalar(o, a, s1, s2, op0, op1))

        def power(after, o, a):
            n = a.shape[-1]
            return pool.do([t_sm, *after], lambda e: e.tensor_tensor(o, a, smv("mhalf")[:, 0:n], ALU.pow))

        def copy(q, after, o, a):
            if q is act:
                return act.do(after, lambda e: e.activation(o, a, ACT.Copy))
            return q.do(after, lambda e: e.tensor_copy(o, a))

        def transposed(after, o, i, n=128):
            idt = ident[0:n, 0:n]
            return pe.do([t_sm, *after], lambda e: e.transpose(o, i, idt))

        def mm(after, o, a, b, start=True, stop=True):
            return pe.do(after, lambda e: e.matmul(o, a, b, start=start, stop=stop, skip_group_check=True))

        def bc(ap, shape, ax):
            return ap.unsqueeze(ax).to_broadcast(shape)

        t_c = [copy(dve, [t_sm], idb[:, :], ident)]
        t_m0 = pool.do([], lambda e: e.memset(mkb[:, :], 0.0))
        t_mk = pool.do([t_m0], lambda e: e.affine_select(
            out=mkb[:, :], in_=mkb[:, :], compare_op=ALU.is_ge, fill=NEG, base=0,
            pattern=[[-1, 128]], channel_multiplier=1))

        xn = [at(f"xn{t}", P + 48 + 4 * t, [128, D]) for t in range(2)]
        norm_used = [[]]

        def norm(gi, ready, final=False):
            nonlocal t_gain
            busy = everything()
            out_t = []
            for tt in range(2):
                ss = st[:, tt:tt + 1]
                ms = st[:, 2 + tt:3 + tt]
                rs = st[:, 4 + tt:5 + tt]
                xt = x[:, tt, :]
                if tt == 0:
                    a = act.do(ready[tt] + busy, lambda e: e.activation(
                        xn[tt][:, :], xt, ACT.Square, accum_out=ss))
                else:
                    a = dve.do(ready[tt] + busy, lambda e: e.tensor_tensor_reduce(
                        out=xn[tt][:, :], in0=xt, in1=xt, scale=1.0, scalar=0.0,
                        op0=ALU.mult, op1=ALU.add, accum_out=ss))
                b = scal(dve, [a], ms, ss, 1.0 / D, EPS, ALU.mult, ALU.add)
                c = power([b], rs, ms)
                o = xt if final else xn[tt][:, :]
                d = dve.do([c, a, t_gain], lambda e: e.scalar_tensor_tensor(
                    o, xt, rs, gain[:, :], ALU.mult, ALU.mult))
                out_t.append(d)
            t_gain = load_gain(gi + 1, out_t) if gi < 6 else None
            if final:
                return [[out_t[0]], [out_t[1]]]
            done = []
            for tt in range(2):
                for half in range(2):
                    b = bank()
                    for j in range(4):
                        k = half * 4 + j
                        t = transposed([out_t[tt], *(bank_free.get(b, []) if j == 0 else [])],
                                       PB[b][:, j * 128:j * 128 + 128], xn[tt][:, k * 128:k * 128 + 128])
                    dst = slice(half * 4, half * 4 + 4), slice(tt * 128, tt * 128 + 128)
                    h = halves(hhi[:, dst[0], dst[1]], hlo[:, dst[0], dst[1]],
                               PB[b][:, :].rearrange("p (k s) -> p k s", k=4), [t, *busy])
                    bank_free[b] = h
                    done += h
            return done

        run_splits(AHEAD)

        def add_to_x(col):
            def evac(tt, ps, t):
                xs = x[:, tt, col:col + 512]
                d = add(dve, [t], xs, ps, xs)
                x_done[tt].append(d)
                return [d]
            return evac

        x_done = [[], []]

        def to_halves_T(src, nblk, dhi, dlo, after):
            res = []
            for tt in range(2):
                for g in range(nblk // 4):
                    b = bank()
                    for j in range(4):
                        k = g * 4 + j
                        t = transposed([*after[tt], *(bank_free.get(b, []) if j == 0 else [])],
                                       PB[b][:, j * 128:j * 128 + 128], src[tt][:, k * 128:k * 128 + 128])
                    h = halves(dhi[:, g * 4:g * 4 + 4, tt * 128:tt * 128 + 128],
                               dlo[:, g * 4:g * 4 + 4, tt * 128:tt * 128 + 128],
                               PB[b][:, :].rearrange("p (k s) -> p k s", k=4), [t])
                    bank_free[b] = h
                    res += h
            return res

        oah = at("oah", P, [128, 4, S], R32)
        oal = at("oal", P + 4, [128, 4, S], R32)
        N0 = P + 8
        qkv = [at(f"qkv{t}", N0 + 5.25 * t, [128, 1304]) for t in range(2)]
        qT = at("qT", N0 + 10.5, [128, 4, S])
        kT = at("kT", N0 + 14.5, [128, 2, S])
        Ex = [at(f"Ex{i}", N0 + 16.5 + 2 * i, [128, 2, S]) for i in range(2)]
        ET = [at(f"ET{i}", N0 + 20.5 + 2 * i, [128, 4, 128]) for i in range(2)]
        oa = [at(f"oa{t}", N0 + 24.5 + 2 * t, [128, 512]) for t in range(2)]
        Tm = at("Tm", N0 + 28.5, [128, 512])
        Sw = at("Sw", N0 + 30.5, [128, 2, 16, 31])
        Hs = at("Hs", N0 + 34.5, [128, 128])
        Hg = at("Hg", N0 + 35, [128, 2, 2, 32])
        Hr = at("Hr", N0 + 35.5, [128, 2, 120])
        kcT = at("kcT", N0 + 36.5, [128, 16])
        VC = at("VC", N0 + 36.75, [128, 8, 64])
        cs_ = at("cs_", N0 + 38.75, [128, 8, 15])
        cp = at("cp", N0 + 39.25, [128, 120])
        cpT = at("cpT", N0 + 39.75, [128, 128])
        rt = at("rt", N0 + 40.25, [128, 16])
        R0 = N0 + 41
        qrT = at("qrT", R0, [128, 4, S])
        krT = at("krT", R0 + 4, [128, 4, S])
        vr = [at(f"vr{t}", R0 + 8 + 4 * t, [128, D]) for t in range(2)]
        sg = at("sg", R0 + 16, [128, 2, D])
        ra = at("ra", R0 + 24, [128, 512])
        rb = at("rb", R0 + 26, [128, 512])
        gnw = at("gnw", R0 + 24, [128, D])
        dec = at("dec", R0 + 28, [128, 4, 384])
        STt = [at(f"STt{i}", R0 + 34 + 1.5 * i, [128, 384]) for i in range(2)]
        ctab = at("ctab", R0 + 37, [128, 2, 256])
        gm = at("gm", N0, [128, 16, S])
        orh = at("orh", N0 + 16, [128, 8, S], R32)
        orl = at("orl", N0 + 24, [128, 8, S], R32)
        orr = [at(f"orr{t}", N0 + 32 + 4 * t, [128, D]) for t in range(2)]
        mh = at("mh", R0, [128, 8, S], R32)
        ml = at("ml", R0 + 8, [128, 8, S], R32)
        mg = at("mg", R0 + 16, [128, 8, S])

        t_h = norm(0, [[t_x[0]], [t_x[1]]])
        t_dec = load("d_dec", dec[:, :, :], tabs["dec"], t_h)
        t_ctab = load("d_ctab", ctab[:, :, :], tabs["ctab"], t_h)

        gt = st[:, 64:112].rearrange("p (t n) -> p t n", t=2)
        ropen = smv("ropen").rearrange("p (t a n) -> p t a n", t=2, a=2)

        def rope_small(q, v, shape, tt, table, half, tmp1, tmp2, after):
            full = [*shape[:-1], 2 * half]
            cosb, sinb = table[:, tt, 0, :], table[:, tt, 1, :]
            for ax in range(len(shape) - 2):
                cosb, sinb = cosb.unsqueeze(1), sinb.unsqueeze(1)
            lo_, hi_ = [slice(None)] * (len(shape) - 1) + [slice(0, half)], None
            lo_ = tuple(lo_)
            hi_ = tuple([slice(None)] * (len(shape) - 1) + [slice(half, 2 * half)])
            hs = [*shape[:-1], half]
            a = mul(q, after, tmp1, v, cosb.to_broadcast(full))
            b = mul(q, after, tmp2[lo_], v[hi_], sinb[lo_].to_broadcast(hs))
            c = mul(q, after, tmp2[hi_], v[lo_], sinb[hi_].to_broadcast(hs))
            return add(q, [a, b, c], v, tmp1, tmp2)

        def r4(ap, a, b):
            return ap.rearrange("p (a b c) -> p a b c", a=a, b=b)

        tq, tk1, tk2 = {}, {}, {}

        def evac_q(tt, ps, t):
            a = act.do([t], lambda e: e.activation(qkv[tt][:, 0:512], ps, ACT.Copy, scale=0.125))
            v = qkv[tt][:, 0:512].rearrange("p (h d) -> p h d", h=8)[:, :, 0:16]
            t1, t2 = (st[:, o:o + 128].rearrange("p (h d) -> p h d", h=8) for o in (128, 256))
            tq[tt] = rope_small(dve, v, [128, 8, 16], tt, ropen, 8, t1, t2, [a])
            return [a]

        def evac_kv1(tt, ps, t):
            tk1[tt] = copy(act, [t], qkv[tt][:, 512:1024], ps)
            return [tk1[tt]]

        def evac_kv2(tt, ps, t):
            a = copy(act, [t], qkv[tt][:, 1024:1304], ps)
            v = qkv[tt][:, 768:1280].rearrange("p (a g d) -> p a g d", a=2, g=4)[:, :, 0:2, 0:16]
            t1, t2 = (st[:, o:o + 64].rearrange("p (a g d) -> p a g d", a=2, g=2) for o in (128, 256))
            tk2[tt] = rope_small(dve, v, [128, 2, 2, 16], tt, ropen, 8, t1, t2, [a, tk1[tt], tq[tt]])
            b = copy(dve, [a], gt[:, tt, :], qkv[tt][:, 1280:1304])
            tg.append(b)
            return [a]

        tg = []
        run(chain(rows_out(hhi, hlo, t_h, evac_q), rows_out(hhi, hlo, [], evac_kv1),
                  rows_out(hhi, hlo, [], evac_kv2)))
        tg = [act.do(tg, lambda e: e.activation(st[:, 64:112], st[:, 64:112], ACT.Sigmoid))]

        tqT = []
        for tt in range(2):
            b = bank()
            for j in range(4):
                t = transposed([tq[tt], *bank_free.get(b, [])], PB[b][:, j * 128:j * 128 + 128],
                               qkv[tt][:, j * 128:j * 128 + 128])
            c = copy(act, [t], qT[:, :, tt * 128:tt * 128 + 128], PB[b][:, :].rearrange("p (k s) -> p k s", k=4))
            bank_free[b] = [c]
            tqT.append(c)
            b = bank()
            for j in range(2):
                o = 768 + 256 * j
                t = transposed([tk2[tt], *bank_free.get(b, [])], PB[b][:, j * 128:j * 128 + 128],
                               qkv[tt][:, o:o + 128])
            c = copy(dve, [t], kT[:, :, tt * 128:tt * 128 + 128],
                     PB[b][:, 0:256].rearrange("p (k s) -> p k s", k=2))
            bank_free[b] = [c]
            tqT.append(c)

        X2 = TP[:, :].rearrange("p (v g s) -> p v g s", v=2, g=2)
        for kv in range(2):
            for g in range(2):
                for tt in range(2):
                    for par in range(2):
                        o = X2[par * 64:par * 64 + 64, kv, g, tt * 64:tt * 64 + 64]
                        src = qkv[tt][:, 512 + kv * 128 + g * 64:512 + kv * 128 + g * 64 + 64]
                        sel = ident.rearrange("p (s e) -> p e s", e=2)[:, par, :]
                        t = mm([tk1[tt]], o, src, sel)
        tS = []
        for kv in range(2):
            for half in range(2):
                o = Sw[:, kv, half * 8:half * 8 + 8, 0:30].rearrange("p j (g c) -> p j g c", g=2)
                i = X2[:, kv, :, half * 8:half * 8 + 120].rearrange("p g (c j) -> p j g c", j=8)
                tS.append(copy(dve, [t], o, i))
            pev = smv("pe").rearrange("p (v j) -> p v j", v=2)[:, kv, :]
            tS.append(copy(dve, [t], Sw[:, kv, :, 30], pev))
        Hp = SC[0][:, 0:128].rearrange("p (v h c) -> p v h c", v=2, h=2)
        for kv in range(2):
            for c in range(2):
                i, (w1, _, _) = take()
                for j in range(8):
                    for half in range(2):
                        t = mm([landed[i], *tS], Hp[:, kv, half, 0:31], w1[:, j, half * 128:half * 128 + 128],
                               Sw[:, kv, c * 8 + j, :], start=(c == 0 and j == 0 and half == 0),
                               stop=(c == 1 and j == 7))
                taken(i, t)
        tH = copy(dve, [t], Hs[:, :].rearrange("p (v h c) -> p v h c", v=2, h=2)[:, :, :, 0:31], Hp[:, :, :, 0:31])
        Hsv = Hs[:, :].rearrange("p (v h c) -> p v h c", v=2, h=2)
        for kv in range(2):
            for half in range(2):
                tG = act.do([tH], lambda e, a=Hg[:, kv, half, 0:30], b=Hsv[:, kv, half, 0:30],
                            c=Hsv[:, kv, half, 30:31]: e.activation(a, b, ACT.Gelu_apprx_tanh, bias=c))
        w2 = [smv(n).rearrange("p (h d) -> p h d", h=2) for n in ("w2k", "w2v")]
        for g in range(2):
            for half in range(2):
                t = mm([tG, tH], SC[1][g * 64:g * 64 + 64, 0:15], w2[0][:, half, :],
                       Hg[:, 0, half, g * 15:g * 15 + 15], start=(half == 0), stop=(half == 1))
        tkc = copy(dve, [t], kcT[:, 0:15], SC[1][:, 0:15])
        for half in range(2):
            tr = copy(dve, [tG], Hr[:, half, :].rearrange("p (g r c) -> p g r c", g=2, r=4),
                      bc(Hg[:, 1, half, 0:30].rearrange("p (g c) -> p g c", g=2), [128, 2, 4, 15], 2))
        for half in range(2):
            t = mm([tr, tS[-1]], TP[0:120, 0:64], Hr[:, half, :], w2[1][:, half, :],
                   start=(half == 0), stop=(half == 1))
        bm = smv("bm")[0:120, :]
        tvc = dve.do([t], lambda e: e.tensor_tensor(
            VC[0:120, :, :], bc(TP[0:120, 0:64], [120, 8, 64], 1), bc(bm, [120, 8, 64], 2), ALU.mult))
        sc_free, tp_free, ob_free = [[tH], [tkc]], [tvc], []

        lsum = st[:, 32:48].rearrange("p (h a) -> p h a", a=2)
        toa = {}

        def nsa():
            nonlocal tp_free, ob_free
            units = [(tt, h) for tt in range(2) for h in range(8)]
            exp_t, tr_t, ev_t, pv_t, ls = {}, {}, {}, {}, {}
            lw = st[:, 384:416].rearrange("p (t h a) -> p t h a", t=2, a=2)
            nm = st[:, 416:448].rearrange("p (t h a) -> p t h a", t=2, a=2)
            wq = st[:, 448:480].rearrange("p (t h a) -> p t h a", t=2, a=2)
            gates = gt.rearrange("p t (h c) -> p t h c", c=3)

            def compressed(tt):
                nonlocal tp_free, ob_free
                for g in range(2):
                    for b in range(4):
                        t = mm([*tqT, tkc, *sc_free[g]], SC[g][:, b * 16:b * 16 + 15],
                               qT[g * 64:g * 64 + 64, b, tt * 128:tt * 128 + 128],
                               kcT[g * 64:g * 64 + 64, 0:15])
                madd = smv("madd").rearrange("p (t c) -> p t c", t=2)[:, tt, 0:15]
                m01 = smv("m01").rearrange("p (t c) -> p t c", t=2)[:, tt, 0:15]
                prev = [pe.last()]
                a = []
                for g in range(2):
                    a.append(dve.do([t, *prev], lambda e, g=g: e.tensor_tensor(
                        cs_[:, g * 4:g * 4 + 4, :], SC[g][:, 0:64].rearrange("p (h c) -> p h c", c=16)[:, :, 0:15],
                        bc(madd, [128, 4, 15], 1), ALU.add)))
                    sc_free[g] = [a[-1]]
                mx, l, r = rt[:, 0:8], st[:, 480:488], st[:, 488:496]
                b_ = dve.do(a, lambda e: e.tensor_reduce(mx, cs_[:, :, :], AXX, ALU.max))
                c_ = dve.do([b_], lambda e: e.tensor_tensor(cs_[:, :, :], cs_[:, :, :], bc(mx, [128, 8, 15], 2),
                                                            ALU.subtract))
                d_ = act.do([c_], lambda e: e.activation(cs_[:, :, :], cs_[:, :, :], ACT.Exp))
                yield
                f_ = dve.do([d_], lambda e: e.tensor_reduce(l, cs_[:, :, :], AXX, ALU.add))
                g_ = dve.do([f_], lambda e: e.reciprocal(r, l))
                h_ = mul(dve, [g_, *tg], r, r, gates[:, tt, :, 0])
                p3 = cp[:, :].rearrange("p (h c) -> p h c", h=8)
                i_ = mul(dve, [d_, *prev], p3, cs_[:, :, :], bc(m01, [128, 8, 15], 1))
                t = transposed([i_, *tp_free], TP[0:120, 0:128], cp[:, :])
                yield
                j_ = copy(act, [t], cpT[0:120, :], TP[0:120, 0:128])
                tp_free = [j_]
                t = mm([j_, tvc, *ob_free], OB[:, :], cpT[0:120, :], VC[0:120, :, :])
                yield
                toa[tt] = dve.do([t, h_], lambda e: e.tensor_tensor(
                    oa[tt][:, :].rearrange("p (h d) -> p h d", h=8), OB[:, :].rearrange("p (h d) -> p h d", h=8),
                    bc(r, [128, 8, 64], 2), ALU.mult))
                ob_free = [toa[tt]]

            def scores(u):
                tt, h = units[u]
                g, b = h // 4, h % 4
                n = 128 * (tt + 1)
                bk = SC[u % 2]
                for a in range(2):
                    mm([*tqT, *sc_free[u % 2]], bk[:, a * S:a * S + n],
                       qT[g * 64:g * 64 + 64, b, tt * 128:tt * 128 + 128], kT[g * 64:g * 64 + 64, a, 0:n],
                       start=(a == 0), stop=False)
                for a in range(2):
                    t = mm([t_c[0], t_mk], bk[:, a * S + n - 128:a * S + n], idb[:, :], mkb[:, :],
                           start=False, stop=True)
                s = bk[:, :].rearrange("p (a k) -> p a k", a=2)
                m = dve.do([t], lambda e: e.tensor_reduce(nm[:, tt, h, :], s[:, :, 0:n], AXX, ALU.max, negate=True))
                for a in range(2):
                    x_ = act.do([m, *tr_t.get(u - 2, [])], lambda e, a=a: e.activation(
                        Ex[u % 2][:, a, 0:n], s[:, a, 0:n], ACT.Exp, bias=nm[:, tt, h, a:a + 1],
                        accum_out=lw[:, tt, h, a:a + 1]))
                exp_t[u] = [x_]
                sc_free[u % 2] = [x_]

            def turned(u):
                nonlocal tp_free
                tt, h = units[u]
                nk = tt + 1
                for a in range(2):
                    for k in range(nk):
                        t = transposed([*exp_t[u], *tp_free], TP[:, (a * nk + k) * 128:(a * nk + k) * 128 + 128],
                                       Ex[u % 2][:, a, k * 128:k * 128 + 128])
                tr_t[u] = [t]
                ev_t[u] = copy(act if u % 2 else dve, [t, *pv_t.get(u - 2, [])], ET[u % 2][:, 0:2 * nk, :],
                               TP[:, 0:2 * nk * 128].rearrange("p (k s) -> p k s", k=2 * nk))
                tp_free = [ev_t[u]]

            def values(u):
                nonlocal ob_free
                tt, h = units[u]
                g, nk = h // 4, tt + 1
                for a in range(2):
                    for k in range(nk):
                        t = mm([ev_t[u], *ob_free], OB[:, ((h % 4) * 2 + a) * 64:((h % 4) * 2 + a) * 64 + 64],
                               ET[u % 2][:, a * nk + k, :],
                               qkv[k][:, 896 + 256 * a + 64 * g:896 + 256 * a + 64 * g + 64],
                               start=(k == 0), stop=(k == nk - 1))
                pv_t[u] = [t]
                if h % 4 == 3:
                    hs = slice(h - 3, h + 1)
                    r_ = dve.do(exp_t[u], lambda e: e.reciprocal(wq[:, tt, hs, :], lw[:, tt, hs, :]))
                    w_ = mul(dve, [r_, *tg], wq[:, tt, hs, :], wq[:, tt, hs, :], gates[:, tt, hs, 1:3])
                    o8 = lambda ap: ap.rearrange("p (h d) -> p h d", d=64)
                    m_ = dve.do([w_, t], lambda e: e.tensor_tensor(
                        o8(Tm[:, :]), o8(OB[:, :]),
                        bc(wq[:, tt, hs, :].rearrange("p h a -> p (h a)"), [128, 8, 64], 2), ALU.mult))
                    ob_free = [m_]
                    dst = oa[tt][:, (h - 3) * 64:(h + 1) * 64].rearrange("p (h d) -> p h d", d=64)
                    T4 = Tm[:, :].rearrange("p (h a d) -> p h a d", h=4, a=2)
                    a_ = add(dve, [m_, toa[tt]], dst, dst, T4[:, :, 0, :])
                    toa[tt] = add(dve, [a_], dst, dst, T4[:, :, 1, :])

            yield
            for tt in range(2):
                yield from compressed(tt)
                lo_, hi_ = 8 * tt, 8 * tt + 8
                for s_ in range(lo_, hi_ + 2):
                    if lo_ <= s_ - 1 < hi_:
                        turned(s_ - 1)
                    if lo_ <= s_ - 2:
                        values(s_ - 2)
                    if s_ < hi_:
                        scores(s_)
                    yield

        tqr, tkr, tv, tsg = [], [], [], []
        rab = [None]

        def evac_rot(dstT, toks):
            def evac(tt, ps, t):
                b4 = lambda ap: ap.rearrange("p (h d) -> p h d", h=4)
                free = rab[0] or t_h
                cosb = bc(ctab[:, tt, 0:128], [128, 4, 128], 1)
                a = mul(dve, [t, t_ctab, *free], b4(ra[:, :]), b4(ps), cosb)
                b = mul(dve, [t, *free], b4(rb[:, :])[:, :, 0:64], b4(ps)[:, :, 64:128],
                        bc(ctab[:, tt, 128:192], [128, 4, 64], 1))
                c = mul(dve, [t, *free], b4(rb[:, :])[:, :, 64:128], b4(ps)[:, :, 0:64],
                        bc(ctab[:, tt, 192:256], [128, 4, 64], 1))
                d = add(pool, [a, b, c], ra[:, :], ra[:, :], rb[:, :])
                bk = bank()
                for j in range(4):
                    t2 = transposed([d, *bank_free.get(bk, [])], PB[bk][:, j * 128:j * 128 + 128],
                                    ra[:, j * 128:j * 128 + 128])
                f = copy(act, [t2], dstT[:, :, tt * 128:tt * 128 + 128],
                         PB[bk][:, :].rearrange("p (k s) -> p k s", k=4))
                bank_free[bk] = [f]
                rab[0] = [t2]
                toks.append(f)
                return [a, b, c]
            return evac

        def evac_to(dst, toks, q=None):
            def evac(tt, ps, t):
                toks.append(copy(q or (act if tt else dve), [t], dst(tt), ps))
                return [toks[-1]]
            return evac

        back = chain(
            rows_out(hhi, hlo, [], evac_rot(qrT, tqr)),
            rows_out(hhi, hlo, [], evac_rot(krT, tkr)),
            rows_out(hhi, hlo, [], evac_to(lambda tt: vr[tt][:, 0:512], tv)),
            rows_out(hhi, hlo, [], evac_to(lambda tt: vr[tt][:, 512:1024], tv)),
            rows_out(hhi, hlo, [], evac_to(lambda tt: sg[:, tt, 0:512], tsg)),
            rows_out(hhi, hlo, [], evac_to(lambda tt: sg[:, tt, 512:1024], tsg)),
        )
        weave(nsa(), back, 2)
        toaT = to_halves_T(oa, 4, oah, oal, [[toa[0]], [toa[1]]])

        t_gnw = load("d_gnw", gnw[:, :], rows[7:8, :].to_broadcast([128, D]), [*rab[0], *tkr])
        nsa_done = everything()
        tor = [[], []]

        def ret():
            s_t, o_t = {}, {}
            mv = st[:, 128:144].rearrange("p (h t c) -> p h t c", h=4, t=2)
            bn = st[:, 144:192].rearrange("p (h t c) -> p h t c", h=4, t=2)
            sf, of = [[*nsa_done], [*nsa_done]], [[*nsa_done], [*nsa_done]]
            stf = {}
            a0 = act.do([*tsg], lambda e: e.activation(sg[:, :, :], sg[:, :, :], ACT.Silu))
            tsil = [mul(pool, [a0, t_gnw], sg[:, tt, :], sg[:, tt, :], gnw[:, :]) for tt in range(2)]
            for h in range(6):
                if 0 <= h - 1 < 4:
                    k = h - 1
                    b = (TP, OB)[k % 2]
                    vs = slice(k * 256, k * 256 + 256)
                    mm([s_t[k], *tv, *of[k % 2]], b[:, 0:256], STt[k % 2][:, 0:128], vr[0][:, vs])
                    mm([], b[:, 256:512], STt[k % 2][:, 128:256], vr[0][:, vs], start=True, stop=False)
                    t = mm([], b[:, 256:512], STt[k % 2][:, 256:384], vr[1][:, vs], start=False, stop=True)
                    stf[k] = [t]
                    for tt in range(2):
                        c = dve.do([t], lambda e, tt=tt: e.bn_stats(bn[:, k, tt, :], b[:, tt * 256:tt * 256 + 256]))
                        c = dve.do([c], lambda e, tt=tt: e.bn_aggr(mv[:, k, tt, :], bn[:, k, tt, :]))
                    rk = st[:, 192 + 2 * k:194 + 2 * k]
                    c = scal(dve, [c], rk, mv[:, k, :, 1], 1.0, EPS, ALU.mult, ALU.add)
                    o_t[k] = power([c], st[:, 200 + 2 * k:202 + 2 * k], rk)
                if h < 4:
                    b = SC[h % 2]
                    mm([*tqr, *tkr, *sf[h % 2]], b[:, 0:256], krT[:, h, 0:128], qrT[:, h, :])
                    t = mm([], b[:, 256:384], krT[:, h, 128:256], qrT[:, h, 128:256])
                    s_t[h] = mul(dve, [t, t_dec, *stf.get(h - 2, [])], STt[h % 2][:, :], b[:, 0:384], dec[:, h, :])
                    sf[h % 2] = [s_t[h]]
                yield
                if 0 <= h - 1 < 4:
                    k = h - 1
                    b = (TP, OB)[k % 2]
                    for tt in range(2):
                        d = scal(dve, [o_t[k], *nsa_done], orr[tt][:, k * 256:k * 256 + 256],
                                 b[:, tt * 256:tt * 256 + 256], mv[:, k, tt, 0:1],
                                 st[:, 200 + 2 * k + tt:201 + 2 * k + tt], ALU.subtract, ALU.mult)
                        tor[tt].append(d)
                    of[k % 2] = [d]
                yield
            for tt in range(2):
                tor[tt] = [mul(dve, [*tor[tt], tsil[tt]], orr[tt][:, :], orr[tt][:, :], sg[:, tt, :])]
                yield

        tgm = []

        def evac_gm(f):
            def evac(p, ps, t):
                tgm.append(copy(act, [t, *nsa_done], gm[:, 2 * f:2 * f + 2, :], ps))
                return [tgm[-1]]
            return evac

        weave(ret(), chain(*[feats_out(hhi, hlo, 8, [], evac_gm(f)) for f in range(8)]), 4)
        torT = to_halves_T(orr, 8, orh, orl, tor)
        tgs = [act.do(tgm, lambda e, f=f: e.activation(gm[:, 8 * f:8 * f + 8, :], gm[:, 8 * f:8 * f + 8, :],
                                                       ACT.Sigmoid)) for f in range(2)]
        ret_done = everything()
        tmg, tm = {}, []

        def evac_ya(f):
            def evac(p, ps, t):
                j = 4 * f + 2 * p
                tmg[j] = mul(dve, [t, *tgs, *ret_done], mg[:, j:j + 2, :], ps, gm[:, j:j + 2, :])
                return [tmg[j]]
            return evac

        def evac_yb(f):
            def evac(p, ps, t):
                j = 2 * f
                a = mul(dve, [t, *tgs], gm[:, 8 + j:10 + j, :], ps, gm[:, 8 + j:10 + j, :])
                b = add(pool, [a, tmg[j]], mg[:, j:j + 2, :], mg[:, j:j + 2, :], gm[:, 8 + j:10 + j, :])
                tm.extend(halves(mh[:, j:j + 2, :], ml[:, j:j + 2, :], mg[:, j:j + 2, :], [b, *ret_done]))
                return [a]
            return evac

        run(chain(*[feats_out(oah, oal, 4, toaT, evac_ya(f)) for f in range(2)]))
        run(chain(*[feats_out(orh, orl, 8, torT, evac_yb(f)) for f in range(4)]))
        run(chain(*[rows_out(mh, ml, tm, add_to_x(512 * f)) for f in range(2)]))

        ghi = at("ghi", P, [128, NFT, S], R32)
        glo = at("glo", P + 22, [128, NFT, S], R32)
        fu = [at(f"fu{i}", P + 56 + 2 * i, [128, 2, S]) for i in range(2)]
        fs = [at(f"fs{i}", P + 60 + i, [128, S]) for i in range(2)]
        fg = [at(f"fg{i}", P + 62 + i, [128, S]) for i in range(2)]

        def ffn(conv):
            nonlocal x_done
            gi, ready = (1, x_done) if conv else (3 + 2 * conv_l[0], x_done)
            x_done = [[], []]
            th = norm(gi if conv else gi + 1, ready)
            busy = everything()
            tgx, used = [], {}
            fc = smv("fconv").rearrange("p (f v c) -> p f v c", f=NFT, v=2)

            def evac(f):
                def ev(p, ps, t):
                    u, s_, g = fu[f % 2], fs[f % 2], fg[f % 2]
                    free = [*used.get(f - 2, busy)]
                    if conv:
                        for v in range(2):
                            a = act.do([t, *free], lambda e, v=v: e.activation(
                                u[:, v, :], ps[:, v, :], ACT.Identity, scale=fc[:, f, v, 2:3], bias=fc[:, f, v, 3:4]))
                        for v in range(2):
                            b = dve.do([a], lambda e, v=v: e.scalar_tensor_tensor(
                                u[:, v, 1:S], ps[:, v, 0:S - 1], fc[:, f, v, 1:2], u[:, v, 1:S], ALU.mult, ALU.add))
                            b = dve.do([b], lambda e, v=v: e.scalar_tensor_tensor(
                                u[:, v, 2:S], ps[:, v, 0:S - 2], fc[:, f, v, 0:1], u[:, v, 2:S], ALU.mult, ALU.add))
                        c = act.do([b], lambda e: e.activation(s_[:, :], u[:, 0, :], ACT.Silu))
                        d = mul(pool, [c, b], g[:, :], s_[:, :], u[:, 1, :])
                        done = [b]
                    else:
                        c = act.do([t, *free], lambda e: e.activation(s_[:, :], ps[:, 0, :], ACT.Silu))
                        d = mul(dve, [c, *free], g[:, :], ps[:, 1, :], s_[:, :])
                        done = [d]
                    h = halves(ghi[:, f, :], glo[:, f, :], g[:, :], [d, *busy])
                    used[f] = h
                    tgx.append(h)
                    return done
                return ev

            run(chain(*[feats_out(hhi, hlo, 8, th, evac(f)) for f in range(NFT)]))
            b0 = [bank() for _ in range(4)]
            for c in range(NFT // 2):
                i, (_, wh, wl) = take()
                for k in range(2):
                    kg = 2 * c + k
                    for tt in range(2):
                        for half in range(2):
                            b = b0[tt * 2 + half]
                            sl = slice(tt * 128, tt * 128 + 128)
                            cs = slice(half * 512, half * 512 + 512)
                            after = [*split[i], *tgx[kg], *(bank_free.get(b, []) if kg == 0 else [])]
                            t = mm3(PB[b][:, :], ghi[:, kg, sl], glo[:, kg, sl], wh[:, k, cs], wl[:, k, cs],
                                    kg == 0, kg == NFT - 1, after)
                            if t:
                                bank_free[b] = add_to_x(half * 512)(tt, PB[b][:, :], t)
                taken(i, t or pe_mark())

        conv_l = [0]
        ffn(True)
        ready = norm(2, x_done, final=True)

        ath, atl, cvh, cvl, frh, frl = (at(n, P + 4 * j, [128, 4, S], R32) for j, n in
                                        enumerate(("ath", "atl", "cvh", "cvl", "frh", "frl")))
        gm2 = at("gm2", P + 24, [128, 24, S])
        Z = P + 48
        q2T = at("q2T", Z, [128, 4, S])
        k2T = at("k2T", Z + 4, [128, 4, S])
        v2 = [at(f"v2{t}", Z + 8 + 2 * t, [128, 512]) for t in range(2)]
        gp = at("gp", Z + 12, [128, 4, 288])
        Y = Z + 16.5
        qn = [at(f"qn{t}", Y + 2 * t, [128, 512]) for t in range(2)]
        sq = at("sq", Y + 4, [128, 512])
        xf = [at(f"xf{t}", Y + 6 + 2 * t, [128, 512]) for t in range(2)]
        T12 = [at(f"T12{t}", Y + 10 + 2 * t, [128, 512]) for t in range(2)]
        csT = at("csT", Y + 14, [128, 2, 512])
        cdT = at("cdT", Y + 18, [128, 2, 128])
        E2 = [at(f"E2{t}", Y + 2 * t, [128, 2, S]) for t in range(2)]
        W2 = [at(f"W2{t}", Y + 4 + t, [128, S]) for t in range(2)]
        WT = [at(f"WT{t}", Y + 6 + 2 * t, [128, 2, S]) for t in range(2)]
        o2 = at("o2", Y + 10, [128, 2, 512])
        cv = at("cv", Y + 14, [128, 4, S])
        csq = at("csq", Y + 18, [128, 4, S])
        mh2 = at("mh2", Z, [128, 8, S], R32)
        ml2 = at("ml2", Z + 8, [128, 8, S], R32)
        mg2 = at("mg2", Z + 16, [128, 8, S])
        mt2 = [at(f"mt2{t}", Z + 24 + 2 * t, [128, 2, S]) for t in range(2)]
        rope4 = smv("rope4").rearrange("p (t a n) -> p t a n", t=2, a=2)
        o2q = [o2[:, tt, :] for tt in range(2)]

        def layer(l):
            nonlocal x_done, ready
            li = 0.8 - 0.6 * math.exp(-0.3 * l)
            th = norm(3 + 2 * l, ready)
            busy = everything()
            tcs = load(f"d_cs{l}", csT[:, :, :], tabs["cs"], busy)
            tcd = load(f"d_cd{l}", cdT[:, :, :], tabs["cd"], busy)
            lam = smv("lam").rearrange("p (l a d) -> p l a d", l=2, a=4)[:, l, :, :]
            lp = st[:, 256:320].rearrange("p (a d) -> p a d", a=2)
            nl = st[:, 8 + 4 * l:12 + 4 * l]
            a = mul(dve, [t_sm], lp, lam[:, 0:4:2, :], lam[:, 1:4:2, :])
            a = dve.do([a], lambda e: e.tensor_reduce(nl[:, 0:2], lp, AXX, ALU.add))
            a = act.do([a], lambda e: e.activation(nl[:, 0:2], nl[:, 0:2], ACT.Exp))
            tlam = dve.do([a], lambda e: e.scalar_tensor_tensor(
                nl[:, 2:3], nl[:, 1:2], -li, nl[:, 0:1], ALU.add, ALU.subtract))
            neglam = nl[:, 2:3]
            tz = pool.do(busy, lambda e: e.memset(gp[:, :, :], 0.0))

            tT, tv2, trq = {0: [], 1: []}, [], {}
            qfree = [busy, busy]

            def evac_qk(w):
                def evac(tt, ps, t):
                    n = 2 * w + tt
                    g16 = lambda ap: ap.rearrange("p (g d) -> p g d", d=32)
                    ss = st[:, 128 + 16 * n:144 + 16 * n]
                    rs = st[:, 192 + 16 * n:208 + 16 * n]
                    a = act.do([t, *busy, *trq.get("sq", [])], lambda e: e.activation(sq[:, :], ps, ACT.Square))
                    b = dve.do([a], lambda e: e.tensor_reduce(ss, g16(sq[:, :]), AXX, ALU.add))
                    trq["sq"] = [b]
                    k = 1.0 if w == 0 else 1.0 / 32
                    c = scal(dve, [b], ss, ss, k, EPS * 32 * k, ALU.mult, ALU.add)
                    d = power([c], rs, ss)
                    q = qn[n % 2]
                    f = dve.do([d, *qfree[n % 2]], lambda e: e.tensor_tensor(
                        g16(q[:, :]), g16(ps), bc(rs, [128, 16, 32], 2), ALU.mult))
                    gg = smv("qkg").rearrange("p (l w d) -> p l w d", l=2, w=2)[:, l, w, :]
                    g = mul(pool, [f], g16(q[:, :]), g16(q[:, :]), bc(gg, [128, 16, 32], 1))
                    t1, t2 = (st[:, o:o + 128].rearrange("p (g d) -> p g d", d=8) for o in (256, 384))
                    r = rope_small(pool, g16(q[:, :])[:, :, 0:8], [128, 16, 8], tt, rope4, 4, t1, t2, [g, tlam])
                    pend.append((w, tt, q, r, n))
                    return [f, a]
                return evac

            pend = []

            def turn_qk():
                for w, tt, q, r, n in pend:
                    b = bank()
                    for j in range(4):
                        t = transposed([r, *bank_free.get(b, [])], PB[b][:, j * 128:j * 128 + 128],
                                       q[:, j * 128:j * 128 + 128])
                    c = copy(act, [t], (q2T, k2T)[w][:, :, tt * 128:tt * 128 + 128],
                             PB[b][:, :].rearrange("p (k s) -> p k s", k=4))
                    bank_free[b] = [c]
                    qfree[n % 2] = [t]
                    tT[w].append(c)
                pend.clear()
                yield

            tgl, txf = [], []

            def evac_glu(f):
                def evac(p, ps, t):
                    a = act.do([t, *busy, *tgl[-1:]], lambda e: e.activation(sq[:, 0:S], ps[:, 1, :], ACT.Sigmoid))
                    b = mul(dve, [a, tz], gp[:, f, 15:15 + S], ps[:, 0, :], sq[:, 0:S])
                    tgl.append(b)
                    return [b]
                return evac

            run(chain(rows_out(hhi, hlo, th, evac_qk(0)),
                      (rows_out(hhi, hlo, [], evac_qk(1)))) if False else rows_out(hhi, hlo, th, evac_qk(0)))
            g1 = rows_out(hhi, hlo, [], evac_qk(1))
            for _ in range(7):
                next(g1)
            run(turn_qk())
            run(g1)
            run(rows_out(hhi, hlo, [], evac_to(lambda tt: v2[tt][:, :], tv2)))
            run(turn_qk())
            for f in range(4):
                run(feats_out(hhi, hlo, 8, [], evac_glu(f)))
            run(rows_out(hhi, hlo, [], evac_to(lambda tt: xf[tt][:, :], txf)))

            tgm2 = []
            bgv = smv("bg").rearrange("p (l f) -> p l f", l=2)[:, l, :]

            def evac_g(f):
                def evac(p, ps, t):
                    for v in range(2):
                        a = act.do([t, *busy], lambda e, v=v: e.activation(
                            gm2[:, 2 * f + v, :], ps[:, v, :], ACT.Identity, bias=bgv[:, 2 * f + v:2 * f + v + 1]))
                    tgm2.append(a)
                    return [a]
                return evac

            back = chain(*[feats_out(hhi, hlo, 8, [], evac_g(f)) for f in range(12)])

            tfr = []

            def fourier():
                tf, ev = {}, {}
                for g in range(5):
                    if g >= 1:
                        k = g - 1
                        o = OB[:, 0:256]
                        fr = ev.get("o", busy)
                        mm([tf[k], tcd, *fr], o, cdT[:, 0, :], T12[k % 2][:, 0:256], start=True, stop=False)
                        t = mm([], o, cdT[:, 1, :], T12[k % 2][:, 256:512], start=False, stop=True)
                        ev[k] = [t]
                        h = halves(frh[:, k, :], frl[:, k, :], o, [t, *busy])
                        ev["o"] = h
                        tfr.extend(h)
                    if g < 4:
                        for tt in range(2):
                            t = mm([*txf, tcs, *busy, *([tf[g - 2]] if g >= 2 else [])], SC[g % 2][:, :],
                                   xf[tt][:, g * 128:g * 128 + 128], csT[:, tt, :], start=(tt == 0), stop=(tt == 1))
                        tf[g] = copy(act, [t, *ev.get(g - 2, busy)], T12[g % 2][:, :], SC[g % 2][:, :])
                    yield

            to2 = []
            tconv = [[], [], [], []]

            def attention():
                done1 = everything()
                scf, tpf, obf = [done1, done1], done1, done1
                ex, trn, wv, pv = {}, {}, {}, {}
                lw = st[:, 128:160].rearrange("p (h t c) -> p h t c", h=8, t=2)
                nm = st[:, 160:192].rearrange("p (h t c) -> p h t c", h=8, t=2)
                rr = st[:, 192:224].rearrange("p (h t c) -> p h t c", h=8, t=2)
                cc = st[:, 224:240].rearrange("p (h t) -> p h t", h=8)
                wtf = {}
                yield
                for u in range(19):
                    if 0 <= u - 1 < 16:
                        n = u - 1
                        h, tt = n // 2, n % 2
                        for k in range(2):
                            t = transposed([wv[n], *(tpf if tt == 0 else [])],
                                           TP[:, k * 256 + tt * 128:k * 256 + tt * 128 + 128],
                                           W2[n % 2][:, k * 128:k * 128 + 128])
                        trn[n] = [t]
                        if tt == 1:
                            a = copy(act, [t, *pv.get(h - 2, done1)], WT[h % 2][:, :, :],
                                     TP[:, :].rearrange("p (k s) -> p k s", k=2))
                            tpf = [a]
                            wtf[h] = a
                    if u >= 3 and (u - 3) % 2 == 0:
                        h = (u - 3) // 2
                        for tt in range(2):
                            for k in range(2):
                                t = mm([wtf[h], *tv2, *obf],
                                       OB[:, (tt * 4 + h % 4) * 64:(tt * 4 + h % 4) * 64 + 64],
                                       WT[h % 2][:, k, tt * 128:tt * 128 + 128], v2[k][:, h * 64:h * 64 + 64],
                                       start=(k == 0), stop=(k == 1))
                        pv[h] = [t]
                        if h % 4 == 3:
                            for tt in range(2):
                                b = dve.do([t, *done1], lambda e, tt=tt, h=h: e.tensor_tensor(
                                    o2[:, tt, (h - 3) * 64:(h + 1) * 64].rearrange("p (h d) -> p h d", d=64),
                                    OB[:, tt * 256:tt * 256 + 256].rearrange("p (h d) -> p h d", d=64),
                                    bc(rr[:, h - 3:h + 1, tt, 0], [128, 4, 64], 2), ALU.mult))
                                to2.append(b)
                            obf = [b]
                    if u < 16:
                        h, tt = u // 2, u % 2
                        rg = slice((h % 4) * 32, (h % 4) * 32 + 32)
                        bk = SC[u % 2]
                        for c in range(2):
                            t = mm([*tT[0], *tT[1], *scf[u % 2]], bk[:, c * S:c * S + S],
                                   q2T[rg, c * 2 + h // 4, tt * 128:tt * 128 + 128], k2T[rg, c * 2 + h // 4, :])
                        s = bk[:, :].rearrange("p (c k) -> p c k", c=2)
                        m = dve.do([t], lambda e, s=s, h=h, tt=tt: e.tensor_reduce(
                            nm[:, h, tt, :], s, AXX, ALU.max, negate=True))
                        for c in range(2):
                            a = act.do([m, *([wv[u - 2]] if u >= 2 else done1)], lambda e, c=c, s=s, h=h, tt=tt, u=u:
                                       e.activation(E2[u % 2][:, c, :], s[:, c, :], ACT.Exp,
                                                    bias=nm[:, h, tt, c:c + 1], accum_out=lw[:, h, tt, c:c + 1]))
                        scf[u % 2] = [a]
                        b = dve.do([a], lambda e, h=h, tt=tt: e.reciprocal(rr[:, h, tt, :], lw[:, h, tt, :]))
                        c_ = dve.do([b, tlam], lambda e, h=h, tt=tt: e.tensor_scalar(
                            cc[:, h, tt:tt + 1], lw[:, h, tt, 0:1], neglam, rr[:, h, tt, 1:2], ALU.mult, ALU.mult))
                        wv[u] = dve.do([c_, *trn.get(u - 2, done1)], lambda e, h=h, tt=tt, u=u: e.scalar_tensor_tensor(
                            W2[u % 2][:, :], E2[u % 2][:, 1, :], cc[:, h, tt:tt + 1], E2[u % 2][:, 0, :],
                            ALU.mult, ALU.add))
                    conv_some(9, done1)
                    yield

            cwv = smv("cw").rearrange("p (l f j) -> p l f j", l=2, f=4)[:, l, :, :]
            cvec = smv("cvec").rearrange("p (l a f) -> p l a f", l=2, a=3)[:, l, :, :]
            todo = [(f, j) for f in range(4) for j in range(31)]

            def conv_some(n, done1):
                for _ in range(n):
                    if not todo:
                        return
                    f, j = todo.pop(0)
                    if j == 0:
                        tconv[f] = [scal(dve, [*tgl, *done1], cv[:, f, :], gp[:, f, 0:S], cwv[:, f, 0:1],
                                         cvec[:, 0, f:f + 1], ALU.mult, ALU.add)]
                    else:
                        tconv[f] = [dve.do(tconv[f], lambda e, f=f, j=j: e.scalar_tensor_tensor(
                            cv[:, f, :], gp[:, f, j:j + S], cwv[:, f, j:j + 1], cv[:, f, :], ALU.mult, ALU.add))]

            tat, tcv = [], []

            def after_attention():
                o16 = o2[:, :, :].rearrange("p t (h d) -> p (t h) d", d=64)
                sqv = csq[:, :, :].rearrange("p f s -> p (f s)")
                ss, rs = st[:, 240:256], st[:, 256:272]
                a = act.do([*to2], lambda e: e.activation(
                    sqv, o2[:, :, :].rearrange("p t n -> p (t n)"), ACT.Square))
                b = dve.do([a], lambda e: e.tensor_reduce(ss, sqv.rearrange("p (g d) -> p g d", d=64), AXX, ALU.add))
                z = (1 - li) ** 2
                c = scal(dve, [b], ss, ss, 1.0 / 64 / z, EPS / z, ALU.mult, ALU.add)
                d = power([c], rs, ss)
                yield
                allcv = [t for f in range(4) for t in tconv[f]]
                for f in range(4):
                    t = mm([*allcv, *everything()] if f == 0 else [], SC[0][:, 0:S], ones, cv[:, f, :],
                           start=(f == 0), stop=(f == 3))
                for f in range(4):
                    m = dve.do([t], lambda e, f=f: e.scalar_tensor_tensor(
                        cv[:, f, :], SC[0][:, 0:S], -1.0 / 512, cv[:, f, :], ALU.mult, ALU.add))
                q = act.do([m, b], lambda e: e.activation(csq[:, :, :], cv[:, :, :], ACT.Square))
                yield
                f1 = mul(dve, [d, *to2], o16, o16, bc(rs, [128, 16, 64], 2))
                sgv = smv("subg").rearrange("p (l d) -> p l d", l=2)[:, l, :]
                f2 = mul(pool, [f1], o16, o16, bc(sgv, [128, 16, 64], 1))
                for tt in range(2):
                    for f in range(4):
                        t = mm([q], SC[1][:, tt:tt + 1], csq[:, f, tt * 128:tt * 128 + 128], ones[:, 0:1],
                               start=(f == 0), stop=(f == 3))
                vs, vr_ = st[:, 272:274], st[:, 274:276]
                g = scal(dve, [t], vs, SC[1][:, 0:2], 1.0 / 512, EPS, ALU.mult, ALU.add)
                h = power([g], vr_, vs)
                rb2 = W2
                yield
                for tt in range(2):
                    k = copy(dve, [h], rb2[tt][:, 0:128], vr_[:, tt:tt + 1].to_broadcast([128, 128]))
                    t = mm([k, t_sm], SC[0][:, tt * 128:tt * 128 + 128], rb2[tt][:, 0:128], ident)
                m = dve.do([t], lambda e: e.tensor_tensor(cv[:, :, :], cv[:, :, :], bc(SC[0][:, 0:S], [128, 4, S], 1),
                                                          ALU.mult))
                yield
                tat.extend(to_halves_T(o2q, 4, ath, atl, [[f2], [f2]]))
                for f in range(4):
                    n = act.do([m], lambda e, f=f: e.activation(
                        csq[:, f, :], cv[:, f, :], ACT.Silu, scale=cvec[:, 1, f:f + 1], bias=cvec[:, 2, f:f + 1]))
                tcv.extend(halves(cvh[:, :, :], cvl[:, :, :], csq[:, :, :], [n]))
                yield

            def front():
                yield from fourier()
                yield from attention()
                yield from after_attention()

            weave(front(), back, 3)
            tgs2 = [act.do(tgm2, lambda e, f=f: e.activation(gm2[:, 8 * f:8 * f + 8, :], gm2[:, 8 * f:8 * f + 8, :],
                                                             ACT.Sigmoid)) for f in range(3)]
            done2 = everything()
            tmg2, tm2 = {}, []

            def evac_y(n, f):
                def evac(p, ps, t):
                    j = 4 * f + 2 * p
                    g = gm2[:, 8 * n + j:8 * n + j + 2, :]
                    if n == 0:
                        tmg2[j] = mul(dve, [t, *tgs2, *done2], mg2[:, j:j + 2, :], ps, g)
                        return [tmg2[j]]
                    a = mul(dve, [t, *tgs2], g, ps, g)
                    tmg2[j] = add(pool, [a, tmg2[j]], mg2[:, j:j + 2, :], mg2[:, j:j + 2, :], g)
                    if n == 2:
                        tm2.extend(halves(mh2[:, j:j + 2, :], ml2[:, j:j + 2, :], mg2[:, j:j + 2, :],
                                          [tmg2[j], *done2]))
                    return [a]
                return evac

            for n, (hi, lo, tk) in enumerate(((ath, atl, tat), (cvh, cvl, tcv), (frh, frl, tfr))):
                run(chain(*[feats_out(hi, lo, 4, tk, evac_y(n, f)) for f in range(2)]))
            x_done = [[], []]
            run(chain(*[rows_out(mh2, ml2, tm2, add_to_x(512 * f)) for f in range(2)]))
            conv_l[0] = l
            ffn(False)
            ready = x_done

        for l in range(2):
            layer(l)

        s_out = sem("s_out")
        for tt in range(2):
            t = sp.dma(ready[tt], s_out, 16 * (tt + 1),
                       lambda e, tt=tt: e.dma_start(out[tt * 128:(tt + 1) * 128, :], x[:, tt, :]))
        sp.wait([t])



def _pack(arrays):
    f = np.float32
    parts = []
    for name, layer, cs, k0, kk, _ in chunk_plan():
        w = arrays[name][layer]
        b = w[k0 * 128:(k0 + kk) * 128, :][:, np.asarray(cs)]
        parts.append(np.ascontiguousarray(b.reshape(kk, 128, len(cs)).transpose(1, 0, 2)).reshape(-1))
    return np.concatenate(parts)


def _small(a):
    f = np.float32
    sm = np.zeros((128, NSMALL), f)

    def put(name, v):
        o, n = SOFF[name]
        v = np.asarray(v)
        v = v.reshape(v.shape[0], -1)
        assert v.shape[1] == n, (name, v.shape)
        sm[:v.shape[0], o:o + n] = v

    def every(v):
        return np.broadcast_to(np.asarray(v).reshape(1, -1), (128, np.asarray(v).size))

    put("ident", np.eye(128, dtype=f))
    put("ones", np.ones((128, 128), f))
    put("mhalf", np.full((128, 16), -0.5, f))

    def rope(dim, theta):
        half = dim // 2
        inv = np.power(f(theta), -np.arange(half, dtype=f) / f(half)).astype(f)
        ang = (np.arange(S, dtype=f)[:, None] * inv[None, :]).astype(f).astype(np.float64)
        c, s = np.cos(ang).astype(f), np.sin(ang).astype(f)
        t = np.stack([np.concatenate([c, c], 1), np.concatenate([-s, s], 1)], 1)
        return t.reshape(2, 128, 2, dim).transpose(1, 0, 2, 3)

    put("ropen", rope(16, 500000.0))
    put("rope4", rope(8, 500000.0))
    ctab = np.ascontiguousarray(rope(128, 10000.0).reshape(128, 2, 256))
    seen = (np.arange(16)[None, :] * 16 + 31 <= np.arange(S)[:, None])
    put("madd", np.where(seen, 0.0, NEG).astype(f).reshape(2, 128, 16).transpose(1, 0, 2))
    put("m01", seen.astype(f).reshape(2, 128, 16).transpose(1, 0, 2))
    put("bm", (np.arange(120)[:, None] // 15 == np.arange(8)[None, :]).astype(f))
    put("w2k", a["cmp_w2_k"][0].reshape(2, 128, 64).transpose(1, 0, 2))
    put("w2v", a["cmp_w2_v"][0].reshape(2, 128, 64).transpose(1, 0, 2))
    put("pe", np.stack([a[n][0].reshape(16, 128).T for n in ("cmp_pe_k", "cmp_pe_v")], 1))
    fc = np.concatenate([a["ffn_conv_w"][0], a["ffn_conv_b"]], 0)
    put("fconv", fc.reshape(4, 2, NFT, 128).transpose(3, 2, 1, 0))
    put("lam", every(np.stack([a[n] for n in ("lambda_q1_2", "lambda_k1_2", "lambda_q2_2", "lambda_k2_2")], 1)))
    put("qkg", every(np.stack([a["qnorm_g_2"], a["knorm_g_2"]], 1)))
    put("subg", every(a["subln_g_2"]))
    put("cw", a["conv_w_2"].reshape(2, 31, 4, 128).transpose(3, 0, 2, 1))
    put("cvec", np.stack([a[n].reshape(2, 4, 128) for n in ("conv_b_2", "conv_ln_g_2", "conv_ln_b_2")], 1)
        .transpose(3, 0, 1, 2))
    put("bg", a["b_gate_2"].reshape(2, 24, 128).transpose(2, 0, 1))
    lg = np.log1p(-np.exp2(-5.0 - np.arange(4, dtype=np.float64)))
    j, i = np.arange(128)[:, None], np.arange(256)[None, :]
    full = np.concatenate([i - j, (i - j)[:, 0:128]], 1)[:, None, :]
    dec = np.where(full >= 0, np.exp(lg[None, :, None] * np.maximum(full, 0)), 0.0) * 128 ** -0.5
    n = np.arange(256)
    cs = 2 * np.pi * ((n[:, None] * n[None, :]) % 256) / 256
    cs = np.concatenate([np.cos(cs), np.sin(cs)], 1).astype(f).reshape(2, 128, 512).transpose(1, 0, 2)
    m = np.arange(128)
    cd = 2 * np.pi * ((m[:, None] * m[None, :]) % 128) / 128
    cd = (np.stack([np.cos(cd), -np.sin(cd)], 1) / math.sqrt(256 * 128)).astype(f)
    return sm, {"dec": dec.astype(f), "ctab": ctab, "cs": np.ascontiguousarray(cs), "cd": cd}


def kernel(**inputs):
    import concourse.bacc as _bacc
    from concourse import mybir as _mybir
    from concourse.bass_utils import run_bass_kernel_spmd as _run

    a = {k: np.asarray(v) for k, v in inputs.items()}
    sm, tabs = _small(a)
    rows = np.stack([a["norm_mix_w"][0], a["norm_ffn_w"][0], a["norm_final_w"],
                     a["norm1_g_2"][0], a["norm2_g_2"][0], a["norm1_g_2"][1], a["norm2_g_2"][1],
                     a["ret_gn_w"][0].reshape(-1)])
    arrays = {"in_w": _pack(a), "in_small": sm, "in_rows": rows,
              "in_x": np.ascontiguousarray(a["x"][0])}
    arrays.update({f"in_{k}": v for k, v in tabs.items()})
    nc = _bacc.Bacc("TRN2", target_bir_lowering=False, num_devices=1)
    d = {k: nc.dram_tensor(k, v.shape, _mybir.dt.from_np(v.dtype), kind="ExternalInput").ap()
         for k, v in arrays.items()}
    out = nc.dram_tensor("out_0", (S, D), _mybir.dt.float32, kind="ExternalOutput").ap()
    program(nc, d["in_w"], d["in_small"], {k: d[f"in_{k}"] for k in tabs}, d["in_rows"], d["in_x"], out)
    r = _run(nc, [arrays], core_ids=[0])
    return r.results[0]["out_0"].reshape(1, S, D)
```

```python
import math
from contextlib import ExitStack

import numpy as np

import concourse.bass as bass
from concourse import mybir

F32 = mybir.dt.float32
R32 = mybir.dt.float32r
BF16 = mybir.dt.bfloat16
ALU = mybir.AluOpType
ACT = mybir.ActivationFunctionType
AXX = mybir.AxisListType.X

D = 1024
S = 256
EPS = 1e-6
NEG = -1e30
FF = 2816
NFT = FF // 128
CW = 2048
NRAW, NHL, AHEAD = 4, 3, 2


def cols(*spans):
    return [c for a, n in spans for c in range(a, a + n)]


def chunk_plan():
    plan = []

    def wide(name, layer, cs, nk, per, split=True):
        for k in range(0, nk, per):
            plan.append((name, layer, cs, k, per, split))

    def in1(a, n):
        wide("w_in", 0, cols((a, n)), 8, 4)

    wide("w_in", 0, cols(*[(64 * h, 64) for h in (0, 4, 1, 5, 2, 6, 3, 7)]), 8, 4)
    in1(512, 512)
    in1(1024, 280)
    wide("cmp_w1_k", 0, cols((0, 256)), 16, 8, False)
    wide("cmp_w1_v", 0, cols((0, 256)), 16, 8, False)
    for a in range(1304, 4376, 512):
        in1(a, 512)
    for f in range(8):
        wide("w_in", 0, cols((4376 + 256 * f, 256)), 8, 8)
    for f in range(2):
        wide("w_nsa_branch", 0, cols((512 * f, 512)), 4, 4)
    for f in range(4):
        wide("w_ret_branch", 0, cols((256 * f, 256)), 8, 8)
    for f in range(2):
        wide("w_mix_out", 0, cols((512 * f, 512)), 8, 4)
    for f in range(NFT):
        wide("w_ffn_up", 0, cols((128 * f, 128), (FF + 128 * f, 128)), 8, 8)
    wide("w_ffn_down", 0, cols((0, 1024)), NFT, 2)
    for l in range(2):
        qk = [64 * h + 32 * c + d for c in range(2) for h in range(8) for d in range(32)]
        wide("w_in_2", l, qk, 8, 4)
        wide("w_in_2", l, [512 + c for c in qk], 8, 4)
        for f in range(4):
            wide("w_in_2", l, cols((1536 + 128 * f, 128), (2048 + 128 * f, 128)), 8, 8)
        wide("w_in_2", l, cols((1024, 512)), 8, 4)
        wide("w_in_2", l, cols((2560, 512)), 8, 4)
        for f in range(12):
            wide("w_gate_2", l, cols((256 * f, 256)), 8, 8)
        for n in "abc":
            for f in range(2):
                wide(f"w_proj_{n}_2", l, cols((512 * f, 512)), 4, 4)
        for f in range(2):
            wide("w_out_2", l, cols((512 * f, 512)), 8, 4)
        for f in range(NFT):
            wide("w_ffn_in_2", l, cols((128 * f, 128), (FF + 128 * f, 128)), 8, 8)
        wide("w_ffn_out_2", l, cols((0, 1024)), NFT, 2)
    return plan


SMALL = [
    ("ident", 128), ("ones", 128), ("ropen", 64), ("madd", 32), ("m01", 32), ("bm", 8),
    ("w2k", 128), ("w2v", 128), ("pe", 32), ("fconv", 4 * 2 * NFT),
    ("lam", 256), ("qkg", 128), ("subg", 128), ("cw", 248), ("cvec", 24), ("bg", 48), ("rope4", 32),
    ("mhalf", 16),
]
SOFF, _n = {}, 0
for _name, _w in SMALL:
    SOFF[_name] = (_n, _w)
    _n += _w
NSMALL = _n


class Token:

    def __init__(self, sem, count):
        self.sem, self.count = sem, count


class Queue:

    def __init__(self, engine, sem, linked=False):
        self.linked = linked
        self.engine, self.sem, self.count, self.waited, self.prev = engine, sem, 0, {}, None

    def wait(self, tokens):
        for t in tokens:
            if t is not None and self.waited.get(t.sem.num, 0) < t.count:
                self.waited[t.sem.num] = t.count
                self.engine.wait_ge(t.sem, t.count)

    def do(self, after, make, link=True):
        if self.linked and link:
            self.wait([self.last()])
        self.quiet(after, make)
        return self.mark()

    def quiet(self, after, make):
        self.wait(after)
        self.prev = make(self.engine)

    def mark(self):
        self.prev.then_inc(self.sem, 1)
        self.count += 1
        return self.last()

    def dma(self, after, sem, count, make):
        self.wait(after)
        make(self.engine).then_inc(sem, 16)
        return Token(sem, count)

    def last(self):
        return Token(self.sem, self.count)


def program(nc, wts, small, tabs, rows, x_in, out):
    ctx = ExitStack()
    with ctx:
        base = 16640
        used = [0]

        def at(name, kb, shape, dt=F32):
            n = int(np.prod(shape[1:])) * (2 if dt == BF16 else 4)
            assert base + int(kb * 1024) + n <= 229344, name
            return nc.alloc_sbuf_tensor_at(name, shape, dt, offset=base + int(kb * 1024))

        def sem(name):
            return ctx.enter_context(nc.semaphore(name))

        raw = [at(f"raw{i}", 8 * i, [128, CW]) for i in range(NRAW)]
        whi = [at(f"whi{i}", 32 + 8 * i, [128, CW], R32) for i in range(NHL)]
        wlo = [at(f"wlo{i}", 56 + 8 * i, [128, CW], R32) for i in range(NHL)]
        x = at("x", 80, [128, 2, D])
        hhi = at("hhi", 88, [128, 8, S], R32)
        hlo = at("hlo", 96, [128, 8, S], R32)
        gain = at("gain", 104, [128, D])
        sm = at("sm", 108, [128, NSMALL])
        P0 = 108 + (NSMALL * 4 + 1023) // 1024
        idb = at("idb", P0, [128, 128], BF16)
        mkb = at("mkb", P0 + 0.25, [128, 128], BF16)
        st = at("st", P0 + 0.5, [128, 512])
        P = P0 + 2.5
        assert P <= 119, P

        def smv(name):
            a, n = SOFF[name]
            return sm[:, a:a + n]

        ident, ones = smv("ident"), smv("ones")

        PS = [ctx.enter_context(nc.psum_tensor(f"ps{i}", [128, 512], F32)) for i in range(8)]
        PB = PS[0:4]
        SC, TP, OB = PS[4:6], PS[6], PS[7]

        pe, act, dve, pool, sp = (Queue(e, sem(n), n in ("s_act", "s_dve", "s_pool")) for e, n in (
            (nc.tensor, "s_pe"), (nc.scalar, "s_act"), (nc.vector, "s_dve"), (nc.gpsimd, "s_pool"),
            (nc.sync, "s_sp")))

        def everything():
            return [pe.last(), act.last(), dve.last(), pool.last()]

        def load(name, dst, src, after=()):
            s = sem(name)
            return sp.dma(after, s, 16, lambda e: e.dma_start(dst, src))

        t_x = [load(f"d_x{t}", x[:, t, :], x_in[t * 128:(t + 1) * 128, :]) for t in range(2)]
        t_sm = load("d_sm", sm[:, :], small)
        gain_sem = sem("d_gain")
        gain_n = [0]

        def load_gain(i, after):
            gain_n[0] += 1
            src = rows[i:i + 1, :].partition_broadcast(128) if False else rows[i:i + 1, :].to_broadcast([128, D])
            return sp.dma(after, gain_sem, 16 * gain_n[0], lambda e: e.dma_start(gain[:, :], src))

        t_gain = load_gain(0, [])

        plan = chunk_plan()
        offs, n = [], 0
        for _, _, cs, _, kk, _ in plan:
            offs.append(n)
            n += 128 * kk * len(cs)
        raw_sem = [sem(f"d_w{i}") for i in range(NRAW)]
        raw_free = {}
        landed, split, hl_free = {}, {}, {}
        nxt = {"dma": 0, "split": 0, "use": 0}

        def run_dmas():
            while nxt["dma"] < len(plan):
                i = nxt["dma"]
                if i >= NRAW and i - NRAW not in raw_free:
                    return
                w = plan[i][4] * len(plan[i][2])
                src = wts[offs[i]:offs[i] + 128 * w].rearrange("(p n) -> p n", p=128)
                dst = raw[i % NRAW][:, 0:w]
                landed[i] = sp.dma(raw_free.get(i - NRAW, []), raw_sem[i % NRAW], 16 * (i // NRAW + 1),
                                   lambda e, dst=dst, src=src: e.dma_start(dst, src))
                nxt["dma"] += 1

        share = [0.8]

        def run_splits(upto):
            while nxt["split"] <= min(upto, len(plan) - 1):
                run_dmas()
                i = nxt["split"]
                nxt["split"] += 1
                if not plan[i][5]:
                    continue
                w = plan[i][4] * len(plan[i][2])
                r, h, l = raw[i % NRAW][:, 0:w], whi[i % NHL][:, 0:w], wlo[i % NHL][:, 0:w]
                free = hl_free.get(i - NHL, [])
                t1 = act.do([landed[i], *free], lambda e: e.activation(h, r, ACT.Copy), link=False)
                c = int(w * share[0]) // 32 * 32
                split[i] = [t1]
                for q, a, b in ((dve, 0, c), (pool, c, w)):
                    if a < b:
                        split[i].append(q.do([landed[i], t1, *free], lambda e: e.tensor_tensor(
                            l[:, a:b], r[:, a:b], h[:, a:b].bitcast(F32), ALU.subtract), link=False))
                raw_free[i] = split[i]
                run_dmas()

        def take():
            i = nxt["use"]
            nxt["use"] += 1
            run_splits(i + AHEAD)
            kk, ncol = plan[i][4], len(plan[i][2])
            v = [t[:, 0:kk * ncol].rearrange("p (k n) -> p k n", k=kk)
                 for t in (raw[i % NRAW], whi[i % NHL], wlo[i % NHL])]
            return i, v

        def taken(i, token):
            hl_free[i] = [token]
            if not plan[i][5]:
                raw_free[i] = [token]
                run_dmas()

        bank_free = {}
        turn = [0]

        def bank():
            b = turn[0] % 4
            turn[0] += 1
            return b

        def mm3(out, sh, sl, mh, ml, start, stop, after=()):
            pe.quiet(after, lambda e: e.matmul(out, sh, mh, start=start, stop=False, skip_group_check=True))
            pe.quiet([], lambda e: e.matmul(out, sh, ml, start=False, stop=False, skip_group_check=True))
            make = lambda e: e.matmul(out, sl, mh, start=False, stop=stop, skip_group_check=True)
            if stop:
                return pe.do([], make)
            pe.quiet([], make)

        def by_k(ready, k):
            return ready[min(k // 4, len(ready) - 1)] if ready and isinstance(ready[0], list) else ready

        def rows_out(hi, lo, ready, evac):
            b = [bank(), bank()]
            for c in range(2):
                i, (_, wh, wl) = take()
                kk, ncol = plan[i][4], len(plan[i][2])
                order = [(k, tt) for k in range(kk) for tt in range(2)]
                if c:
                    order = [(k, tt) for tt in range(2) for k in range(kk)]
                for n, (k, tt) in enumerate(order):
                    kg = c * kk + k
                    o = PB[b[tt]][:, 0:ncol]
                    sl = slice(tt * 128, tt * 128 + 128)
                    after = [*split[i], *by_k(ready, kg)]
                    if kg == 0:
                        after += bank_free.get(b[tt], [])
                    t = mm3(o, hi[:, kg, sl], lo[:, kg, sl], wh[:, k, :], wl[:, k, :], kg == 0, kg == 7, after)
                    if n == 2 * kk - 1:
                        taken(i, t or pe.mark())
                    if kg == 7:
                        bank_free[b[tt]] = evac(tt, o, t)
                    if n % 2:
                        yield

        def feats_out(hi, lo, nk, ready, evac):
            i, (_, wh, wl) = take()
            npair = len(plan[i][2]) // 256
            for p in range(npair):
                b = bank()
                toks = None
                for k in range(nk):
                    for f in range(2):
                        o = PB[b][:, f * S:f * S + S]
                        c = p * 256 + f * 128
                        first = k == 0 and f == 0
                        after = [*split[i], *by_k(ready, k)]
                        if first:
                            after += bank_free.get(b, [])
                        wsh, wsl = wh[:, k, c:c + 128], wl[:, k, c:c + 128]
                        pe.quiet(after, lambda e, o=o, a=wsh, m=hi[:, k, :], s=first: e.matmul(
                            o, a, m, start=s, stop=False, skip_group_check=True))
                        pe.quiet([], lambda e, o=o, a=wsh, m=lo[:, k, :]: e.matmul(
                            o, a, m, start=False, stop=False, skip_group_check=True))
                        pe.quiet([], lambda e, o=o, a=wsl, m=hi[:, k, :], s=(k == nk - 1): e.matmul(
                            o, a, m, start=False, stop=s, skip_group_check=True))
                    if k == nk - 1:
                        toks = pe.mark()
                        if p == npair - 1:
                            taken(i, toks)
                        bank_free[b] = evac(p, PB[b][:, :].rearrange("p (f s) -> p f s", f=2), toks)
                    yield

        def run(g):
            for _ in g:
                pass

        def chain(*gs):
            for g in gs:
                yield from g

        def weave(front, back, n):
            for _ in front:
                for _ in range(n):
                    next(back, None)
            run(back)

        def halves(dst_hi, dst_lo, src, after):
            a = act.do(after, lambda e: e.activation(dst_hi, src, ACT.Copy), link=False)
            b = dve.do([a, *after], lambda e: e.tensor_tensor(dst_lo, src, dst_hi.bitcast(F32), ALU.subtract),
                       link=False)
            return [a, b]

        def mul(q, after, o, a, b):
            return q.do(after, lambda e: e.tensor_tensor(o, a, b, ALU.mult))

        def add(q, after, o, a, b):
            return q.do(after, lambda e: e.tensor_tensor(o, a, b, ALU.add))

        def scal(q, after, o, a, s1, s2, op0, op1):
            return q.do(after, lambda e: e.tensor_scalar(o, a, s1, s2, op0, op1))

        def power(after, o, a):
            n = a.shape[-1]
            return pool.do([t_sm, *after], lambda e: e.tensor_tensor(o, a, smv("mhalf")[:, 0:n], ALU.pow))

        def copy(q, after, o, a, link=False):
            if q is act:
                return act.do(after, lambda e: e.activation(o, a, ACT.Copy), link=link)
            return q.do(after, lambda e: e.tensor_copy(o, a), link=link)

        def transposed(after, o, i, n=128):
            idt = ident[0:n, 0:n]
            return pe.do([t_sm, *after], lambda e: e.transpose(o, i, idt))

        def mm(after, o, a, b, start=True, stop=True):
            return pe.do(after, lambda e: e.matmul(o, a, b, start=start, stop=stop, skip_group_check=True))

        def bc(ap, shape, ax):
            return ap.unsqueeze(ax).to_broadcast(shape)

        t_c = [copy(dve, [t_sm], idb[:, :], ident)]
        t_m0 = pool.do([], lambda e: e.memset(mkb[:, :], 0.0))
        t_mk = pool.do([t_m0], lambda e: e.affine_select(
            out=mkb[:, :], in_=mkb[:, :], compare_op=ALU.is_ge, fill=NEG, base=0,
            pattern=[[-1, 128]], channel_multiplier=1))

        xn = [at(f"xn{t}", P + 48 + 4 * t, [128, D]) for t in range(2)]
        norm_used = [[]]

        def norm(gi, ready, final=False):
            nonlocal t_gain
            busy = everything()
            out_t = {}
            for tt in range(2):
                sq2 = st[:, 2 * tt:2 * tt + 2]
                ms = st[:, 4 + tt:5 + tt]
                rs = st[:, 6 + tt:7 + tt]
                a = []
                for half in range(2):
                    hs = slice(half * 512, half * 512 + 512)
                    a.append(act.do([*ready[tt][half], *busy], lambda e: e.activation(
                        xn[tt][:, hs], x[:, tt, hs], ACT.Square, accum_out=sq2[:, half:half + 1]), link=False))
                b = dve.do([*a, *busy], lambda e: e.tensor_scalar(
                    ms, sq2[:, 0:1], sq2[:, 1:2], EPS * D, ALU.add, ALU.add), link=False)
                b = dve.do([b], lambda e: e.tensor_scalar(ms, ms, 1.0 / D, None, ALU.mult), link=False)
                c = power([b], rs, ms)
                for half in range(2):
                    hs = slice(half * 512, half * 512 + 512)
                    o = x[:, tt, hs] if final else xn[tt][:, hs]
                    out_t[tt, half] = dve.do([c, t_gain], lambda e: e.scalar_tensor_tensor(
                        o, x[:, tt, hs], rs, gain[:, hs], ALU.mult, ALU.mult), link=False)
            t_gain = load_gain(gi + 1, out_t.values()) if gi < 6 else None
            if final:
                return [[[out_t[tt, half]] for half in range(2)] for tt in range(2)]
            done = [[], []]
            for half in range(2):
                for tt in range(2):
                    b = bank()
                    for j in range(4):
                        k = half * 4 + j
                        t = transposed([out_t[tt, half], *(bank_free.get(b, []) if j == 0 else [])],
                                       PB[b][:, j * 128:j * 128 + 128], xn[tt][:, k * 128:k * 128 + 128])
                    dst = slice(half * 4, half * 4 + 4), slice(tt * 128, tt * 128 + 128)
                    h = halves(hhi[:, dst[0], dst[1]], hlo[:, dst[0], dst[1]],
                               PB[b][:, :].rearrange("p (k s) -> p k s", k=4), [t, *busy])
                    bank_free[b] = h
                    done[half] += h
            return done

        run_splits(AHEAD)

        def add_to_x(col):
            def evac(tt, ps, t):
                xs = x[:, tt, col:col + 512]
                d = dve.do([t], lambda e: e.tensor_tensor(xs, ps, xs, ALU.add), link=False)
                x_done[tt][col // 512].append(d)
                return [d]
            return evac

        x_done = [[[], []], [[], []]]

        def to_halves_T(src, nblk, dhi, dlo, after):
            res = []
            for tt in range(2):
                for g in range(nblk // 4):
                    b = bank()
                    for j in range(4):
                        k = g * 4 + j
                        t = transposed([*after[tt], *(bank_free.get(b, []) if j == 0 else [])],
                                       PB[b][:, j * 128:j * 128 + 128], src[tt][:, k * 128:k * 128 + 128])
                    h = halves(dhi[:, g * 4:g * 4 + 4, tt * 128:tt * 128 + 128],
                               dlo[:, g * 4:g * 4 + 4, tt * 128:tt * 128 + 128],
                               PB[b][:, :].rearrange("p (k s) -> p k s", k=4), [t])
                    bank_free[b] = h
                    res += h
            return res

        oah = at("oah", P, [128, 4, S], R32)
        oal = at("oal", P + 4, [128, 4, S], R32)
        N0 = P + 8
        qkv = [at(f"qkv{t}", N0 + 5.25 * t, [128, 1304]) for t in range(2)]
        qT = at("qT", N0 + 10.5, [128, 4, S])
        kT = at("kT", N0 + 14.5, [128, 2, S])
        Ex = [at(f"Ex{i}", N0 + 16.5 + 2 * i, [128, 2, S]) for i in range(2)]
        ET = [at(f"ET{i}", N0 + 20.5 + 2 * i, [128, 4, 128]) for i in range(2)]
        oa = [at(f"oa{t}", N0 + 24.5 + 2 * t, [128, 512]) for t in range(2)]
        Tm = at("Tm", N0 + 28.5, [128, 512])
        Sw = at("Sw", N0 + 30.5, [128, 2, 16, 31])
        Hs = at("Hs", N0 + 34.5, [128, 128])
        Hg = at("Hg", N0 + 35, [128, 2, 2, 32])
        Hr = at("Hr", N0 + 35.5, [128, 2, 120])
        kcT = at("kcT", N0 + 36.5, [128, 16])
        VC = at("VC", N0 + 36.75, [128, 8, 64])
        cs_ = at("cs_", N0 + 38.75, [128, 8, 15])
        cp = at("cp", N0 + 39.25, [128, 120])
        cpT = at("cpT", N0 + 39.75, [128, 128])
        rt = at("rt", N0 + 40.25, [128, 16])
        R0 = N0 + 41
        qrT = at("qrT", R0, [128, 4, S])
        krT = at("krT", R0 + 4, [128, 4, S])
        vr = [at(f"vr{t}", R0 + 8 + 4 * t, [128, D]) for t in range(2)]
        sg = at("sg", R0 + 16, [128, 2, D])
        ra = at("ra", R0 + 24, [128, 512])
        rb = at("rb", R0 + 26, [128, 512])
        gnw = at("gnw", R0 + 24, [128, D])
        dec = at("dec", R0 + 28, [128, 4, 384])
        STt = [at(f"STt{i}", R0 + 34 + 1.5 * i, [128, 384]) for i in range(2)]
        ctab = at("ctab", R0 + 37, [128, 2, 256])
        gm = at("gm", N0, [128, 16, S])
        orh = at("orh", N0 + 16, [128, 8, S], R32)
        orl = at("orl", N0 + 24, [128, 8, S], R32)
        orr = [at(f"orr{t}", N0 + 32 + 4 * t, [128, D]) for t in range(2)]
        mh = at("mh", R0, [128, 8, S], R32)
        ml = at("ml", R0 + 8, [128, 8, S], R32)
        mg = at("mg", R0 + 16, [128, 8, S])

        t_h = norm(0, [[[t_x[0]]] * 2, [[t_x[1]]] * 2])
        t_dec = load("d_dec", dec[:, :, :], tabs["dec"], sum(t_h, []))
        t_ctab = load("d_ctab", ctab[:, :, :], tabs["ctab"], sum(t_h, []))

        gt = st[:, 64:112].rearrange("p (t n) -> p t n", t=2)
        ropen = smv("ropen").rearrange("p (t a n) -> p t a n", t=2, a=2)

        def rope_small(q, v, shape, tt, table, half, tmp1, tmp2, after):
            full = [*shape[:-1], 2 * half]
            cosb, sinb = table[:, tt, 0, :], table[:, tt, 1, :]
            for ax in range(len(shape) - 2):
                cosb, sinb = cosb.unsqueeze(1), sinb.unsqueeze(1)
            lo_, hi_ = [slice(None)] * (len(shape) - 1) + [slice(0, half)], None
            lo_ = tuple(lo_)
            hi_ = tuple([slice(None)] * (len(shape) - 1) + [slice(half, 2 * half)])
            hs = [*shape[:-1], half]
            a = mul(q, after, tmp1, v, cosb.to_broadcast(full))
            b = mul(q, after, tmp2[lo_], v[hi_], sinb[lo_].to_broadcast(hs))
            c = mul(q, after, tmp2[hi_], v[lo_], sinb[hi_].to_broadcast(hs))
            return add(q, [a, b, c], v, tmp1, tmp2)

        def r4(ap, a, b):
            return ap.rearrange("p (a b c) -> p a b c", a=a, b=b)

        tq, tk1, tk2 = {}, {}, {}

        def evac_q(tt, ps, t):
            a = act.do([t], lambda e: e.activation(qkv[tt][:, 0:512], ps, ACT.Copy, scale=0.125))
            v = qkv[tt][:, 0:512].rearrange("p (h d) -> p h d", h=8)[:, :, 0:16]
            t1, t2 = (st[:, o:o + 128].rearrange("p (h d) -> p h d", h=8) for o in (128, 256))
            tq[tt] = rope_small(dve, v, [128, 8, 16], tt, ropen, 8, t1, t2, [a])
            return [a]

        def evac_kv1(tt, ps, t):
            tk1[tt] = copy(act, [t], qkv[tt][:, 512:1024], ps)
            return [tk1[tt]]

        def evac_kv2(tt, ps, t):
            a = copy(act, [t], qkv[tt][:, 1024:1304], ps)
            v = qkv[tt][:, 768:1280].rearrange("p (a g d) -> p a g d", a=2, g=4)[:, :, 0:2, 0:16]
            t1, t2 = (st[:, o:o + 64].rearrange("p (a g d) -> p a g d", a=2, g=2) for o in (128, 256))
            tk2[tt] = rope_small(dve, v, [128, 2, 2, 16], tt, ropen, 8, t1, t2, [a, tk1[tt], tq[tt]])
            b = copy(dve, [a], gt[:, tt, :], qkv[tt][:, 1280:1304])
            tg.append(b)
            return [a]

        tg = []
        run(chain(rows_out(hhi, hlo, t_h, evac_q), rows_out(hhi, hlo, [], evac_kv1),
                  rows_out(hhi, hlo, [], evac_kv2)))
        tg = [act.do(tg, lambda e: e.activation(st[:, 64:112], st[:, 64:112], ACT.Sigmoid))]

        tqT = []
        for tt in range(2):
            b = bank()
            for j in range(4):
                t = transposed([tq[tt], *bank_free.get(b, [])], PB[b][:, j * 128:j * 128 + 128],
                               qkv[tt][:, j * 128:j * 128 + 128])
            c = copy(act, [t], qT[:, :, tt * 128:tt * 128 + 128], PB[b][:, :].rearrange("p (k s) -> p k s", k=4))
            bank_free[b] = [c]
            tqT.append(c)
            b = bank()
            for j in range(2):
                o = 768 + 256 * j
                t = transposed([tk2[tt], *bank_free.get(b, [])], PB[b][:, j * 128:j * 128 + 128],
                               qkv[tt][:, o:o + 128])
            c = copy(dve, [t], kT[:, :, tt * 128:tt * 128 + 128],
                     PB[b][:, 0:256].rearrange("p (k s) -> p k s", k=2))
            bank_free[b] = [c]
            tqT.append(c)

        X2 = TP[:, :].rearrange("p (v g s) -> p v g s", v=2, g=2)
        for kv in range(2):
            for g in range(2):
                for tt in range(2):
                    for par in range(2):
                        o = X2[par * 64:par * 64 + 64, kv, g, tt * 64:tt * 64 + 64]
                        src = qkv[tt][:, 512 + kv * 128 + g * 64:512 + kv * 128 + g * 64 + 64]
                        sel = ident.rearrange("p (s e) -> p e s", e=2)[:, par, :]
                        t = mm([tk1[tt]], o, src, sel)
        tS = []
        for kv in range(2):
            for half in range(2):
                o = Sw[:, kv, half * 8:half * 8 + 8, 0:30].rearrange("p j (g c) -> p j g c", g=2)
                i = X2[:, kv, :, half * 8:half * 8 + 120].rearrange("p g (c j) -> p j g c", j=8)
                tS.append(copy(dve, [t], o, i))
            pev = smv("pe").rearrange("p (v j) -> p v j", v=2)[:, kv, :]
            tS.append(copy(dve, [t], Sw[:, kv, :, 30], pev))
        Hp = SC[0][:, 0:128].rearrange("p (v h c) -> p v h c", v=2, h=2)
        for kv in range(2):
            for c in range(2):
                i, (w1, _, _) = take()
                for j in range(8):
                    for half in range(2):
                        t = mm([landed[i], *tS], Hp[:, kv, half, 0:31], w1[:, j, half * 128:half * 128 + 128],
                               Sw[:, kv, c * 8 + j, :], start=(c == 0 and j == 0 and half == 0),
                               stop=(c == 1 and j == 7))
                taken(i, t)
        tH = copy(dve, [t], Hs[:, :].rearrange("p (v h c) -> p v h c", v=2, h=2)[:, :, :, 0:31], Hp[:, :, :, 0:31])
        Hsv = Hs[:, :].rearrange("p (v h c) -> p v h c", v=2, h=2)
        for kv in range(2):
            for half in range(2):
                tG = act.do([tH], lambda e, a=Hg[:, kv, half, 0:30], b=Hsv[:, kv, half, 0:30],
                            c=Hsv[:, kv, half, 30:31]: e.activation(a, b, ACT.Gelu_apprx_tanh, bias=c))
        w2 = [smv(n).rearrange("p (h d) -> p h d", h=2) for n in ("w2k", "w2v")]
        for g in range(2):
            for half in range(2):
                t = mm([tG, tH], SC[1][g * 64:g * 64 + 64, 0:15], w2[0][:, half, :],
                       Hg[:, 0, half, g * 15:g * 15 + 15], start=(half == 0), stop=(half == 1))
        tkc = copy(dve, [t], kcT[:, 0:15], SC[1][:, 0:15])
        for half in range(2):
            tr = copy(dve, [tG], Hr[:, half, :].rearrange("p (g r c) -> p g r c", g=2, r=4),
                      bc(Hg[:, 1, half, 0:30].rearrange("p (g c) -> p g c", g=2), [128, 2, 4, 15], 2))
        for half in range(2):
            t = mm([tr, tS[-1]], TP[0:120, 0:64], Hr[:, half, :], w2[1][:, half, :],
                   start=(half == 0), stop=(half == 1))
        bm = smv("bm")[0:120, :]
        tvc = dve.do([t], lambda e: e.tensor_tensor(
            VC[0:120, :, :], bc(TP[0:120, 0:64], [120, 8, 64], 1), bc(bm, [120, 8, 64], 2), ALU.mult))
        sc_free, tp_free, ob_free = [[tH], [tkc]], [tvc], []

        lsum = st[:, 32:48].rearrange("p (h a) -> p h a", a=2)
        toa = {}

        def nsa():
            nonlocal tp_free, ob_free
            units = [(tt, h) for tt in range(2) for h in range(8)]
            exp_t, tr_t, ev_t, pv_t, ls = {}, {}, {}, {}, {}
            lw = st[:, 384:416].rearrange("p (t h a) -> p t h a", t=2, a=2)
            nm = st[:, 416:448].rearrange("p (t h a) -> p t h a", t=2, a=2)
            wq = st[:, 448:480].rearrange("p (t h a) -> p t h a", t=2, a=2)
            gates = gt.rearrange("p t (h c) -> p t h c", c=3)

            def compressed(tt):
                nonlocal tp_free, ob_free
                for g in range(2):
                    for b in range(4):
                        t = mm([*tqT, tkc, *sc_free[g]], SC[g][:, b * 16:b * 16 + 15],
                               qT[g * 64:g * 64 + 64, b, tt * 128:tt * 128 + 128],
                               kcT[g * 64:g * 64 + 64, 0:15])
                madd = smv("madd").rearrange("p (t c) -> p t c", t=2)[:, tt, 0:15]
                m01 = smv("m01").rearrange("p (t c) -> p t c", t=2)[:, tt, 0:15]
                prev = [pe.last()]
                a = []
                for g in range(2):
                    a.append(dve.do([t, *prev], lambda e, g=g: e.tensor_tensor(
                        cs_[:, g * 4:g * 4 + 4, :], SC[g][:, 0:64].rearrange("p (h c) -> p h c", c=16)[:, :, 0:15],
                        bc(madd, [128, 4, 15], 1), ALU.add)))
                    sc_free[g] = [a[-1]]
                mx, l, r = rt[:, 0:8], st[:, 480:488], st[:, 488:496]
                b_ = dve.do(a, lambda e: e.tensor_reduce(mx, cs_[:, :, :], AXX, ALU.max))
                c_ = dve.do([b_], lambda e: e.tensor_tensor(cs_[:, :, :], cs_[:, :, :], bc(mx, [128, 8, 15], 2),
                                                            ALU.subtract))
                d_ = act.do([c_], lambda e: e.activation(cs_[:, :, :], cs_[:, :, :], ACT.Exp))
                yield
                f_ = dve.do([d_], lambda e: e.tensor_reduce(l, cs_[:, :, :], AXX, ALU.add))
                g_ = dve.do([f_], lambda e: e.reciprocal(r, l))
                h_ = mul(dve, [g_, *tg], r, r, gates[:, tt, :, 0])
                p3 = cp[:, :].rearrange("p (h c) -> p h c", h=8)
                i_ = mul(dve, [d_, *prev], p3, cs_[:, :, :], bc(m01, [128, 8, 15], 1))
                t = transposed([i_, *tp_free], TP[0:120, 0:128], cp[:, :])
                yield
                j_ = copy(act, [t], cpT[0:120, :], TP[0:120, 0:128])
                tp_free = [j_]
                t = mm([j_, tvc, *ob_free], OB[:, :], cpT[0:120, :], VC[0:120, :, :])
                yield
                toa[tt] = dve.do([t, h_], lambda e: e.tensor_tensor(
                    oa[tt][:, :].rearrange("p (h d) -> p h d", h=8), OB[:, :].rearrange("p (h d) -> p h d", h=8),
                    bc(r, [128, 8, 64], 2), ALU.mult))
                ob_free = [toa[tt]]

            def scores(u):
                tt, h = units[u]
                g, b = h // 4, h % 4
                n = 128 * (tt + 1)
                bk = SC[u % 2]
                for a in range(2):
                    mm([*tqT, *sc_free[u % 2]], bk[:, a * S:a * S + n],
                       qT[g * 64:g * 64 + 64, b, tt * 128:tt * 128 + 128], kT[g * 64:g * 64 + 64, a, 0:n],
                       start=(a == 0), stop=False)
                for a in range(2):
                    t = mm([t_c[0], t_mk], bk[:, a * S + n - 128:a * S + n], idb[:, :], mkb[:, :],
                           start=False, stop=True)
                s = bk[:, :].rearrange("p (a k) -> p a k", a=2)
                m = dve.do([t], lambda e: e.tensor_reduce(nm[:, tt, h, :], s[:, :, 0:n], AXX, ALU.max, negate=True),
                           link=False)
                for a in range(2):
                    x_ = act.do([m, *tr_t.get(u - 2, [])], lambda e, a=a: e.activation(
                        Ex[u % 2][:, a, 0:n], s[:, a, 0:n], ACT.Exp, bias=nm[:, tt, h, a:a + 1],
                        accum_out=lw[:, tt, h, a:a + 1]), link=False)
                exp_t[u] = [x_]
                sc_free[u % 2] = [x_]

            def turned(u):
                nonlocal tp_free
                tt, h = units[u]
                nk = tt + 1
                for a in range(2):
                    for k in range(nk):
                        t = transposed([*exp_t[u], *tp_free], TP[:, (a * nk + k) * 128:(a * nk + k) * 128 + 128],
                                       Ex[u % 2][:, a, k * 128:k * 128 + 128])
                tr_t[u] = [t]
                ev_t[u] = copy(act if u % 2 else dve, [t, *pv_t.get(u - 2, [])], ET[u % 2][:, 0:2 * nk, :],
                               TP[:, 0:2 * nk * 128].rearrange("p (k s) -> p k s", k=2 * nk))
                tp_free = [ev_t[u]]

            def values(u):
                nonlocal ob_free
                tt, h = units[u]
                g, nk = h // 4, tt + 1
                for a in range(2):
                    for k in range(nk):
                        t = mm([ev_t[u], *ob_free], OB[:, ((h % 4) * 2 + a) * 64:((h % 4) * 2 + a) * 64 + 64],
                               ET[u % 2][:, a * nk + k, :],
                               qkv[k][:, 896 + 256 * a + 64 * g:896 + 256 * a + 64 * g + 64],
                               start=(k == 0), stop=(k == nk - 1))
                pv_t[u] = [t]
                if h % 4 == 3:
                    hs = slice(h - 3, h + 1)
                    r_ = dve.do(exp_t[u], lambda e: e.reciprocal(wq[:, tt, hs, :], lw[:, tt, hs, :]))
                    w_ = mul(dve, [r_, *tg], wq[:, tt, hs, :], wq[:, tt, hs, :], gates[:, tt, hs, 1:3])
                    o8 = lambda ap: ap.rearrange("p (h d) -> p h d", d=64)
                    m_ = dve.do([w_, t], lambda e: e.tensor_tensor(
                        o8(Tm[:, :]), o8(OB[:, :]),
                        bc(wq[:, tt, hs, :].rearrange("p h a -> p (h a)"), [128, 8, 64], 2), ALU.mult))
                    ob_free = [m_]
                    dst = oa[tt][:, (h - 3) * 64:(h + 1) * 64].rearrange("p (h d) -> p h d", d=64)
                    T4 = Tm[:, :].rearrange("p (h a d) -> p h a d", h=4, a=2)
                    a_ = add(dve, [m_, toa[tt]], dst, dst, T4[:, :, 0, :])
                    toa[tt] = add(dve, [a_], dst, dst, T4[:, :, 1, :])

            yield
            for tt in range(2):
                yield from compressed(tt)
                lo_, hi_ = 8 * tt, 8 * tt + 8
                for s_ in range(lo_, hi_ + 2):
                    if lo_ <= s_ - 1 < hi_:
                        turned(s_ - 1)
                    if lo_ <= s_ - 2:
                        values(s_ - 2)
                    if s_ < hi_:
                        scores(s_)
                    yield

        tqr, tkr, tv, tsg = [], [], [], []
        rab = [None]

        def evac_rot(dstT, toks):
            def evac(tt, ps, t):
                b4 = lambda ap: ap.rearrange("p (h d) -> p h d", h=4)
                free = rab[0] or sum(t_h, [])
                cosb = bc(ctab[:, tt, 0:128], [128, 4, 128], 1)
                a = mul(dve, [t, t_ctab, *free], b4(ra[:, :]), b4(ps), cosb)
                b = mul(dve, [t, *free], b4(rb[:, :])[:, :, 0:64], b4(ps)[:, :, 64:128],
                        bc(ctab[:, tt, 128:192], [128, 4, 64], 1))
                c = mul(dve, [t, *free], b4(rb[:, :])[:, :, 64:128], b4(ps)[:, :, 0:64],
                        bc(ctab[:, tt, 192:256], [128, 4, 64], 1))
                d = add(pool, [a, b, c], ra[:, :], ra[:, :], rb[:, :])
                bk = bank()
                for j in range(4):
                    t2 = transposed([d, *bank_free.get(bk, [])], PB[bk][:, j * 128:j * 128 + 128],
                                    ra[:, j * 128:j * 128 + 128])
                f = copy(act, [t2], dstT[:, :, tt * 128:tt * 128 + 128],
                         PB[bk][:, :].rearrange("p (k s) -> p k s", k=4))
                bank_free[bk] = [f]
                rab[0] = [t2]
                toks.append(f)
                return [a, b, c]
            return evac

        def evac_to(dst, toks, q=None, free=()):
            def evac(tt, ps, t):
                toks.append(copy(q or (act if tt else dve), [t, *free], dst(tt), ps))
                return [toks[-1]]
            return evac

        back = chain(
            rows_out(hhi, hlo, [], evac_rot(qrT, tqr)),
            rows_out(hhi, hlo, [], evac_rot(krT, tkr)),
            rows_out(hhi, hlo, [], evac_to(lambda tt: vr[tt][:, 0:512], tv)),
            rows_out(hhi, hlo, [], evac_to(lambda tt: vr[tt][:, 512:1024], tv)),
            rows_out(hhi, hlo, [], evac_to(lambda tt: sg[:, tt, 0:512], tsg)),
            rows_out(hhi, hlo, [], evac_to(lambda tt: sg[:, tt, 512:1024], tsg)),
        )
        weave(nsa(), back, 2)
        toaT = to_halves_T(oa, 4, oah, oal, [[toa[0]], [toa[1]]])

        t_gnw = load("d_gnw", gnw[:, :], rows[7:8, :].to_broadcast([128, D]), [*rab[0], *tkr])
        nsa_done = everything()
        tor = [[], []]

        def ret():
            s_t, o_t = {}, {}
            mv = st[:, 128:144].rearrange("p (h t c) -> p h t c", h=4, t=2)
            bn = st[:, 144:192].rearrange("p (h t c) -> p h t c", h=4, t=2)
            sf, of = [[*nsa_done], [*nsa_done]], [[*nsa_done], [*nsa_done]]
            stf = {}
            a0 = act.do([*tsg], lambda e: e.activation(sg[:, :, :], sg[:, :, :], ACT.Silu))
            tsil = [mul(pool, [a0, t_gnw], sg[:, tt, :], sg[:, tt, :], gnw[:, :]) for tt in range(2)]
            for h in range(6):
                if 0 <= h - 1 < 4:
                    k = h - 1
                    b = (TP, OB)[k % 2]
                    vs = slice(k * 256, k * 256 + 256)
                    mm([s_t[k], *tv, *of[k % 2]], b[:, 0:256], STt[k % 2][:, 0:128], vr[0][:, vs])
                    mm([], b[:, 256:512], STt[k % 2][:, 128:256], vr[0][:, vs], start=True, stop=False)
                    t = mm([], b[:, 256:512], STt[k % 2][:, 256:384], vr[1][:, vs], start=False, stop=True)
                    stf[k] = [t]
                    for tt in range(2):
                        c = dve.do([t], lambda e, tt=tt: e.bn_stats(bn[:, k, tt, :], b[:, tt * 256:tt * 256 + 256]))
                        c = dve.do([c], lambda e, tt=tt: e.bn_aggr(mv[:, k, tt, :], bn[:, k, tt, :]))
                    rk = st[:, 192 + 2 * k:194 + 2 * k]
                    c = scal(dve, [c], rk, mv[:, k, :, 1], 1.0, EPS, ALU.mult, ALU.add)
                    o_t[k] = power([c], st[:, 200 + 2 * k:202 + 2 * k], rk)
                if h < 4:
                    b = SC[h % 2]
                    mm([*tqr, *tkr, *sf[h % 2]], b[:, 0:256], krT[:, h, 0:128], qrT[:, h, :])
                    t = mm([], b[:, 256:384], krT[:, h, 128:256], qrT[:, h, 128:256])
                    s_t[h] = mul(dve, [t, t_dec, *stf.get(h - 2, [])], STt[h % 2][:, :], b[:, 0:384], dec[:, h, :])
                    sf[h % 2] = [s_t[h]]
                yield
                if 0 <= h - 1 < 4:
                    k = h - 1
                    b = (TP, OB)[k % 2]
                    for tt in range(2):
                        d = scal(dve, [o_t[k], *nsa_done], orr[tt][:, k * 256:k * 256 + 256],
                                 b[:, tt * 256:tt * 256 + 256], mv[:, k, tt, 0:1],
                                 st[:, 200 + 2 * k + tt:201 + 2 * k + tt], ALU.subtract, ALU.mult)
                        tor[tt].append(d)
                    of[k % 2] = [d]
                yield
            for tt in range(2):
                tor[tt] = [mul(dve, [*tor[tt], tsil[tt]], orr[tt][:, :], orr[tt][:, :], sg[:, tt, :])]
                yield

        tgm = []

        def evac_gm(f):
            def evac(p, ps, t):
                tgm.append(copy(act, [t, *nsa_done], gm[:, 2 * f:2 * f + 2, :], ps))
                return [tgm[-1]]
            return evac

        weave(ret(), chain(*[feats_out(hhi, hlo, 8, [], evac_gm(f)) for f in range(8)]), 4)
        torT = to_halves_T(orr, 8, orh, orl, tor)
        tgs = [act.do(tgm, lambda e, f=f: e.activation(gm[:, 8 * f:8 * f + 8, :], gm[:, 8 * f:8 * f + 8, :],
                                                       ACT.Sigmoid)) for f in range(2)]
        ret_done = everything()
        tmg, tm = {}, []

        def evac_ya(f):
            def evac(p, ps, t):
                j = 4 * f + 2 * p
                tmg[j] = mul(dve, [t, *tgs, *ret_done], mg[:, j:j + 2, :], ps, gm[:, j:j + 2, :])
                return [tmg[j]]
            return evac

        def evac_yb(f):
            def evac(p, ps, t):
                j = 2 * f
                a = mul(dve, [t, *tgs], gm[:, 8 + j:10 + j, :], ps, gm[:, 8 + j:10 + j, :])
                b = add(pool, [a, tmg[j]], mg[:, j:j + 2, :], mg[:, j:j + 2, :], gm[:, 8 + j:10 + j, :])
                tm.extend(halves(mh[:, j:j + 2, :], ml[:, j:j + 2, :], mg[:, j:j + 2, :], [b, *ret_done]))
                return [a]
            return evac

        run(chain(*[feats_out(oah, oal, 4, toaT, evac_ya(f)) for f in range(2)]))
        run(chain(*[feats_out(orh, orl, 8, torT, evac_yb(f)) for f in range(4)]))
        run(chain(*[rows_out(mh, ml, tm, add_to_x(512 * f)) for f in range(2)]))

        ghi = at("ghi", P, [128, NFT, S], R32)
        glo = at("glo", P + 22, [128, NFT, S], R32)
        fu = [at(f"fu{i}", P + 56 + 2 * i, [128, 2, S]) for i in range(2)]
        fs = [at(f"fs{i}", P + 60 + i, [128, S]) for i in range(2)]
        fg = [at(f"fg{i}", P + 62 + i, [128, S]) for i in range(2)]

        def ffn(conv):
            nonlocal x_done
            gi, ready = (1, x_done) if conv else (3 + 2 * conv_l[0], x_done)
            x_done = [[[], []], [[], []]]
            th = norm(gi if conv else gi + 1, ready)
            busy = everything()
            tgx, used = [], {}
            fc = smv("fconv").rearrange("p (f v c) -> p f v c", f=NFT, v=2)

            later = []

            def split_g(f, d):
                def go():
                    used[f] = halves(ghi[:, f, :], glo[:, f, :], fg[f % 2][:, :], [d, *busy])
                    tgx.append(used[f])
                return go

            def gate_g(f, b):
                def go():
                    c = act.do([b], lambda e: e.activation(fs[f % 2][:, :], fu[f % 2][:, 0, :], ACT.Silu),
                               link=False)
                    d = pool.do([c, b], lambda e: e.tensor_tensor(
                        fg[f % 2][:, :], fs[f % 2][:, :], fu[f % 2][:, 1, :], ALU.mult), link=False)
                    later.append(split_g(f, d))
                return go

            def evac(f):
                def ev(p, ps, t):
                    while later:
                        go = later.pop(0)
                        n = len(later)
                        go()
                        if len(later) > n:
                            break
                    u, s_, g = fu[f % 2], fs[f % 2], fg[f % 2]
                    free = [*used.get(f - 2, busy)]
                    if conv:
                        for v in range(2):
                            a = act.do([t, *free], lambda e: e.activation(
                                u[:, v, :], ps[:, v, :], ACT.Identity, scale=fc[:, f, v, 2:3], bias=fc[:, f, v, 3:4]),
                                link=False)
                        b = [a, a]
                        for j in (1, 2):
                            for v in range(2):
                                b[v] = dve.do([b[v]], lambda e: e.scalar_tensor_tensor(
                                    u[:, v, j:S], ps[:, v, 0:S - j], fc[:, f, v, 2 - j:3 - j], u[:, v, j:S],
                                    ALU.mult, ALU.add), link=False)
                        later.append(gate_g(f, b[1]))
                        return [b[1]]
                    c = act.do([t, *free], lambda e: e.activation(s_[:, :], ps[:, 0, :], ACT.Silu), link=False)
                    d = dve.do([c, *free], lambda e: e.tensor_tensor(g[:, :], ps[:, 1, :], s_[:, :], ALU.mult),
                               link=False)
                    later.append(split_g(f, d))
                    return [d]
                return ev

            run(chain(*[feats_out(hhi, hlo, 8, th, evac(f)) for f in range(NFT)]))
            while later:
                later.pop(0)()
            b0 = [bank() for _ in range(4)]
            for c in range(NFT // 2):
                i, (_, wh, wl) = take()
                order = [(k, tt) for k in range(2) for tt in range(2)]
                if c == NFT // 2 - 1:
                    order = [(k, tt) for tt in range(2) for k in range(2)]
                for k, tt in order:
                    kg = 2 * c + k
                    for half in range(2):
                        b = b0[tt * 2 + half]
                        sl = slice(tt * 128, tt * 128 + 128)
                        cs = slice(half * 512, half * 512 + 512)
                        after = [*split[i], *tgx[kg], *(bank_free.get(b, []) if kg == 0 else [])]
                        t = mm3(PB[b][:, :], ghi[:, kg, sl], glo[:, kg, sl], wh[:, k, cs], wl[:, k, cs],
                                kg == 0, kg == NFT - 1, after)
                        if t:
                            bank_free[b] = add_to_x(half * 512)(tt, PB[b][:, :], t)
                taken(i, t or pe.mark())

        conv_l = [0]
        ffn(True)
        ready = norm(2, x_done, final=True)

        ath, atl, cvh, cvl, frh, frl = (at(n, P + 4 * j, [128, 4, S], R32) for j, n in
                                        enumerate(("ath", "atl", "cvh", "cvl", "frh", "frl")))
        gm2 = at("gm2", P + 24, [128, 24, S])
        Z = P + 48
        q2T = at("q2T", Z, [128, 4, S])
        k2T = at("k2T", Z + 4, [128, 4, S])
        v2 = [at(f"v2{t}", Z + 8 + 2 * t, [128, 512]) for t in range(2)]
        gp = at("gp", Z + 12, [128, 4, 288])
        Y = Z + 16.5
        qn = [at(f"qn{t}", Y + (0, 2, 6, 8)[t], [128, 512]) for t in range(4)]
        sq = at("sq", Y + 4, [128, 512])
        xf = [at(f"xf{t}", Y + 6 + 2 * t, [128, 512]) for t in range(2)]
        T12 = [at(f"T12{t}", Y + 10 + 2 * t, [128, 512]) for t in range(2)]
        csT = at("csT", Y + 14, [128, 2, 512])
        cdT = at("cdT", Y + 18, [128, 2, 128])
        E2 = [at(f"E2{t}", Y + 2 * t, [128, 2, S]) for t in range(2)]
        W2 = [at(f"W2{t}", Y + 4 + t, [128, S]) for t in range(2)]
        WT = [at(f"WT{t}", Y + 6 + 2 * t, [128, 2, S]) for t in range(2)]
        o2 = at("o2", Y + 10, [128, 2, 512])
        csq = at("csq", Y + 14, [128, 4, S])
        cv = at("cv", Y + 20, [128, 4, S])
        mh2 = at("mh2", Z, [128, 8, S], R32)
        ml2 = at("ml2", Z + 8, [128, 8, S], R32)
        mg2 = at("mg2", Z + 16, [128, 8, S])
        mt2 = [at(f"mt2{t}", Z + 24 + 2 * t, [128, 2, S]) for t in range(2)]
        rope4 = smv("rope4").rearrange("p (t a n) -> p t a n", t=2, a=2)
        o2q = [o2[:, tt, :] for tt in range(2)]

        def layer(l):
            nonlocal x_done, ready
            li = 0.8 - 0.6 * math.exp(-0.3 * l)
            th = norm(3 + 2 * l, ready)
            busy = everything()
            tcs = load(f"d_cs{l}", csT[:, :, :], tabs["cs"], busy)
            tcd = load(f"d_cd{l}", cdT[:, :, :], tabs["cd"], busy)
            lam = smv("lam").rearrange("p (l a d) -> p l a d", l=2, a=4)[:, l, :, :]
            lp = st[:, 256:320].rearrange("p (a d) -> p a d", a=2)
            nl = st[:, 8 + 4 * l:12 + 4 * l]
            a = mul(dve, [t_sm], lp, lam[:, 0:4:2, :], lam[:, 1:4:2, :])
            a = dve.do([a], lambda e: e.tensor_reduce(nl[:, 0:2], lp, AXX, ALU.add))
            a = act.do([a], lambda e: e.activation(nl[:, 0:2], nl[:, 0:2], ACT.Exp))
            tlam = dve.do([a], lambda e: e.scalar_tensor_tensor(
                nl[:, 2:3], nl[:, 1:2], -li, nl[:, 0:1], ALU.add, ALU.subtract))
            neglam = nl[:, 2:3]
            tz = pool.do(busy, lambda e: e.memset(gp[:, :, :], 0.0))

            tT, tv2, trq = {0: [], 1: []}, [], {}
            qfree = [[], [], [], []]

            def evac_qk(w):
                def evac(tt, ps, t):
                    n = 2 * w + tt
                    g16 = lambda ap: ap.rearrange("p (g d) -> p g d", d=32)
                    ss = st[:, 128 + 16 * n:144 + 16 * n]
                    rs = st[:, 192 + 16 * n:208 + 16 * n]
                    a = act.do([t, *busy, *trq.get("sq", [])], lambda e: e.activation(sq[:, :], ps, ACT.Square))
                    b = dve.do([a], lambda e: e.tensor_reduce(ss, g16(sq[:, :]), AXX, ALU.add))
                    trq["sq"] = [b]
                    k = 1.0 if w == 0 else 1.0 / 32
                    c = scal(dve, [b], ss, ss, k, EPS * 32 * k, ALU.mult, ALU.add)
                    d = power([c], rs, ss)
                    q = qn[n]
                    f = dve.do([d, *busy], lambda e: e.tensor_tensor(
                        g16(q[:, :]), g16(ps), bc(rs, [128, 16, 32], 2), ALU.mult))
                    gg = smv("qkg").rearrange("p (l w d) -> p l w d", l=2, w=2)[:, l, w, :]
                    g = mul(pool, [f], g16(q[:, :]), g16(q[:, :]), bc(gg, [128, 16, 32], 1))
                    t1, t2 = (st[:, o:o + 128].rearrange("p (g d) -> p g d", d=8) for o in (256, 384))
                    r = rope_small(pool, g16(q[:, :])[:, :, 0:8], [128, 16, 8], tt, rope4, 4, t1, t2, [g, tlam])
                    pend.append((w, tt, q, r, n))
                    return [f, a]
                return evac

            pend = []

            def turn_qk():
                for w, tt, q, r, n in pend:
                    b = bank()
                    for j in range(4):
                        t = transposed([r, *bank_free.get(b, [])], PB[b][:, j * 128:j * 128 + 128],
                                       q[:, j * 128:j * 128 + 128])
                    c = copy(act, [t], (q2T, k2T)[w][:, :, tt * 128:tt * 128 + 128],
                             PB[b][:, :].rearrange("p (k s) -> p k s", k=4))
                    bank_free[b] = [c]
                    qfree[n] = [t]
                    tT[w].append(c)
                pend.clear()

            tgl, txf = [], []
            tconv = [[], [], [], []]
            cwv = smv("cw").rearrange("p (l f j) -> p l f j", l=2, f=4)[:, l, :, :]
            cvec = smv("cvec").rearrange("p (l a f) -> p l a f", l=2, a=3)[:, l, :, :]
            todo = [(f, j) for j in range(31) for f in range(4)]

            def conv_some(n):
                for _ in range(n):
                    if not todo:
                        return
                    f, j = todo.pop(0)
                    if j == 0:
                        tconv[f] = [dve.do([*tgl, *busy, t_sm], lambda e: e.tensor_scalar(
                            cv[:, f, :], gp[:, f, 0:S], cwv[:, f, 0:1], cvec[:, 0, f:f + 1], ALU.mult, ALU.add),
                            link=False)]
                    else:
                        tconv[f] = [dve.do(tconv[f], lambda e: e.scalar_tensor_tensor(
                            cv[:, f, :], gp[:, f, j:j + S], cwv[:, f, j:j + 1], cv[:, f, :], ALU.mult, ALU.add),
                            link=False)]


            def evac_glu(f):
                def evac(p, ps, t):
                    a = act.do([t, *busy, *trq["sq"], *tgl[-1:]], lambda e: e.activation(sq[:, 0:S], ps[:, 1, :], ACT.Sigmoid))
                    b = mul(dve, [a, tz], gp[:, f, 15:15 + S], ps[:, 0, :], sq[:, 0:S])
                    tgl.append(b)
                    return [b]
                return evac

            run(rows_out(hhi, hlo, th, evac_qk(0)))
            run(rows_out(hhi, hlo, [], evac_qk(1)))
            for f in range(4):
                run(feats_out(hhi, hlo, 8, [], evac_glu(f)))
                if f == 1:
                    turn_qk()
            for _ in rows_out(hhi, hlo, [], evac_to(lambda tt: v2[tt][:, :], tv2)):
                conv_some(2)
            for _ in rows_out(hhi, hlo, [], evac_to(lambda tt: xf[tt][:, :], txf, None, [*qfree[2], *qfree[3]])):
                conv_some(2)

            tgm2, tgs2, direct = [], [], []
            bgv = smv("bg").rearrange("p (l f) -> p l f", l=2)[:, l, :]

            def evac_g(f):
                def evac(p, ps, t):
                    for v in range(2):
                        a = act.do([t, *busy], lambda e, v=v: e.activation(
                            gm2[:, 2 * f + v, :], ps[:, v, :], ACT.Sigmoid if direct else ACT.Identity,
                            bias=bgv[:, 2 * f + v:2 * f + v + 1]), link=False)
                    (tgs2 if direct else tgm2).append(a)
                    return [a]
                return evac

            back = chain(*[feats_out(hhi, hlo, 8, [], evac_g(f)) for f in range(12)])

            tfr = []

            def fourier():
                tf, ev = {}, {}
                for g in range(5):
                    if g >= 1:
                        k = g - 1
                        o = OB[:, 0:256]
                        fr = ev.get("o", busy)
                        mm([tf[k], tcd, *fr], o, cdT[:, 0, :], T12[k % 2][:, 0:256], start=True, stop=False)
                        t = mm([], o, cdT[:, 1, :], T12[k % 2][:, 256:512], start=False, stop=True)
                        ev[k] = [t]
                        h = halves(frh[:, k, :], frl[:, k, :], o, [t, *busy])
                        ev["o"] = h
                        tfr.extend(h)
                    if g < 4:
                        for tt in range(2):
                            t = mm([*txf, tcs, *busy, *([tf[g - 2]] if g >= 2 else [])], SC[g % 2][:, :],
                                   xf[tt][:, g * 128:g * 128 + 128], csT[:, tt, :], start=(tt == 0), stop=(tt == 1))
                        tf[g] = copy(act, [t, *ev.get(g - 2, busy)], T12[g % 2][:, :], SC[g % 2][:, :])
                    yield

            to2 = []
            def attention():
                done1 = everything()
                scf, tpf, obf = [done1, done1], done1, done1
                ex, trn, wv, pv = {}, {}, {}, {}
                lw = st[:, 128:160].rearrange("p (h t c) -> p h t c", h=8, t=2)
                nm = st[:, 160:192].rearrange("p (h t c) -> p h t c", h=8, t=2)
                rr = st[:, 192:224].rearrange("p (h t c) -> p h t c", h=8, t=2)
                cc = st[:, 224:240].rearrange("p (h t) -> p h t", h=8)
                wtf = {}
                yield
                for u in range(19):
                    if 0 <= u - 1 < 16:
                        n = u - 1
                        h, tt = n // 2, n % 2
                        for k in range(2):
                            t = transposed([wv[n], *(tpf if tt == 0 else [])],
                                           TP[:, k * 256 + tt * 128:k * 256 + tt * 128 + 128],
                                           W2[n % 2][:, k * 128:k * 128 + 128])
                        trn[n] = [t]
                        if tt == 1:
                            a = copy(act, [t, *pv.get(h - 2, done1)], WT[h % 2][:, :, :],
                                     TP[:, :].rearrange("p (k s) -> p k s", k=2))
                            tpf = [a]
                            wtf[h] = a
                    if u >= 3 and (u - 3) % 2 == 0:
                        h = (u - 3) // 2
                        for tt in range(2):
                            for k in range(2):
                                t = mm([wtf[h], *tv2, *obf],
                                       OB[:, (tt * 4 + h % 4) * 64:(tt * 4 + h % 4) * 64 + 64],
                                       WT[h % 2][:, k, tt * 128:tt * 128 + 128], v2[k][:, h * 64:h * 64 + 64],
                                       start=(k == 0), stop=(k == 1))
                        pv[h] = [t]
                        if h % 4 == 3:
                            for tt in range(2):
                                b = dve.do([t, *done1], lambda e, tt=tt, h=h: e.tensor_tensor(
                                    o2[:, tt, (h - 3) * 64:(h + 1) * 64].rearrange("p (h d) -> p h d", d=64),
                                    OB[:, tt * 256:tt * 256 + 256].rearrange("p (h d) -> p h d", d=64),
                                    bc(rr[:, h - 3:h + 1, tt, 0], [128, 4, 64], 2), ALU.mult))
                                to2.append(b)
                            obf = [b]
                    if u < 16:
                        h, tt = u // 2, u % 2
                        rg = slice((h % 4) * 32, (h % 4) * 32 + 32)
                        bk = SC[u % 2]
                        for c in range(2):
                            t = mm([*tT[0], *tT[1], *scf[u % 2]], bk[:, c * S:c * S + S],
                                   q2T[rg, c * 2 + h // 4, tt * 128:tt * 128 + 128], k2T[rg, c * 2 + h // 4, :])
                        s = bk[:, :].rearrange("p (c k) -> p c k", c=2)
                        m = dve.do([t], lambda e, s=s, h=h, tt=tt: e.tensor_reduce(
                            nm[:, h, tt, :], s, AXX, ALU.max, negate=True), link=False)
                        for c in range(2):
                            a = act.do([m, *([wv[u - 2]] if u >= 2 else done1)], lambda e, c=c, s=s, h=h, tt=tt, u=u:
                                       e.activation(E2[u % 2][:, c, :], s[:, c, :], ACT.Exp,
                                                    bias=nm[:, h, tt, c:c + 1], accum_out=lw[:, h, tt, c:c + 1]),
                                       link=False)
                        scf[u % 2] = [a]
                        b = dve.do([a], lambda e, h=h, tt=tt: e.reciprocal(rr[:, h, tt, :], lw[:, h, tt, :]))
                        c_ = dve.do([b, tlam], lambda e, h=h, tt=tt: e.tensor_scalar(
                            cc[:, h, tt:tt + 1], lw[:, h, tt, 0:1], neglam, rr[:, h, tt, 1:2], ALU.mult, ALU.mult))
                        wv[u] = dve.do([c_, *trn.get(u - 2, done1)], lambda e, h=h, tt=tt, u=u: e.scalar_tensor_tensor(
                            W2[u % 2][:, :], E2[u % 2][:, 1, :], cc[:, h, tt:tt + 1], E2[u % 2][:, 0, :],
                            ALU.mult, ALU.add))
                    conv_some(4)
                    yield

            tat, tcv = [], []

            def after_attention():
                o16 = o2[:, :, :].rearrange("p t (h d) -> p (t h) d", d=64)
                sqv = csq[:, :, :].rearrange("p f s -> p (f s)")
                ss, rs = st[:, 240:256], st[:, 256:272]
                a = act.do([*to2], lambda e: e.activation(
                    sqv, o2[:, :, :].rearrange("p t n -> p (t n)"), ACT.Square))
                b = dve.do([a], lambda e: e.tensor_reduce(ss, sqv.rearrange("p (g d) -> p g d", d=64), AXX, ALU.add))
                z = (1 - li) ** 2
                c = scal(dve, [b], ss, ss, 1.0 / 64 / z, EPS / z, ALU.mult, ALU.add)
                d = power([c], rs, ss)
                yield
                conv_some(len(todo))
                allcv = [t for f in range(4) for t in tconv[f]]
                for f in range(4):
                    t = mm([*allcv, *everything()] if f == 0 else [], SC[0][:, 0:S], ones, cv[:, f, :],
                           start=(f == 0), stop=(f == 3))
                for f in range(4):
                    m = dve.do([t], lambda e, f=f: e.scalar_tensor_tensor(
                        cv[:, f, :], SC[0][:, 0:S], -1.0 / 512, cv[:, f, :], ALU.mult, ALU.add))
                q = act.do([m, b], lambda e: e.activation(csq[:, :, :], cv[:, :, :], ACT.Square))
                yield
                f1 = mul(dve, [d, *to2], o16, o16, bc(rs, [128, 16, 64], 2))
                sgv = smv("subg").rearrange("p (l d) -> p l d", l=2)[:, l, :]
                f2 = mul(pool, [f1], o16, o16, bc(sgv, [128, 16, 64], 1))
                for tt in range(2):
                    for f in range(4):
                        t = mm([q], SC[1][:, tt:tt + 1], csq[:, f, tt * 128:tt * 128 + 128], ones[:, 0:1],
                               start=(f == 0), stop=(f == 3))
                vs, vr_ = st[:, 272:274], st[:, 274:276]
                g = scal(dve, [t], vs, SC[1][:, 0:2], 1.0 / 512, EPS, ALU.mult, ALU.add)
                h = power([g], vr_, vs)
                rb2 = W2
                yield
                for tt in range(2):
                    k = copy(dve, [h], rb2[tt][:, 0:128], vr_[:, tt:tt + 1].to_broadcast([128, 128]))
                    t = mm([k, t_sm], SC[0][:, tt * 128:tt * 128 + 128], rb2[tt][:, 0:128], ident)
                m = dve.do([t], lambda e: e.tensor_tensor(cv[:, :, :], cv[:, :, :], bc(SC[0][:, 0:S], [128, 4, S], 1),
                                                          ALU.mult))
                yield
                tat.extend(to_halves_T(o2q, 4, ath, atl, [[f2], [f2]]))
                for f in range(4):
                    n = act.do([m], lambda e, f=f: e.activation(
                        csq[:, f, :], cv[:, f, :], ACT.Silu, scale=cvec[:, 1, f:f + 1], bias=cvec[:, 2, f:f + 1]))
                tcv.extend(halves(cvh[:, :, :], cvl[:, :, :], csq[:, :, :], [n]))
                yield

            def front():
                for _ in fourier():
                    conv_some(6)
                    yield
                yield from attention()
                n = 2 * len(tgm2)
                direct.append(1)
                for g in range(0, n, 6):
                    m = min(g + 6, n)
                    tgs2.append(act.do(tgm2, lambda e: e.activation(gm2[:, g:m, :], gm2[:, g:m, :], ACT.Sigmoid),
                                       link=False))
                yield from after_attention()

            weave(front(), back, 3)
            done2 = everything()
            tmg2, tm2 = {}, []

            def evac_y(n, f):
                def evac(p, ps, t):
                    j = 4 * f + 2 * p
                    g = gm2[:, 8 * n + j:8 * n + j + 2, :]
                    if n == 0:
                        tmg2[j] = mul(dve, [t, *tgs2, *done2], mg2[:, j:j + 2, :], ps, g)
                        return [tmg2[j]]
                    a = mul(dve, [t, *tgs2], g, ps, g)
                    tmg2[j] = add(pool, [a, tmg2[j]], mg2[:, j:j + 2, :], mg2[:, j:j + 2, :], g)
                    if n == 2:
                        tm2.extend(halves(mh2[:, j:j + 2, :], ml2[:, j:j + 2, :], mg2[:, j:j + 2, :],
                                          [tmg2[j], *done2]))
                    return [a]
                return evac

            for n, (hi, lo, tk) in enumerate(((ath, atl, tat), (cvh, cvl, tcv), (frh, frl, tfr))):
                run(chain(*[feats_out(hi, lo, 4, tk, evac_y(n, f)) for f in range(2)]))
            x_done = [[[], []], [[], []]]
            run(chain(*[rows_out(mh2, ml2, tm2, add_to_x(512 * f)) for f in range(2)]))
            conv_l[0] = l
            ffn(False)
            ready = x_done

        for l in range(2):
            layer(l)

        s_out = sem("s_out")
        for tt in range(2):
            t = sp.dma(sum(ready[tt], []), s_out, 16 * (tt + 1),
                       lambda e, tt=tt: e.dma_start(out[tt * 128:(tt + 1) * 128, :], x[:, tt, :]))
        sp.wait([t])



def _pack(arrays):
    f = np.float32
    parts = []
    for name, layer, cs, k0, kk, _ in chunk_plan():
        w = arrays[name][layer]
        b = w[k0 * 128:(k0 + kk) * 128, :][:, np.asarray(cs)]
        parts.append(np.ascontiguousarray(b.reshape(kk, 128, len(cs)).transpose(1, 0, 2)).reshape(-1))
    return np.concatenate(parts)


def _small(a):
    f = np.float32
    sm = np.zeros((128, NSMALL), f)

    def put(name, v):
        o, n = SOFF[name]
        v = np.asarray(v)
        v = v.reshape(v.shape[0], -1)
        assert v.shape[1] == n, (name, v.shape)
        sm[:v.shape[0], o:o + n] = v

    def every(v):
        return np.broadcast_to(np.asarray(v).reshape(1, -1), (128, np.asarray(v).size))

    put("ident", np.eye(128, dtype=f))
    put("ones", np.ones((128, 128), f))
    put("mhalf", np.full((128, 16), -0.5, f))

    def rope(dim, theta):
        half = dim // 2
        inv = np.power(f(theta), -np.arange(half, dtype=f) / f(half)).astype(f)
        ang = (np.arange(S, dtype=f)[:, None] * inv[None, :]).astype(f).astype(np.float64)
        c, s = np.cos(ang).astype(f), np.sin(ang).astype(f)
        t = np.stack([np.concatenate([c, c], 1), np.concatenate([-s, s], 1)], 1)
        return t.reshape(2, 128, 2, dim).transpose(1, 0, 2, 3)

    put("ropen", rope(16, 500000.0))
    put("rope4", rope(8, 500000.0))
    ctab = np.ascontiguousarray(rope(128, 10000.0).reshape(128, 2, 256))
    seen = (np.arange(16)[None, :] * 16 + 31 <= np.arange(S)[:, None])
    put("madd", np.where(seen, 0.0, NEG).astype(f).reshape(2, 128, 16).transpose(1, 0, 2))
    put("m01", seen.astype(f).reshape(2, 128, 16).transpose(1, 0, 2))
    put("bm", (np.arange(120)[:, None] // 15 == np.arange(8)[None, :]).astype(f))
    put("w2k", a["cmp_w2_k"][0].reshape(2, 128, 64).transpose(1, 0, 2))
    put("w2v", a["cmp_w2_v"][0].reshape(2, 128, 64).transpose(1, 0, 2))
    put("pe", np.stack([a[n][0].reshape(16, 128).T for n in ("cmp_pe_k", "cmp_pe_v")], 1))
    fc = np.concatenate([a["ffn_conv_w"][0], a["ffn_conv_b"]], 0)
    put("fconv", fc.reshape(4, 2, NFT, 128).transpose(3, 2, 1, 0))
    put("lam", every(np.stack([a[n] for n in ("lambda_q1_2", "lambda_k1_2", "lambda_q2_2", "lambda_k2_2")], 1)))
    put("qkg", every(np.stack([a["qnorm_g_2"], a["knorm_g_2"]], 1)))
    put("subg", every(a["subln_g_2"]))
    put("cw", a["conv_w_2"].reshape(2, 31, 4, 128).transpose(3, 0, 2, 1))
    put("cvec", np.stack([a[n].reshape(2, 4, 128) for n in ("conv_b_2", "conv_ln_g_2", "conv_ln_b_2")], 1)
        .transpose(3, 0, 1, 2))
    put("bg", a["b_gate_2"].reshape(2, 24, 128).transpose(2, 0, 1))
    lg = np.log1p(-np.exp2(-5.0 - np.arange(4, dtype=np.float64)))
    j, i = np.arange(128)[:, None], np.arange(256)[None, :]
    full = np.concatenate([i - j, (i - j)[:, 0:128]], 1)[:, None, :]
    dec = np.where(full >= 0, np.exp(lg[None, :, None] * np.maximum(full, 0)), 0.0) * 128 ** -0.5
    n = np.arange(256)
    cs = 2 * np.pi * ((n[:, None] * n[None, :]) % 256) / 256
    cs = np.concatenate([np.cos(cs), np.sin(cs)], 1).astype(f).reshape(2, 128, 512).transpose(1, 0, 2)
    m = np.arange(128)
    cd = 2 * np.pi * ((m[:, None] * m[None, :]) % 128) / 128
    cd = (np.stack([np.cos(cd), -np.sin(cd)], 1) / math.sqrt(256 * 128)).astype(f)
    return sm, {"dec": dec.astype(f), "ctab": ctab, "cs": np.ascontiguousarray(cs), "cd": cd}


def kernel(**inputs):
    import concourse.bacc as _bacc
    from concourse import mybir as _mybir
    from concourse.bass_utils import run_bass_kernel_spmd as _run

    a = {k: np.asarray(v) for k, v in inputs.items()}
    sm, tabs = _small(a)
    rows = np.stack([a["norm_mix_w"][0], a["norm_ffn_w"][0], a["norm_final_w"],
                     a["norm1_g_2"][0], a["norm2_g_2"][0], a["norm1_g_2"][1], a["norm2_g_2"][1],
                     a["ret_gn_w"][0].reshape(-1)])
    arrays = {"in_w": _pack(a), "in_small": sm, "in_rows": rows,
              "in_x": np.ascontiguousarray(a["x"][0])}
    arrays.update({f"in_{k}": v for k, v in tabs.items()})
    nc = _bacc.Bacc("TRN2", target_bir_lowering=False, num_devices=1)
    d = {k: nc.dram_tensor(k, v.shape, _mybir.dt.from_np(v.dtype), kind="ExternalInput").ap()
         for k, v in arrays.items()}
    out = nc.dram_tensor("out_0", (S, D), _mybir.dt.float32, kind="ExternalOutput").ap()
    program(nc, d["in_w"], d["in_small"], {k: d[f"in_{k}"] for k in tabs}, d["in_rows"], d["in_x"], out)
    r = _run(nc, [arrays], core_ids=[0])
    return r.results[0]["out_0"].reshape(1, S, D)
```

```python
import math
from contextlib import ExitStack

import numpy as np

import concourse.bass as bass
from concourse import mybir

F32 = mybir.dt.float32
R32 = mybir.dt.float32r
BF16 = mybir.dt.bfloat16
ALU = mybir.AluOpType
ACT = mybir.ActivationFunctionType
AXX = mybir.AxisListType.X

D = 1024
S = 256
EPS = 1e-6
NEG = -1e30
FF = 2816
NFT = FF // 128
CW = 2048
NRAW, NHL, AHEAD = 4, 3, 2


def cols(*spans):
    return [c for a, n in spans for c in range(a, a + n)]


def chunk_plan():
    plan = []

    def wide(name, layer, cs, nk, per, split=True):
        for k in range(0, nk, per):
            plan.append((name, layer, cs, k, per, split))

    def in1(a, n):
        wide("w_in", 0, cols((a, n)), 8, 4)

    wide("w_in", 0, cols(*[(64 * h, 64) for h in (0, 4, 1, 5, 2, 6, 3, 7)]), 8, 4)
    in1(512, 512)
    in1(1024, 280)
    in1(1304, 512)
    wide("cmp_w1_k", 0, cols((0, 256)), 16, 8)
    wide("cmp_w1_v", 0, cols((0, 256)), 16, 8)
    for a in range(1816, 4376, 512):
        in1(a, 512)
    for f in range(8):
        wide("w_in", 0, cols((4376 + 256 * f, 256)), 8, 8)
    for f in range(2):
        wide("w_nsa_branch", 0, cols((512 * f, 512)), 4, 4)
    for f in range(4):
        wide("w_ret_branch", 0, cols((256 * f, 256)), 8, 8)
    for f in range(2):
        wide("w_mix_out", 0, cols((512 * f, 512)), 8, 4)
    for f in range(NFT):
        wide("w_ffn_up", 0, cols((128 * f, 128), (FF + 128 * f, 128)), 8, 8)
    wide("w_ffn_down", 0, cols((0, 1024)), NFT, 2)
    for l in range(2):
        qk = [64 * h + 32 * c + d for c in range(2) for h in range(8) for d in range(32)]
        wide("w_in_2", l, cols((1024, 512)), 8, 4)
        for f in range(4):
            wide("w_in_2", l, cols((1536 + 128 * f, 128), (2048 + 128 * f, 128)), 8, 8)
        wide("w_in_2", l, [512 + c for c in qk], 8, 4)
        wide("w_in_2", l, qk, 8, 4)
        wide("w_in_2", l, cols((2560, 512)), 8, 4)
        for f in (8, 9, 10, 11, 0, 1, 2, 3, 4, 5, 6, 7):
            wide("w_gate_2", l, cols((256 * f, 256)), 8, 8)
        for n in "cab":
            for f in range(2):
                wide(f"w_proj_{n}_2", l, cols((512 * f, 512)), 4, 4)
        for f in range(2):
            wide("w_out_2", l, cols((512 * f, 512)), 8, 4)
        for f in range(NFT):
            wide("w_ffn_in_2", l, cols((128 * f, 128), (FF + 128 * f, 128)), 8, 8)
        wide("w_ffn_out_2", l, cols((0, 1024)), NFT, 2)
    return plan


SMALL = [
    ("ident", 128), ("mhalf", 16), ("ropen", 64), ("ones", 128), ("madd", 32), ("m01", 32), ("bm", 8),
    ("w2k", 128), ("w2v", 128), ("pe", 32), ("fconv", 4 * 2 * NFT),
    ("lam", 256), ("qkg", 128), ("subg", 128), ("cw", 248), ("cvec", 24), ("bg", 48), ("rope4", 32),
]
NEARLY = 208
SOFF, _n = {}, 0
for _name, _w in SMALL:
    SOFF[_name] = (_n, _w)
    _n += _w
NSMALL = _n


class Token:

    def __init__(self, sem, count):
        self.sem, self.count = sem, count


class Queue:

    def __init__(self, engine, sem, linked=False):
        self.linked = linked
        self.engine, self.sem, self.count, self.waited, self.prev = engine, sem, 0, {}, None

    def wait(self, tokens):
        for t in tokens:
            if t is not None and self.waited.get(t.sem.num, 0) < t.count:
                self.waited[t.sem.num] = t.count
                self.engine.wait_ge(t.sem, t.count)

    def do(self, after, make, link=True):
        if self.linked and link:
            self.wait([self.last()])
        self.quiet(after, make)
        return self.mark()

    def quiet(self, after, make):
        self.wait(after)
        self.prev = make(self.engine)

    def mark(self):
        self.prev.then_inc(self.sem, 1)
        self.count += 1
        return self.last()

    def dma(self, after, sem, count, make):
        self.wait(after)
        make(self.engine).then_inc(sem, 16)
        return Token(sem, count)

    def last(self):
        return Token(self.sem, self.count)


def program(nc, wts, small, tabs, rows, x_in, out):
    ctx = ExitStack()
    with ctx:
        base = 16640

        def at(name, kb, shape, dt=F32):
            n = int(np.prod(shape[1:])) * (2 if dt == BF16 else 4)
            assert base + int(kb * 1024) + n <= 229344, name
            return nc.alloc_sbuf_tensor_at(name, shape, dt, offset=base + int(kb * 1024))

        def sem(name):
            return ctx.enter_context(nc.semaphore(name))

        raw = [at(f"raw{i}", 8 * i, [128, CW]) for i in range(NRAW)]
        whi = [at(f"whi{i}", 32 + 8 * i, [128, CW], R32) for i in range(NHL)]
        wlo = [at(f"wlo{i}", 56 + 8 * i, [128, CW], R32) for i in range(NHL)]
        x = at("x", 80, [128, 2, D])
        hhi = at("hhi", 88, [128, 8, S], R32)
        hlo = at("hlo", 96, [128, 8, S], R32)
        gain = at("gain", 104, [128, D])
        sm = at("sm", 108, [128, NSMALL])
        P0 = 108 + (NSMALL * 4 + 1023) // 1024
        idb = at("idb", P0, [128, 128], BF16)
        mkb = at("mkb", P0 + 0.25, [128, 128], BF16)
        st = at("st", P0 + 0.5, [128, 512])
        P = P0 + 2.5
        assert P <= 119, P

        def smv(name):
            a, n = SOFF[name]
            return sm[:, a:a + n]

        ident, ones = smv("ident"), smv("ones")

        PS = [ctx.enter_context(nc.psum_tensor(f"ps{i}", [128, 512], F32)) for i in range(8)]
        PB = PS[0:4]
        SC, TP, OB = PS[4:6], PS[6], PS[7]

        pe, act, dve, pool, sp = (Queue(e, sem(n), n in ("s_act", "s_dve", "s_pool")) for e, n in (
            (nc.tensor, "s_pe"), (nc.scalar, "s_act"), (nc.vector, "s_dve"), (nc.gpsimd, "s_pool"),
            (nc.sync, "s_sp")))

        def everything():
            return [pe.last(), act.last(), dve.last(), pool.last()]

        def load(name, dst, src, after=()):
            s = sem(name)
            return sp.dma(after, s, 16, lambda e: e.dma_start(dst, src))

        def load_x(t):
            t_x.append(load(f"d_x{t}", x[:, t, :], x_in[t * 128:(t + 1) * 128, :]))

        t_x = []
        load_x(0)
        t_sm = load("d_sm", sm[:, 0:NEARLY], small[:, 0:NEARLY])
        gain_sem = sem("d_gain")
        gain_n = [0]

        def load_gain(i, after):
            gain_n[0] += 1
            src = rows[i:i + 1, :].to_broadcast([128, D])
            return sp.dma(after, gain_sem, 16 * gain_n[0], lambda e: e.dma_start(gain[:, :], src))

        t_gain = load_gain(0, [])
        t_sm2 = None

        plan = chunk_plan()
        offs, n = [], 0
        for _, _, cs, _, kk, _ in plan:
            offs.append(n)
            n += 128 * kk * len(cs)
        raw_sem = [sem(f"d_w{i}") for i in range(NRAW)]
        raw_free = {}
        landed, split, hl_free = {}, {}, {}
        nxt = {"dma": 0, "split": 0, "use": 0}

        def run_dmas():
            nonlocal t_sm2
            while nxt["dma"] < len(plan):
                i = nxt["dma"]
                if i >= NRAW and i - NRAW not in raw_free:
                    return
                w = plan[i][4] * len(plan[i][2])
                src = wts[offs[i]:offs[i] + 128 * w].rearrange("(p n) -> p n", p=128)
                dst = raw[i % NRAW][:, 0:w]
                landed[i] = sp.dma(raw_free.get(i - NRAW, []), raw_sem[i % NRAW], 16 * (i // NRAW + 1),
                                   lambda e, dst=dst, src=src: e.dma_start(dst, src))
                nxt["dma"] += 1
                if i == 0:
                    load_x(1)
                if i == 2:
                    t_sm2 = load("d_sm2", sm[:, NEARLY:NSMALL], small[:, NEARLY:NSMALL])

        share = [0.7]

        def run_splits(upto):
            while nxt["split"] <= min(upto, len(plan) - 1):
                run_dmas()
                i = nxt["split"]
                nxt["split"] += 1
                if not plan[i][5]:
                    continue
                w = plan[i][4] * len(plan[i][2])
                r, h, l = raw[i % NRAW][:, 0:w], whi[i % NHL][:, 0:w], wlo[i % NHL][:, 0:w]
                free = hl_free.get(i - NHL, [])
                t1 = act.do([landed[i], *free], lambda e: e.activation(h, r, ACT.Copy), link=False)
                c = int(w * share[0]) // 32 * 32
                split[i] = [t1]
                for q, a, b in ((dve, 0, c), (pool, c, w)):
                    if a < b:
                        split[i].append(q.do([landed[i], t1, *free], lambda e: e.tensor_tensor(
                            l[:, a:b], r[:, a:b], h[:, a:b].bitcast(F32), ALU.subtract), link=False))
                raw_free[i] = split[i]
                run_dmas()

        def take(ahead=AHEAD):
            i = nxt["use"]
            nxt["use"] += 1
            run_splits(i + ahead)
            kk, ncol = plan[i][4], len(plan[i][2])
            v = [t[:, 0:kk * ncol].rearrange("p (k n) -> p k n", k=kk)
                 for t in (raw[i % NRAW], whi[i % NHL], wlo[i % NHL])]
            return i, v

        def taken(i, token):
            hl_free[i] = [token]
            if not plan[i][5]:
                raw_free[i] = [token]
                run_dmas()

        bank_free = {}
        turn = [0]

        def bank():
            b = turn[0] % 4
            turn[0] += 1
            return b

        def mm3(out, sh, sl, mh, ml, start, stop, after=()):
            pe.quiet(after, lambda e: e.matmul(out, sh, mh, start=start, stop=False, skip_group_check=True))
            pe.quiet([], lambda e: e.matmul(out, sh, ml, start=False, stop=False, skip_group_check=True))
            make = lambda e: e.matmul(out, sl, mh, start=False, stop=stop, skip_group_check=True)
            if stop:
                return pe.do([], make)
            pe.quiet([], make)

        def by_k(ready, k, tts=(0, 1)):
            if isinstance(ready, dict):
                return [t for tt in tts for t in ready[tt, k // 4]]
            return ready[min(k // 4, len(ready) - 1)] if ready and isinstance(ready[0], list) else ready

        def rows_held(hi, lo, ready, evac, hooks, tail=False):
            b = [bank(), bank()]
            ch = [take(1), take(0)]
            late = max(hooks) if hooks and not tail else 0
            n = 0
            for tt in range(2):
                for c, (i, (_, wh, wl)) in enumerate(ch):
                    kk, ncol = plan[i][4], len(plan[i][2])
                    o = PB[b[tt]][:, 0:ncol]
                    sl = slice(tt * 128, tt * 128 + 128)
                    for k in range(kk):
                        kg = c * kk + k
                        if n in hooks:
                            hooks[n]()
                        if n == late:
                            run_splits(ch[0][0] + AHEAD)
                        after = [*split[i], *by_k(ready, kg, (tt,)), *(bank_free.get(b[tt], []) if kg == 0 else [])]
                        t = mm3(o, hi[:, kg, sl], lo[:, kg, sl], wh[:, k, :], wl[:, k, :], kg == 0, kg == 7, after)
                        if tt and k == kk - 1:
                            taken(i, t or pe.mark())
                            if c == 0 and not tail:
                                run_splits(ch[1][0] + AHEAD)
                        if kg == 7:
                            bank_free[b[tt]] = evac(tt, o, t)
                        n += 1
                        if n % 2 == 0:
                            yield

        def rows_out(hi, lo, ready, evac):
            b = [bank(), bank()]
            for c in range(2):
                i, (_, wh, wl) = take()
                kk, ncol = plan[i][4], len(plan[i][2])
                order = [(k, tt) for k in range(kk) for tt in range(2)]
                if c:
                    order = [(k, tt) for tt in range(2) for k in range(kk)]
                for n, (k, tt) in enumerate(order):
                    kg = c * kk + k
                    o = PB[b[tt]][:, 0:ncol]
                    sl = slice(tt * 128, tt * 128 + 128)
                    after = [*split[i], *by_k(ready, kg, (tt,))]
                    if kg == 0:
                        after += bank_free.get(b[tt], [])
                    t = mm3(o, hi[:, kg, sl], lo[:, kg, sl], wh[:, k, :], wl[:, k, :], kg == 0, kg == 7, after)
                    if n == 2 * kk - 1:
                        taken(i, t or pe.mark())
                    if kg == 7:
                        bank_free[b[tt]] = evac(tt, o, t)
                    if n % 2:
                        yield

        def feats_out(hi, lo, nk, ready, evac):
            i, (_, wh, wl) = take()
            npair = len(plan[i][2]) // 256
            for p in range(npair):
                b = bank()
                toks = None
                for k in range(nk):
                    for f in range(2):
                        o = PB[b][:, f * S:f * S + S]
                        c = p * 256 + f * 128
                        first = k == 0 and f == 0
                        after = [*split[i], *by_k(ready, k)]
                        if first:
                            after += bank_free.get(b, [])
                        wsh, wsl = wh[:, k, c:c + 128], wl[:, k, c:c + 128]
                        pe.quiet(after, lambda e, o=o, a=wsh, m=hi[:, k, :], s=first: e.matmul(
                            o, a, m, start=s, stop=False, skip_group_check=True))
                        pe.quiet([], lambda e, o=o, a=wsh, m=lo[:, k, :]: e.matmul(
                            o, a, m, start=False, stop=False, skip_group_check=True))
                        pe.quiet([], lambda e, o=o, a=wsl, m=hi[:, k, :], s=(k == nk - 1): e.matmul(
                            o, a, m, start=False, stop=s, skip_group_check=True))
                    if k == nk - 1:
                        toks = pe.mark()
                        if p == npair - 1:
                            taken(i, toks)
                        bank_free[b] = evac(p, PB[b][:, :].rearrange("p (f s) -> p f s", f=2), toks)
                    yield

        def run(g):
            for _ in g:
                pass

        def chain(*gs):
            for g in gs:
                yield from g

        def weave(front, back, n):
            for m in front:
                for _ in range(n if m is None else m):
                    next(back, None)
            run(back)

        def halves(dst_hi, dst_lo, src, after):
            a = act.do(after, lambda e: e.activation(dst_hi, src, ACT.Copy), link=False)
            b = dve.do([a, *after], lambda e: e.tensor_tensor(dst_lo, src, dst_hi.bitcast(F32), ALU.subtract),
                       link=False)
            return [a, b]

        def mul(q, after, o, a, b):
            return q.do(after, lambda e: e.tensor_tensor(o, a, b, ALU.mult))

        def add(q, after, o, a, b):
            return q.do(after, lambda e: e.tensor_tensor(o, a, b, ALU.add))

        def scal(q, after, o, a, s1, s2, op0, op1):
            return q.do(after, lambda e: e.tensor_scalar(o, a, s1, s2, op0, op1))

        def power(after, o, a):
            n = a.shape[-1]
            return pool.do([t_sm, *after], lambda e: e.tensor_tensor(o, a, smv("mhalf")[:, 0:n], ALU.pow))

        def copy(q, after, o, a, link=False):
            if q is act:
                return act.do(after, lambda e: e.activation(o, a, ACT.Copy), link=link)
            return q.do(after, lambda e: e.tensor_copy(o, a), link=link)

        def transposed(after, o, i, n=128):
            idt = ident[0:n, 0:n]
            return pe.do([t_sm, *after], lambda e: e.transpose(o, i, idt))

        def mm(after, o, a, b, start=True, stop=True):
            return pe.do(after, lambda e: e.matmul(o, a, b, start=start, stop=stop, skip_group_check=True))

        def bc(ap, shape, ax):
            return ap.unsqueeze(ax).to_broadcast(shape)

        t_c = [copy(dve, [t_sm], idb[:, :], ident)]
        t_m0 = pool.do([], lambda e: e.memset(mkb[:, :], 0.0))
        t_mk = pool.do([t_m0], lambda e: e.affine_select(
            out=mkb[:, :], in_=mkb[:, :], compare_op=ALU.is_ge, fill=NEG, base=0,
            pattern=[[-1, 128]], channel_multiplier=1))

        xn = [at(f"xn{t}", P + 74 + 4 * t, [128, D]) for t in range(2)]
        safe = [[]]

        def square_norm(tt, ready, busy, o, g, t_g):
            sq2 = st[:, 2 * tt:2 * tt + 2]
            ms = st[:, 4 + tt:5 + tt]
            rs = st[:, 6 + tt:7 + tt]
            a = []
            for half in range(2):
                hs = slice(half * 512, half * 512 + 512)
                a.append(act.do([*ready[half], *busy], lambda e: e.activation(
                    xn[tt][:, hs], x[:, tt, hs], ACT.Square, scale=1.0 / 32, accum_out=sq2[:, half:half + 1]),
                    link=False))
            b = dve.do([*a, *busy], lambda e: e.tensor_scalar(
                ms, sq2[:, 0:1], sq2[:, 1:2], EPS, ALU.add, ALU.add), link=False)
            c = power([b], rs, ms)
            res = []
            for half in range(2):
                hs = slice(half * 512, half * 512 + 512)
                res.append([dve.do([c, t_g], lambda e: e.scalar_tensor_tensor(
                    o[:, hs], x[:, tt, hs], rs, g[:, hs], ALU.mult, ALU.mult), link=False)])
            return res

        class Norm:

            def __init__(self, gi, first=None):
                self.gi, self.first, self.busy, self.t_gain = gi, first, safe[0], t_gain
                self.rows, self.done = {}, {}

            def scaled(self, tt):
                ready = x_done[tt]
                if self.first:
                    ready = square_norm(tt, ready, self.busy, x[:, tt, :], *self.first)
                self.rows[tt] = square_norm(tt, ready, self.busy, xn[tt], gain, self.t_gain)
                if tt == 1:
                    self.load_next()

            def load_next(self):
                nonlocal t_gain
                n = {0: 1, 1: 3}.get(self.gi, self.gi + 1)
                t_gain = load_gain(n, sum([*self.rows[0], *self.rows[1]], [])) if n < 7 else None

            def turned(self, tt):
                for half in range(2):
                    b = bank()
                    for j in range(4):
                        k = half * 4 + j
                        t = transposed([*self.rows[tt][half], *(bank_free.get(b, []) if j == 0 else [])],
                                       PB[b][:, j * 128:j * 128 + 128], xn[tt][:, k * 128:k * 128 + 128])
                    dst = slice(half * 4, half * 4 + 4), slice(tt * 128, tt * 128 + 128)
                    self.done[tt, half] = halves(hhi[:, dst[0], dst[1]], hlo[:, dst[0], dst[1]],
                                                 PB[b][:, :].rearrange("p (k s) -> p k s", k=4), [t, *self.busy])
                    bank_free[b] = self.done[tt, half]

        def tail_hooks(nm):
            return {8: lambda: nm.scaled(0), 13: lambda: nm.turned(0)}

        def add_to_x(col):
            def evac(tt, ps, t):
                xs = x[:, tt, col:col + 512]
                d = dve.do([t], lambda e: e.tensor_tensor(xs, ps, xs, ALU.add), link=False)
                x_done[tt][col // 512].append(d)
                return [d]
            return evac

        def to_halves_T(src, nblk, dhi, dlo, after):
            res = []
            for tt in range(2):
                for g in range(nblk // 4):
                    b = bank()
                    for j in range(4):
                        k = g * 4 + j
                        t = transposed([*after[tt], *(bank_free.get(b, []) if j == 0 else [])],
                                       PB[b][:, j * 128:j * 128 + 128], src[tt][:, k * 128:k * 128 + 128])
                    h = halves(dhi[:, g * 4:g * 4 + 4, tt * 128:tt * 128 + 128],
                               dlo[:, g * 4:g * 4 + 4, tt * 128:tt * 128 + 128],
                               PB[b][:, :].rearrange("p (k s) -> p k s", k=4), [t])
                    bank_free[b] = h
                    res += h
            return res

        oah = at("oah", P, [128, 4, S], R32)
        oal = at("oal", P + 4, [128, 4, S], R32)
        N0 = P + 8
        qkv = [at(f"qkv{t}", N0 + 5.25 * t, [128, 1304]) for t in range(2)]
        qT = at("qT", N0 + 10.5, [128, 4, S])
        kT = at("kT", N0 + 14.5, [128, 2, S])
        Ex = [at(f"Ex{i}", (N0 + 16.5, N0 + 18.5, N0 + 80)[i], [128, 2, S]) for i in range(3)]
        ET = [at(f"ET{i}", N0 + 20.5 + 2 * i, [128, 4, 128]) for i in range(2)]
        oa = [at(f"oa{t}", N0 + 24.5 + 2 * t, [128, 512]) for t in range(2)]
        Tm = at("Tm", N0 + 28.5, [128, 512])
        Sw = at("Sw", N0 + 30.5, [128, 2, 16, 32])
        Swh = at("Swh", N0 + 16.5, [128, 36, 32], R32)
        Swl = at("Swl", N0 + 21, [128, 36, 32], R32)
        Hs = at("Hs", N0 + 28.5, [32, 512])
        Hg = at("Hg", N0 + 35, [128, 2, 2, 32])
        Hr = at("Hr", N0 + 35.5, [128, 2, 120])
        kcT = at("kcT", N0 + 36.5, [128, 16])
        VC = at("VC", N0 + 36.75, [128, 8, 64])
        cs_ = at("cs_", N0 + 38.75, [128, 8, 15])
        cp = at("cp", N0 + 39.25, [128, 120])
        cpT = at("cpT", N0 + 39.75, [128, 128])
        rt = at("rt", N0 + 40.25, [128, 16])
        R0 = N0 + 41
        qrT = at("qrT", R0, [128, 4, S])
        krT = at("krT", R0 + 4, [128, 4, S])
        vr = [at(f"vr{t}", R0 + 8 + 4 * t, [128, D]) for t in range(2)]
        sg = at("sg", R0 + 16, [128, 2, D])
        ra = [at(f"ra{i}", R0 + (8, 10, 16, 18)[i], [128, 512]) for i in range(4)]
        rb = [at(f"rb{i}", R0 + 24 + 2 * i, [128, 512]) for i in range(2)]
        gnw = at("gnw", N0 + 16, [128, D])
        gm_e = at("gm_e", R0 + 24, [128, 4, S])
        dec = at("dec", R0 + 28, [128, 4, 384])
        STt = [at(f"STt{i}", R0 + 34 + 1.5 * i, [128, 384]) for i in range(2)]
        ctab = at("ctab", R0 + 37, [128, 2, 256])
        gm = at("gm", N0, [128, 16, S])
        orh = at("orh", N0 + 16, [128, 8, S], R32)
        orl = at("orl", N0 + 24, [128, 8, S], R32)
        orr = [at(f"orr{t}", N0 + 32 + 4 * t, [128, D]) for t in range(2)]
        mh = at("mh", R0, [128, 8, S], R32)
        ml = at("ml", R0 + 8, [128, 8, S], R32)
        mg = at("mg", R0 + 16, [128, 8, S])

        run_dmas()
        x_done = [[[t_x[0]]] * 2, [[t_x[1]]] * 2]
        nm0 = Norm(0)
        nm0.scaled(0)
        run_splits(0)
        nm0.turned(0)
        nm0.scaled(1)
        t_h = nm0.done

        gt = st[:, 64:112].rearrange("p (t n) -> p t n", t=2)
        ropen = smv("ropen").rearrange("p (t a n) -> p t a n", t=2, a=2)

        def rope_small(q, v, shape, tt, table, half, tmp1, tmp2, after):
            full = [*shape[:-1], 2 * half]
            cosb, sinb = table[:, tt, 0, :], table[:, tt, 1, :]
            for ax in range(len(shape) - 2):
                cosb, sinb = cosb.unsqueeze(1), sinb.unsqueeze(1)
            lo_ = tuple([slice(None)] * (len(shape) - 1) + [slice(0, half)])
            hi_ = tuple([slice(None)] * (len(shape) - 1) + [slice(half, 2 * half)])
            hs = [*shape[:-1], half]
            a = mul(q, after, tmp1, v, cosb.to_broadcast(full))
            b = mul(q, after, tmp2[lo_], v[hi_], sinb[lo_].to_broadcast(hs))
            c = mul(q, after, tmp2[hi_], v[lo_], sinb[hi_].to_broadcast(hs))
            return add(q, [a, b, c], v, tmp1, tmp2)

        def r4(ap, a, b):
            return ap.rearrange("p (a b c) -> p a b c", a=a, b=b)

        tq, tk1, tk2 = {}, {}, {}

        def evac_q(tt, ps, t):
            a = act.do([t], lambda e: e.activation(qkv[tt][:, 0:512], ps, ACT.Copy, scale=0.125))
            v = qkv[tt][:, 0:512].rearrange("p (h d) -> p h d", h=8)[:, :, 0:16]
            t1, t2 = (st[:, o:o + 128].rearrange("p (h d) -> p h d", h=8) for o in (128, 256))
            tq[tt] = rope_small(dve, v, [128, 8, 16], tt, ropen, 8, t1, t2, [a])
            return [a]

        def evac_kv1(tt, ps, t):
            tk1[tt] = copy(act, [t], qkv[tt][:, 512:1024], ps)
            return [tk1[tt]]

        def evac_kv2(tt, ps, t):
            a = copy(act, [t], qkv[tt][:, 1024:1304], ps)
            v = qkv[tt][:, 768:1280].rearrange("p (a g d) -> p a g d", a=2, g=4)[:, :, 0:2, 0:16]
            t1, t2 = (st[:, o:o + 64].rearrange("p (a g d) -> p a g d", a=2, g=2) for o in (128, 256))
            tk2[tt] = rope_small(dve, v, [128, 2, 2, 16], tt, ropen, 8, t1, t2, [a, tk1[tt], tq[tt]])
            b = copy(dve, [a], gt[:, tt, :], qkv[tt][:, 1280:1304])
            tg.append(b)
            return [a]

        tg = []
        busy0 = everything()
        run(rows_held(hhi, hlo, t_h, evac_q, {5: lambda: nm0.turned(1)}))
        t_h = sum(t_h.values(), [])
        t_dec = load("d_dec", dec[:, :, :], tabs["dec"], t_h)
        t_ctab = load("d_ctab", ctab[:, :, :], tabs["ctab"], t_h)

        tqr, tkr, tv, tsg = [], [], [], []
        rbf, turns = {}, []

        def evac_rot(w, dstT, toks):
            def evac(tt, ps, t):
                b4 = lambda ap: ap.rearrange("p (h d) -> p h d", h=4)
                a_, b_ = ra[2 * w + tt], rb[tt]
                free = rbf.get(tt, t_h)
                cosb = bc(ctab[:, tt, 0:128], [128, 4, 128], 1)
                a = mul(dve, [t, t_ctab, *t_h], b4(a_[:, :]), b4(ps), cosb)
                b = mul(dve, [t, *free], b4(b_[:, :])[:, :, 0:64], b4(ps)[:, :, 64:128],
                        bc(ctab[:, tt, 128:192], [128, 4, 64], 1))
                c = mul(dve, [t, *free], b4(b_[:, :])[:, :, 64:128], b4(ps)[:, :, 0:64],
                        bc(ctab[:, tt, 192:256], [128, 4, 64], 1))
                d = add(pool, [a, b, c], a_[:, :], a_[:, :], b_[:, :])
                rbf[tt] = [d]

                def turn():
                    bk = bank()
                    for j in range(4):
                        t2 = transposed([d, *bank_free.get(bk, [])], PB[bk][:, j * 128:j * 128 + 128],
                                        a_[:, j * 128:j * 128 + 128])
                    f = copy(act, [t2], dstT[:, :, tt * 128:tt * 128 + 128],
                             PB[bk][:, :].rearrange("p (k s) -> p k s", k=4))
                    bank_free[bk] = [f]
                    toks.append(f)

                turns.append(turn)
                return [a, b, c]
            return evac

        run(rows_out(hhi, hlo, [], evac_kv1))
        kgen = rows_out(hhi, hlo, [], evac_kv2)
        for _ in range(4):
            next(kgen)
        X2 = TP[:, :].rearrange("p (v g s) -> p v g s", v=2, g=2)
        for kv in range(2):
            for g in range(2):
                for tt in range(2):
                    for par in range(2):
                        o = X2[par * 64:par * 64 + 64, kv, g, tt * 64:tt * 64 + 64]
                        src = qkv[tt][:, 512 + kv * 128 + g * 64:512 + kv * 128 + g * 64 + 64]
                        sel = ident.rearrange("p (s e) -> p e s", e=2)[:, par, :]
                        t = mm([tk1[tt]], o, src, sel)
        z0 = dve.do(busy0, lambda e: e.memset(Sw[:, :, :, 30:32], 0.0), link=False)
        z1 = act.do([t_sm, *busy0], lambda e: e.activation(Swh[:, 32:36, :], ident.rearrange(
            "p (a b) -> p a b", b=32), ACT.Copy), link=False)
        for kv in range(2):
            for half in range(2):
                o = Sw[:, kv, half * 8:half * 8 + 8, 0:30].rearrange("p j (g c) -> p j g c", g=2)
                i = X2[:, kv, :, half * 8:half * 8 + 120].rearrange("p g (c j) -> p j g c", j=8)
                pev = smv("pe").rearrange("p (v j) -> p v j", v=2)[:, kv, half * 8:half * 8 + 8]
                t2 = dve.do([t, t_sm2, *busy0], lambda e: e.tensor_tensor(
                    o, i, pev.unsqueeze(2).unsqueeze(3).to_broadcast([128, 8, 2, 15]), ALU.add), link=False)
        tX = t2
        tS = halves(Swh[:, 0:32, :], Swl[:, 0:32, :], Sw[:, :, :, :].rearrange("p v j c -> p (v j) c"),
                    [t2, z0, *busy0])
        z2 = act.do([z1], lambda e: e.activation(Swl[:, 32:36, :], ident.rearrange(
            "p (a b) -> p a b", b=32), ACT.Copy), link=False)

        run(kgen)
        tg = [act.do(tg, lambda e: e.activation(st[:, 64:112], st[:, 64:112], ACT.Sigmoid))]
        kgen = rows_out(hhi, hlo, [], evac_rot(0, qrT, tqr))
        for _ in range(5):
            next(kgen)
        tqT = []
        for tt in range(2):
            b = bank()
            for j in range(4):
                t = transposed([tq[tt], *bank_free.get(b, [])], PB[b][:, j * 128:j * 128 + 128],
                               qkv[tt][:, j * 128:j * 128 + 128])
            c = copy(act, [t], qT[:, :, tt * 128:tt * 128 + 128], PB[b][:, :].rearrange("p (k s) -> p k s", k=4))
            bank_free[b] = [c]
            tqT.append(c)
        run(kgen)

        HB = [SC[0], SC[1]]
        for kv in range(2):
            for c in range(2):
                i, (_, wh, wl) = take()
                for j in range(8):
                    jj = kv * 16 + c * 8 + j
                    col = slice(jj * 32, jj * 32 + 128)
                    sh = Swh[:, :, :].rearrange("p j c -> p (j c)")[:, col]
                    sl = Swl[:, :, :].rearrange("p j c -> p (j c)")[:, col]
                    t = mm3(HB[kv][:, 0:256], sh, sl, wh[:, j, :], wl[:, j, :], c == 0 and j == 0,
                            c == 1 and j == 7, [*split[i], *tS, z1, z2])
                taken(i, t or pe.mark())
                if kv == 0:
                    turns.pop(0)()
            tG = act.do([t], lambda e: e.activation(Hs[0:30, kv * 256:kv * 256 + 256], HB[kv][0:30, 0:256],
                                                    ACT.Gelu_apprx_tanh), link=False)
        for tt in range(2):
            b = bank()
            for j in range(2):
                o = 768 + 256 * j
                t = transposed([tk2[tt], *bank_free.get(b, [])], PB[b][:, j * 128:j * 128 + 128],
                               qkv[tt][:, o:o + 128])
            c = copy(dve, [t], kT[:, :, tt * 128:tt * 128 + 128],
                     PB[b][:, 0:256].rearrange("p (k s) -> p k s", k=2))
            bank_free[b] = [c]
            tqT.append(c)
        def steps(g, n):
            for _ in range(n):
                next(g, None)

        kgen = rows_out(hhi, hlo, [], evac_rot(1, krT, tkr))
        steps(kgen, 1)
        b = bank()
        for j in range(4):
            t = transposed([tG, *bank_free.get(b, [])], PB[b][:, j * 32:j * 32 + 30],
                           Hs[0:30, j * 128:j * 128 + 128], 30)
        tG = copy(dve, [t], Hg[:, :, :, 0:30],
                  PB[b][:, 0:128].rearrange("p (v h c) -> p v h c", v=2, h=2)[:, :, :, 0:30])
        bank_free[b] = [tG]
        steps(kgen, 1)
        w2 = [smv(n).rearrange("p (h d) -> p h d", h=2) for n in ("w2k", "w2v")]
        for g in range(2):
            for half in range(2):
                t = mm([tG, t_sm2], SC[1][g * 64:g * 64 + 64, 0:15], w2[0][:, half, :],
                       Hg[:, 0, half, g * 15:g * 15 + 15], start=(half == 0), stop=(half == 1))
        tkc = copy(dve, [t], kcT[:, 0:15], SC[1][:, 0:15])
        steps(kgen, 1)
        for half in range(2):
            tr = copy(dve, [tG], Hr[:, half, :].rearrange("p (g r c) -> p g r c", g=2, r=4),
                      bc(Hg[:, 1, half, 0:30].rearrange("p (g c) -> p g c", g=2), [128, 2, 4, 15], 2))
        for half in range(2):
            t = mm([tr, tX], TP[0:120, 0:64], Hr[:, half, :], w2[1][:, half, :],
                   start=(half == 0), stop=(half == 1))
        bm = smv("bm")[0:120, :]
        tvc = dve.do([t], lambda e: e.tensor_tensor(
            VC[0:120, :, :], bc(TP[0:120, 0:64], [120, 8, 64], 1), bc(bm, [120, 8, 64], 2), ALU.mult))
        sc_free, tp_free, ob_free = [[tG], [tkc]], [tvc], []
        run(kgen)

        lsum = st[:, 32:48].rearrange("p (h a) -> p h a", a=2)
        toa = {}

        def nsa():
            nonlocal tp_free, ob_free
            units = [(tt, h) for tt in range(2) for h in range(8)]
            exp_t, tr_t, ev_t, pv_t, ls = {}, {}, {}, {}, {}
            lw = st[:, 384:416].rearrange("p (t h a) -> p t h a", t=2, a=2)
            nm = st[:, 416:448].rearrange("p (t h a) -> p t h a", t=2, a=2)
            wq = st[:, 448:480].rearrange("p (t h a) -> p t h a", t=2, a=2)
            gates = gt.rearrange("p t (h c) -> p t h c", c=3)

            def compressed(tt):
                nonlocal tp_free, ob_free
                for g in range(2):
                    for b in range(4):
                        t = mm([*tqT, tkc, *sc_free[g]], SC[g][:, b * 16:b * 16 + 15],
                               qT[g * 64:g * 64 + 64, b, tt * 128:tt * 128 + 128],
                               kcT[g * 64:g * 64 + 64, 0:15])
                madd = smv("madd").rearrange("p (t c) -> p t c", t=2)[:, tt, 0:15]
                m01 = smv("m01").rearrange("p (t c) -> p t c", t=2)[:, tt, 0:15]
                prev = [pe.last()]
                a = []
                for g in range(2):
                    a.append(dve.do([t, *prev], lambda e, g=g: e.tensor_tensor(
                        cs_[:, g * 4:g * 4 + 4, :], SC[g][:, 0:64].rearrange("p (h c) -> p h c", c=16)[:, :, 0:15],
                        bc(madd, [128, 4, 15], 1), ALU.add)))
                    sc_free[g] = [a[-1]]
                mx, l, r = rt[:, 0:8], st[:, 480:488], st[:, 488:496]
                b_ = dve.do(a, lambda e: e.tensor_reduce(mx, cs_[:, :, :], AXX, ALU.max))
                c_ = dve.do([b_], lambda e: e.tensor_tensor(cs_[:, :, :], cs_[:, :, :], bc(mx, [128, 8, 15], 2),
                                                            ALU.subtract))
                d_ = act.do([c_], lambda e: e.activation(cs_[:, :, :], cs_[:, :, :], ACT.Exp))
                yield
                f_ = dve.do([d_], lambda e: e.tensor_reduce(l, cs_[:, :, :], AXX, ALU.add))
                g_ = dve.do([f_], lambda e: e.reciprocal(r, l))
                h_ = mul(dve, [g_, *tg], r, r, gates[:, tt, :, 0])
                p3 = cp[:, :].rearrange("p (h c) -> p h c", h=8)
                i_ = mul(dve, [d_, *prev], p3, cs_[:, :, :], bc(m01, [128, 8, 15], 1))
                t = transposed([i_, *tp_free], TP[0:120, 0:128], cp[:, :])
                yield
                j_ = copy(act, [t], cpT[0:120, :], TP[0:120, 0:128])
                tp_free = [j_]
                t = mm([j_, tvc, *ob_free], OB[:, :], cpT[0:120, :], VC[0:120, :, :])
                yield
                toa[tt] = dve.do([t, h_], lambda e: e.tensor_tensor(
                    oa[tt][:, :].rearrange("p (h d) -> p h d", h=8), OB[:, :].rearrange("p (h d) -> p h d", h=8),
                    bc(r, [128, 8, 64], 2), ALU.mult))
                ob_free = [toa[tt]]

            def scores(u):
                tt, h = units[u]
                g, b = h // 4, h % 4
                n = 128 * (tt + 1)
                bk = SC[u % 2]
                for a in range(2):
                    mm([*tqT, *sc_free[u % 2]], bk[:, a * S:a * S + n],
                       qT[g * 64:g * 64 + 64, b, tt * 128:tt * 128 + 128], kT[g * 64:g * 64 + 64, a, 0:n],
                       start=(a == 0), stop=False)
                for a in range(2):
                    t = mm([t_c[0], t_mk], bk[:, a * S + n - 128:a * S + n], idb[:, :], mkb[:, :],
                           start=False, stop=True)
                s = bk[:, :].rearrange("p (a k) -> p a k", a=2)
                m = dve.do([t], lambda e: e.tensor_reduce(nm[:, tt, h, :], s[:, :, 0:n], AXX, ALU.max, negate=True),
                           link=False)
                for a in range(2):
                    x_ = act.do([m, *tr_t.get(u - 3, [])], lambda e, a=a: e.activation(
                        Ex[u % 3][:, a, 0:n], s[:, a, 0:n], ACT.Exp, bias=nm[:, tt, h, a:a + 1],
                        accum_out=lw[:, tt, h, a:a + 1]), link=False)
                exp_t[u] = [x_]
                sc_free[u % 2] = [x_]

            def turned(u):
                nonlocal tp_free
                tt, h = units[u]
                nk = tt + 1
                for a in range(2):
                    for k in range(nk):
                        t = transposed([*exp_t[u], *tp_free], TP[:, (a * nk + k) * 128:(a * nk + k) * 128 + 128],
                                       Ex[u % 3][:, a, k * 128:k * 128 + 128])
                tr_t[u] = [t]
                ev_t[u] = copy(act if u % 2 else dve, [t, *pv_t.get(u - 2, [])], ET[u % 2][:, 0:2 * nk, :],
                               TP[:, 0:2 * nk * 128].rearrange("p (k s) -> p k s", k=2 * nk))
                tp_free = [ev_t[u]]

            def values(u):
                nonlocal ob_free
                tt, h = units[u]
                g, nk = h // 4, tt + 1
                for a in range(2):
                    for k in range(nk):
                        t = mm([ev_t[u], *ob_free], OB[:, ((h % 4) * 2 + a) * 64:((h % 4) * 2 + a) * 64 + 64],
                               ET[u % 2][:, a * nk + k, :],
                               qkv[k][:, 896 + 256 * a + 64 * g:896 + 256 * a + 64 * g + 64],
                               start=(k == 0), stop=(k == nk - 1))
                pv_t[u] = [t]
                if h % 4 == 3:
                    hs = slice(h - 3, h + 1)
                    r_ = dve.do(exp_t[u], lambda e: e.reciprocal(wq[:, tt, hs, :], lw[:, tt, hs, :]))
                    w_ = mul(dve, [r_, *tg], wq[:, tt, hs, :], wq[:, tt, hs, :], gates[:, tt, hs, 1:3])
                    o8 = lambda ap: ap.rearrange("p (h d) -> p h d", d=64)
                    m_ = dve.do([w_, t], lambda e: e.tensor_tensor(
                        o8(Tm[:, :]), o8(OB[:, :]),
                        bc(wq[:, tt, hs, :].rearrange("p h a -> p (h a)"), [128, 8, 64], 2), ALU.mult))
                    ob_free = [m_]
                    dst = oa[tt][:, (h - 3) * 64:(h + 1) * 64].rearrange("p (h d) -> p h d", d=64)
                    T4 = Tm[:, :].rearrange("p (h a d) -> p h a d", h=4, a=2)
                    a_ = add(dve, [m_, toa[tt]], dst, dst, T4[:, :, 0, :])
                    toa[tt] = add(dve, [a_], dst, dst, T4[:, :, 1, :])

            yield
            for tt in range(2):
                yield from compressed(tt)
                lo_, hi_ = 8 * tt, 8 * tt + 8
                for s_ in range(lo_, hi_ + 3):
                    if lo_ <= s_ - 2 < hi_:
                        turned(s_ - 2)
                    if lo_ <= s_ - 3:
                        values(s_ - 3)
                    if s_ < hi_:
                        scores(s_)
                    yield 2

        def evac_to(dst, toks, q=None, free=()):
            def evac(tt, ps, t):
                toks.append(copy(q or (act if tt else dve), [t, *free], dst(tt), ps))
                return [toks[-1]]
            return evac

        tgm = []

        def gmv(j):
            return gm_e[:, j:j + 2, :] if j < 4 else gm[:, j:j + 2, :]

        def evac_gm(f, free):
            def evac(p, ps, t):
                tgm.append(copy(act, [t, *free], gmv(2 * f), ps))
                return [tgm[-1]]
            return evac

        rb_read = sum(rbf.values(), [])
        back = chain(
            rows_out(hhi, hlo, [], evac_to(lambda tt: vr[tt][:, 0:512], tv, None, tqr)),
            rows_out(hhi, hlo, [], evac_to(lambda tt: vr[tt][:, 512:1024], tv, None, tqr)),
            rows_out(hhi, hlo, [], evac_to(lambda tt: sg[:, tt, 0:512], tsg, None, tkr)),
            rows_out(hhi, hlo, [], evac_to(lambda tt: sg[:, tt, 512:1024], tsg, None, tkr)),
            *[feats_out(hhi, hlo, 8, [], evac_gm(f, rb_read)) for f in range(2)],
        )
        def front():
            for n, m in enumerate(nsa()):
                yield m
                if n in (3, 5):
                    turns.pop(0)()

        weave(front(), back, 2)
        toaT = to_halves_T(oa, 4, oah, oal, [[toa[0]], [toa[1]]])

        nsa_done = everything()
        t_gnw = load("d_gnw", gnw[:, :], rows[7:8, :].to_broadcast([128, D]), nsa_done)
        tor = [[], []]

        def ret():
            s_t, o_t = {}, {}
            mv = st[:, 128:144].rearrange("p (h t c) -> p h t c", h=4, t=2)
            bn = st[:, 144:192].rearrange("p (h t c) -> p h t c", h=4, t=2)
            sf, of = [[*nsa_done], [*nsa_done]], [[*nsa_done], [*nsa_done]]
            stf = {}
            a0 = act.do([*tsg], lambda e: e.activation(sg[:, :, :], sg[:, :, :], ACT.Silu))
            tsil = [mul(pool, [a0, t_gnw], sg[:, tt, :], sg[:, tt, :], gnw[:, :]) for tt in range(2)]
            for h in range(6):
                if 0 <= h - 1 < 4:
                    k = h - 1
                    b = (TP, OB)[k % 2]
                    vs = slice(k * 256, k * 256 + 256)
                    mm([s_t[k], *tv, *of[k % 2]], b[:, 0:256], STt[k % 2][:, 0:128], vr[0][:, vs])
                    mm([], b[:, 256:512], STt[k % 2][:, 128:256], vr[0][:, vs], start=True, stop=False)
                    t = mm([], b[:, 256:512], STt[k % 2][:, 256:384], vr[1][:, vs], start=False, stop=True)
                    stf[k] = [t]
                    for tt in range(2):
                        c = dve.do([t], lambda e, tt=tt: e.bn_stats(bn[:, k, tt, :], b[:, tt * 256:tt * 256 + 256]))
                        c = dve.do([c], lambda e, tt=tt: e.bn_aggr(mv[:, k, tt, :], bn[:, k, tt, :]))
                    rk = st[:, 192 + 2 * k:194 + 2 * k]
                    c = scal(dve, [c], rk, mv[:, k, :, 1], 1.0, EPS, ALU.mult, ALU.add)
                    o_t[k] = power([c], st[:, 200 + 2 * k:202 + 2 * k], rk)
                if h < 4:
                    b = SC[h % 2]
                    mm([*tqr, *tkr, *sf[h % 2]], b[:, 0:256], krT[:, h, 0:128], qrT[:, h, :])
                    t = mm([], b[:, 256:384], krT[:, h, 128:256], qrT[:, h, 128:256])
                    s_t[h] = mul(dve, [t, t_dec, *stf.get(h - 2, [])], STt[h % 2][:, :], b[:, 0:384], dec[:, h, :])
                    sf[h % 2] = [s_t[h]]
                yield
                if 0 <= h - 1 < 4:
                    k = h - 1
                    b = (TP, OB)[k % 2]
                    for tt in range(2):
                        d = scal(dve, [o_t[k], *nsa_done], orr[tt][:, k * 256:k * 256 + 256],
                                 b[:, tt * 256:tt * 256 + 256], mv[:, k, tt, 0:1],
                                 st[:, 200 + 2 * k + tt:201 + 2 * k + tt], ALU.subtract, ALU.mult)
                        tor[tt].append(d)
                    of[k % 2] = [d]
                yield
            for tt in range(2):
                tor[tt] = [mul(dve, [*tor[tt], tsil[tt]], orr[tt][:, :], orr[tt][:, :], sg[:, tt, :])]
                yield

        weave(ret(), chain(*[feats_out(hhi, hlo, 8, [], evac_gm(f, nsa_done)) for f in range(2, 8)]), 3)
        torT = to_halves_T(orr, 8, orh, orl, tor)
        tgs = [act.do(tgm, lambda e, g=g: e.activation(g, g, ACT.Sigmoid))
               for g in (gm_e[:, :, :], gm[:, 4:8, :], gm[:, 8:16, :])]
        ret_done = everything()
        tmg, tm = {}, [[], []]

        def evac_ya(f):
            def evac(p, ps, t):
                j = 4 * f + 2 * p
                tmg[j] = mul(dve, [t, *tgs, *ret_done], mg[:, j:j + 2, :], ps, gmv(j))
                return [tmg[j]]
            return evac

        def evac_yb(f):
            def evac(p, ps, t):
                j = 2 * f
                a = mul(dve, [t, *tgs], gm[:, 8 + j:10 + j, :], ps, gm[:, 8 + j:10 + j, :])
                b = add(pool, [a, tmg[j]], mg[:, j:j + 2, :], mg[:, j:j + 2, :], gm[:, 8 + j:10 + j, :])
                tm[j // 4].extend(halves(mh[:, j:j + 2, :], ml[:, j:j + 2, :], mg[:, j:j + 2, :], [b, *ret_done]))
                return [a]
            return evac

        share[0] = 0.5
        run(chain(*[feats_out(oah, oal, 4, toaT, evac_ya(f)) for f in range(2)]))
        run(chain(*[feats_out(orh, orl, 8, torT, evac_yb(f)) for f in range(4)]))
        safe[0] = everything()
        x_done = [[[], []], [[], []]]
        nm1 = Norm(1)
        run(rows_out(mh, ml, tm, add_to_x(0)))
        run(rows_held(mh, ml, tm, add_to_x(512), tail_hooks(nm1), True))
        nm1.scaled(1)
        nm1.turned(1)
        share[0] = 0.8

        ghi = at("ghi", P, [128, NFT, S], R32)
        glo = at("glo", P + 22, [128, NFT, S], R32)
        fu = [at(f"fu{i}", P + 56 + 2 * i, [128, 2, S]) for i in range(2)]
        fs = [at(f"fs{i}", P + 60 + i, [128, S]) for i in range(2)]
        fg = [at(f"fg{i}", P + 62 + i, [128, S]) for i in range(2)]

        gain_f = at("gain_f", P + 66, [128, D])

        def ffn(conv, th, make_next, turn_at=None):
            nonlocal x_done
            x_done = [[[], []], [[], []]]
            busy = everything()
            if conv:
                t_gf.append(load("d_gf", gain_f[:, :], rows[2:3, :].to_broadcast([128, D]), busy))
            tgx, used = [], {}
            fc = smv("fconv").rearrange("p (f v c) -> p f v c", f=NFT, v=2)

            later = []

            def split_g(f, d):
                def go():
                    used[f] = halves(ghi[:, f, :], glo[:, f, :], fg[f % 2][:, :], [d, *busy])
                    tgx.append(used[f])
                return go

            def gate_g(f, b):
                def go():
                    c = act.do([b], lambda e: e.activation(fs[f % 2][:, :], fu[f % 2][:, 0, :], ACT.Silu),
                               link=False)
                    d = pool.do([c, b], lambda e: e.tensor_tensor(
                        fg[f % 2][:, :], fs[f % 2][:, :], fu[f % 2][:, 1, :], ALU.mult), link=False)
                    later.append(split_g(f, d))
                return go

            def evac(f):
                def ev(p, ps, t):
                    while later:
                        go = later.pop(0)
                        n = len(later)
                        go()
                        if len(later) > n:
                            break
                    u, s_, g = fu[f % 2], fs[f % 2], fg[f % 2]
                    free = [*used.get(f - 2, busy)]
                    if conv:
                        for v in range(2):
                            a = act.do([t, *free], lambda e: e.activation(
                                u[:, v, :], ps[:, v, :], ACT.Identity, scale=fc[:, f, v, 2:3], bias=fc[:, f, v, 3:4]),
                                link=False)
                        b = [a, a]
                        for j in (1, 2):
                            for v in range(2):
                                b[v] = dve.do([b[v]], lambda e: e.scalar_tensor_tensor(
                                    u[:, v, j:S], ps[:, v, 0:S - j], fc[:, f, v, 2 - j:3 - j], u[:, v, j:S],
                                    ALU.mult, ALU.add), link=False)
                        later.append(gate_g(f, b[1]))
                        return [b[1]]
                    c = act.do([t, *free], lambda e: e.activation(s_[:, :], ps[:, 0, :], ACT.Silu), link=False)
                    d = dve.do([c, *free], lambda e: e.tensor_tensor(g[:, :], ps[:, 1, :], s_[:, :], ALU.mult),
                               link=False)
                    later.append(split_g(f, d))
                    return [d]
                return ev

            run(chain(*[feats_out(hhi, hlo, 8, th, evac(f)) for f in range(NFT)]))
            while later:
                later.pop(0)()
            b0 = [bank() for _ in range(4)]
            safe[0] = everything()
            nm = make_next() if make_next else None

            def down(c, i, wh, wl, k, tt, half):
                kg = 2 * c + k
                b = b0[tt * 2 + half]
                sl = slice(tt * 128, tt * 128 + 128)
                cs = slice(half * 512, half * 512 + 512)
                after = [*split[i], *tgx[kg], *(bank_free.get(b, []) if kg == 0 else [])]
                t = mm3(PB[b][:, :], ghi[:, kg, sl], glo[:, kg, sl], wh[:, k, cs], wl[:, k, cs],
                        kg == 0, kg == NFT - 1, after)
                if t:
                    bank_free[b] = add_to_x(half * 512)(tt, PB[b][:, :], t)
                return t or pe.mark()

            nc_ = NFT // 2
            for c in range(nc_ - 2):
                i, (_, wh, wl) = take()
                for k in range(2):
                    for tt in range(2):
                        for half in range(2):
                            t = down(c, i, wh, wl, k, tt, half)
                taken(i, t)
            held = [take(), take(0)]
            for tt in range(2):
                for half in range(2):
                    for c, (i, (_, wh, wl)) in enumerate(held):
                        for k in range(2):
                            t = down(nc_ - 2 + c, i, wh, wl, k, tt, half)
                            if nm and tt and (half, c, k) == turn_at:
                                nm.turned(0)
                        if tt and half:
                            taken(i, t)
                            if c == 0 and nm:
                                old, share[0] = share[0], 0.5
                                run_splits(held[1][0] + AHEAD)
                                share[0] = old
                if nm:
                    if tt and turn_at is None:
                        nm.turned(0)
                    nm.scaled(tt)
            return nm

        t_gf = []
        nm1 = ffn(True, nm1.done, lambda: Norm(3, (gain_f, t_gf[0])))

        ath, atl, cvh, cvl, frh, frl = (at(n, P + 4 * j, [128, 4, S], R32) for j, n in
                                        enumerate(("ath", "atl", "cvh", "cvl", "frh", "frl")))
        gm2 = at("gm2", P + 24, [128, 24, S])
        Z = P + 48
        q2T = at("q2T", Z, [128, 4, S])
        k2T = at("k2T", Z + 4, [128, 4, S])
        v2 = [at(f"v2{t}", Z + 8 + 2 * t, [128, 512]) for t in range(2)]
        gp = at("gp", Z + 12, [128, 4, 288])
        Y = Z + 16.5
        qn = [at(f"qn{t}", Y + (0, 2, 6, 8)[t], [128, 512]) for t in range(4)]
        sq = at("sq", Y + 4, [128, 512])
        xf = [at(f"xf{t}", Y + 6 + 2 * t, [128, 512]) for t in range(2)]
        T12 = [at(f"T12{t}", Y + 10 + 2 * t, [128, 512]) for t in range(2)]
        csT = at("csT", Y + 14, [128, 2, 512])
        cdT = at("cdT", Y + 18, [128, 2, 128])
        E2 = [at(f"E2{t}", Y + 2 * t, [128, 2, S]) for t in range(2)]
        W2 = [at(f"W2{t}", Y + 4 + t, [128, S]) for t in range(2)]
        WT = [at(f"WT{t}", Y + 6 + 2 * t, [128, 2, S]) for t in range(2)]
        o2 = at("o2", Y + 10, [128, 2, 512])
        csq = at("csq", Y + 14, [128, 4, S])
        cv = at("cv", Y + 20, [128, 4, S])
        mh2 = at("mh2", Z, [128, 8, S], R32)
        ml2 = at("ml2", Z + 8, [128, 8, S], R32)
        mg2 = at("mg2", Z + 16, [128, 8, S])
        osq = at("osq", Y, [128, D])
        rope4 = smv("rope4").rearrange("p (t a n) -> p t a n", t=2, a=2)
        o2q = [o2[:, tt, :] for tt in range(2)]

        def layer(l, nm):
            nonlocal x_done
            li = 0.8 - 0.6 * math.exp(-0.3 * l)
            tv2 = []
            run(rows_held(hhi, hlo, nm.done, evac_to(lambda tt: v2[tt][:, :], tv2, None, safe[0]),
                          {5: lambda: nm.turned(1)}))
            busy = everything()
            tcs = load(f"d_cs{l}", csT[:, :, :], tabs["cs"], busy)
            tcd = load(f"d_cd{l}", cdT[:, :, :], tabs["cd"], busy)
            lam = smv("lam").rearrange("p (l a d) -> p l a d", l=2, a=4)[:, l, :, :]
            lp = st[:, 256:320].rearrange("p (a d) -> p a d", a=2)
            nl = st[:, 8 + 4 * l:12 + 4 * l]
            a = mul(dve, [t_sm2], lp, lam[:, 0:4:2, :], lam[:, 1:4:2, :])
            a = dve.do([a], lambda e: e.tensor_reduce(nl[:, 0:2], lp, AXX, ALU.add))
            a = act.do([a], lambda e: e.activation(nl[:, 0:2], nl[:, 0:2], ACT.Exp))
            tlam = dve.do([a], lambda e: e.scalar_tensor_tensor(
                nl[:, 2:3], nl[:, 1:2], -li, nl[:, 0:1], ALU.add, ALU.subtract))
            neglam = nl[:, 2:3]
            tz = pool.do(busy, lambda e: e.memset(gp[:, :, :], 0.0))

            tT, trq = {0: [], 1: []}, {}
            qfree = [[], [], [], []]

            def evac_qk(w):
                def evac(tt, ps, t):
                    n = 2 * w + tt
                    g16 = lambda ap: ap.rearrange("p (g d) -> p g d", d=32)
                    ss = st[:, 128 + 16 * n:144 + 16 * n]
                    rs = st[:, 192 + 16 * n:208 + 16 * n]
                    gg = smv("qkg").rearrange("p (l w d) -> p l w d", l=2, w=2)[:, l, w, :]
                    q = qn[n]
                    a = act.do([t, *trq.get("sq", tgl)], lambda e: e.activation(sq[:, :], ps, ACT.Square),
                               link=False)
                    f = dve.do([a, t_sm2], lambda e: e.tensor_tensor(
                        g16(q[:, :]), g16(ps), bc(gg, [128, 16, 32], 1), ALU.mult), link=False)
                    b = dve.do([a], lambda e: e.tensor_reduce(ss, g16(sq[:, :]), AXX, ALU.add), link=False)
                    trq["sq"] = [b]
                    k = 1.0 if w == 0 else 1.0 / 32
                    c = scal(dve, [b], ss, ss, k, EPS * 32 * k, ALU.mult, ALU.add)
                    d = power([c], rs, ss)
                    g = mul(pool, [d, f], g16(q[:, :]), g16(q[:, :]), bc(rs, [128, 16, 32], 2))
                    t1, t2 = (st[:, o:o + 128].rearrange("p (g d) -> p g d", d=8) for o in (256, 384))
                    r = rope_small(pool, g16(q[:, :])[:, :, 0:8], [128, 16, 8], tt, rope4, 4, t1, t2, [g, tlam])
                    pend.append((w, tt, q, r, n))
                    return [f, a]
                return evac

            pend = []

            def turn_qk(which):
                for w, tt, q, r, n in pend:
                    if w != which:
                        continue
                    b = bank()
                    for j in range(4):
                        t = transposed([r, *bank_free.get(b, [])], PB[b][:, j * 128:j * 128 + 128],
                                       q[:, j * 128:j * 128 + 128])
                    c = copy(act, [t], (q2T, k2T)[w][:, :, tt * 128:tt * 128 + 128],
                             PB[b][:, :].rearrange("p (k s) -> p k s", k=4))
                    bank_free[b] = [c]
                    qfree[n] = [t]
                    tT[w].append(c)

            tgl, txf = [], []
            tconv = [[], [], [], []]
            cwv = smv("cw").rearrange("p (l f j) -> p l f j", l=2, f=4)[:, l, :, :]
            cvec = smv("cvec").rearrange("p (l a f) -> p l a f", l=2, a=3)[:, l, :, :]
            todo = [(f, j) for j in range(31) for f in range(4)]

            def conv_some(n):
                for _ in range(n):
                    if not todo:
                        return
                    f, j = todo.pop(0)
                    if j == 0:
                        tconv[f] = [dve.do([*tgl, *busy, t_sm2], lambda e: e.tensor_scalar(
                            cv[:, f, :], gp[:, f, 0:S], cwv[:, f, 0:1], cvec[:, 0, f:f + 1], ALU.mult, ALU.add),
                            link=False)]
                    else:
                        tconv[f] = [dve.do(tconv[f], lambda e: e.scalar_tensor_tensor(
                            cv[:, f, :], gp[:, f, j:j + S], cwv[:, f, j:j + 1], cv[:, f, :], ALU.mult, ALU.add),
                            link=False)]

            def evac_glu(f):
                def evac(p, ps, t):
                    a = act.do([t, *busy, *tgl[-1:]], lambda e: e.activation(sq[:, 0:S], ps[:, 1, :], ACT.Sigmoid))
                    b = mul(dve, [a, tz], gp[:, f, 15:15 + S], ps[:, 0, :], sq[:, 0:S])
                    tgl.append(b)
                    return [b]
                return evac

            for f in range(4):
                run(feats_out(hhi, hlo, 8, [], evac_glu(f)))
            share[0] = 0.9
            for _ in rows_out(hhi, hlo, [], evac_qk(1)):
                conv_some(2)
            for _ in rows_out(hhi, hlo, [], evac_qk(0)):
                conv_some(2)
            turn_qk(1)
            share[0] = 0.3
            for _ in rows_out(hhi, hlo, [], evac_to(lambda tt: xf[tt][:, :], txf, None, [*qfree[2], *qfree[3]])):
                conv_some(3)
            turn_qk(0)

            tgm2, tgs2, direct = {}, {}, []
            bgv = smv("bg").rearrange("p (l f) -> p l f", l=2)[:, l, :]

            def evac_g(f):
                def evac(p, ps, t):
                    for v in range(2):
                        a = act.do([t, *busy], lambda e, v=v: e.activation(
                            gm2[:, 2 * f + v, :], ps[:, v, :], ACT.Sigmoid if direct else ACT.Identity,
                            bias=bgv[:, 2 * f + v:2 * f + v + 1]), link=False)
                    (tgs2 if direct else tgm2)[f] = a
                    return [a]
                return evac

            tmg2, tm2 = {}, [[], []]

            def evac_y(n, f):
                def evac(p, ps, t):
                    j = 4 * f + 2 * p
                    g = gm2[:, 8 * n + j:8 * n + j + 2, :]
                    tg_ = tgs2[4 * n + j // 2]
                    if n == 2:
                        tmg2[j] = dve.do([t, tg_, *done2], lambda e: e.tensor_tensor(
                            mg2[:, j:j + 2, :], ps, g, ALU.mult), link=False)
                        return [tmg2[j]]
                    a = dve.do([t, tg_], lambda e: e.tensor_tensor(g, ps, g, ALU.mult), link=False)
                    tmg2[j] = (dve if n == 1 else pool).do([a, tmg2[j]], lambda e: e.tensor_tensor(
                        mg2[:, j:j + 2, :], mg2[:, j:j + 2, :], g, ALU.add), link=False)
                    if n == 1:
                        tm2[j // 4].extend(halves(mh2[:, j:j + 2, :], ml2[:, j:j + 2, :], mg2[:, j:j + 2, :],
                                                  [tmg2[j], *done2]))
                    return [a]
                return evac

            tfr, done2 = [], []
            back = chain(*[feats_out(hhi, hlo, 8, [], evac_g(f)) for f in (8, 9, 10, 11, 0, 1, 2, 3, 4, 5, 6, 7)],
                         *[feats_out(frh, frl, 4, tfr, evac_y(2, f)) for f in range(2)])

            def fourier():
                tf, ev = {}, {}
                for g in range(5):
                    if g < 4:
                        for tt in range(2):
                            t = mm([*txf, tcs, *busy, *([tf[g - 2]] if g >= 2 else [])], SC[g % 2][:, :],
                                   xf[tt][:, g * 128:g * 128 + 128], csT[:, tt, :], start=(tt == 0), stop=(tt == 1))
                        tf[g] = copy(act, [t, *ev.get(g - 2, busy)], T12[g % 2][:, :], SC[g % 2][:, :])
                    if g >= 1:
                        k = g - 1
                        o = OB[:, 0:256]
                        fr = ev.get("o", busy)
                        mm([tf[k], tcd, *fr], o, cdT[:, 0, :], T12[k % 2][:, 0:256], start=True, stop=False)
                        t = mm([], o, cdT[:, 1, :], T12[k % 2][:, 256:512], start=False, stop=True)
                        ev[k] = [t]
                        h = halves(frh[:, k, :], frl[:, k, :], o, [t, *busy])
                        ev["o"] = h
                        tfr.extend(h)
                    yield

            to2 = []
            def attention():
                done1 = everything()
                att_done.clear()
                scf, tpf, obf = [done1, done1], done1, done1
                ex, trn, wv, pv = {}, {}, {}, {}
                lw = st[:, 128:160].rearrange("p (h t c) -> p h t c", h=8, t=2)
                nm = st[:, 160:192].rearrange("p (h t c) -> p h t c", h=8, t=2)
                rr = st[:, 192:224].rearrange("p (h t c) -> p h t c", h=8, t=2)
                cc = st[:, 224:240].rearrange("p (h t) -> p h t", h=8)
                wtf = {}
                exd = {}

                def combine(u):
                    h, tt = u // 2, u % 2
                    b = dve.do([exd[u]], lambda e: e.reciprocal(rr[:, h, tt, :], lw[:, h, tt, :]), link=False)
                    c_ = dve.do([b, tlam], lambda e: e.tensor_scalar(
                        cc[:, h, tt:tt + 1], lw[:, h, tt, 0:1], neglam, rr[:, h, tt, 1:2], ALU.mult, ALU.mult),
                        link=False)
                    conv_some(1)
                    wv[u] = dve.do([c_, *trn.get(u - 2, done1)], lambda e: e.scalar_tensor_tensor(
                        W2[u % 2][:, :], E2[u % 2][:, 1, :], cc[:, h, tt:tt + 1], E2[u % 2][:, 0, :],
                        ALU.mult, ALU.add), link=False)

                yield
                for u in range(20):
                    if 0 <= u - 1 < 16:
                        combine(u - 1)
                    if 0 <= u - 2 < 16:
                        n = u - 2
                        h, tt = n // 2, n % 2
                        for k in range(2):
                            t = transposed([wv[n], *(tpf if tt == 0 else [])],
                                           TP[:, k * 256 + tt * 128:k * 256 + tt * 128 + 128],
                                           W2[n % 2][:, k * 128:k * 128 + 128])
                        trn[n] = [t]
                        if tt == 1:
                            a = copy(act, [t, *pv.get(h - 2, done1)], WT[h % 2][:, :, :],
                                     TP[:, :].rearrange("p (k s) -> p k s", k=2))
                            tpf = [a]
                            wtf[h] = a
                    if u >= 4 and u % 2 == 0:
                        h = (u - 4) // 2
                        for tt in range(2):
                            for k in range(2):
                                t = mm([wtf[h], *tv2, *obf],
                                       OB[:, (tt * 4 + h % 4) * 64:(tt * 4 + h % 4) * 64 + 64],
                                       WT[h % 2][:, k, tt * 128:tt * 128 + 128], v2[k][:, h * 64:h * 64 + 64],
                                       start=(k == 0), stop=(k == 1))
                        pv[h] = [t]
                        if h % 4 == 3:
                            for tt in range(2):
                                b = dve.do([t, *done1], lambda e, tt=tt, h=h: e.tensor_tensor(
                                    o2[:, tt, (h - 3) * 64:(h + 1) * 64].rearrange("p (h d) -> p h d", d=64),
                                    OB[:, tt * 256:tt * 256 + 256].rearrange("p (h d) -> p h d", d=64),
                                    bc(rr[:, h - 3:h + 1, tt, 0], [128, 4, 64], 2), ALU.mult))
                                to2.append(b)
                            obf = [b]
                    if u < 16:
                        h, tt = u // 2, u % 2
                        rg = slice((h % 4) * 32, (h % 4) * 32 + 32)
                        bk = SC[u % 2]
                        for c in range(2):
                            t = mm([*tT[0], *tT[1], *scf[u % 2]], bk[:, c * S:c * S + S],
                                   q2T[rg, c * 2 + h // 4, tt * 128:tt * 128 + 128], k2T[rg, c * 2 + h // 4, :])
                        s = bk[:, :].rearrange("p (c k) -> p c k", c=2)
                        conv_some(1)
                        m = dve.do([t], lambda e, s=s, h=h, tt=tt: e.tensor_reduce(
                            nm[:, h, tt, :], s, AXX, ALU.max, negate=True), link=False)
                        for c in range(2):
                            a = act.do([m, *([wv[u - 2]] if u >= 2 else done1)], lambda e, c=c, s=s, h=h, tt=tt, u=u:
                                       e.activation(E2[u % 2][:, c, :], s[:, c, :], ACT.Exp,
                                                    bias=nm[:, h, tt, c:c + 1], accum_out=lw[:, h, tt, c:c + 1]),
                                       link=False)
                        scf[u % 2] = [a]
                        exd[u] = a
                        if u == 15:
                            att_done.append(a)
                    conv_some(2)
                    yield

            tat, tcv, att_done = [], [], []

            def after_attention():
                o16 = o2[:, :, :].rearrange("p t (h d) -> p (t h) d", d=64)
                ss, rs = st[:, 240:256], st[:, 256:272]
                conv_some(len(todo))
                allcv = [t for f in range(4) for t in tconv[f]]
                for f in range(4):
                    t = mm([*allcv, *att_done] if f == 0 else [], SC[0][:, 0:S], ones, cv[:, f, :],
                           start=(f == 0), stop=(f == 3))
                a = act.do([*to2, *att_done], lambda e: e.activation(
                    osq[:, :], o2[:, :, :].rearrange("p t n -> p (t n)"), ACT.Square), link=False)
                pieces = [f for f in (8, 9, 10, 11, 0, 1, 2, 3, 4, 5, 6, 7) if f in tgm2]

                def sigmoids(n):
                    for _ in range(n):
                        if pieces:
                            f = pieces.pop(0)
                            tgs2[f] = act.do([tgm2[f]], lambda e: e.activation(
                                gm2[:, 2 * f:2 * f + 2, :], gm2[:, 2 * f:2 * f + 2, :], ACT.Sigmoid), link=False)

                m = dve.do([t], lambda e: e.scalar_tensor_tensor(
                    cv[:, :, :], bc(SC[0][:, 0:S], [128, 4, S], 1), -1.0 / 512, cv[:, :, :], ALU.mult, ALU.add))
                b = dve.do([a], lambda e: e.tensor_reduce(
                    ss, osq[:, :].rearrange("p (g d) -> p g d", d=64), AXX, ALU.add))
                z = (1 - li) ** 2
                c = scal(dve, [b], ss, ss, 1.0 / 64 / z, EPS / z, ALU.mult, ALU.add)
                d = power([c], rs, ss)
                q = act.do([m, *att_done], lambda e: e.activation(csq[:, :, :], cv[:, :, :], ACT.Square), link=False)
                sgv = smv("subg").rearrange("p (l d) -> p l d", l=2)[:, l, :]
                f1 = mul(dve, [a], o16, o16, bc(sgv, [128, 16, 64], 1))
                f2 = mul(dve, [d, f1], o16, o16, bc(rs, [128, 16, 64], 2))
                sigmoids(4)
                yield 8
                for tt in range(2):
                    for f in range(4):
                        t = mm([q, *att_done], SC[1][:, tt:tt + 1], csq[:, f, tt * 128:tt * 128 + 128],
                               ones[:, 0:1], start=(f == 0), stop=(f == 3))
                vs, vr_ = st[:, 272:274], st[:, 274:276]
                g = scal(dve, [t], vs, SC[1][:, 0:2], 1.0 / 512, EPS, ALU.mult, ALU.add)
                h = power([g], vr_, vs)
                ks = [copy(dve, [h], W2[tt][:, 0:128], vr_[:, tt:tt + 1].to_broadcast([128, 128]))
                      for tt in range(2)]
                sigmoids(4)
                yield 8
                for tt in range(2):
                    t = mm([ks[tt], t_sm], SC[0][:, tt * 128:tt * 128 + 128], W2[tt][:, 0:128], ident)
                tat.extend(to_halves_T(o2q, 4, ath, atl, [[f2], [f2]]))
                m = dve.do([t], lambda e: e.tensor_tensor(cv[:, :, :], cv[:, :, :], bc(SC[0][:, 0:S], [128, 4, S], 1),
                                                          ALU.mult))
                sigmoids(16)
                yield 5
                run(back)
                for f in range(4):
                    n = act.do([m], lambda e, f=f: e.activation(
                        csq[:, f, :], cv[:, f, :], ACT.Silu, scale=cvec[:, 1, f:f + 1], bias=cvec[:, 2, f:f + 1]),
                        link=False)
                tcv.extend(halves(cvh[:, :, :], cvl[:, :, :], csq[:, :, :], [n]))

            def front():
                for _ in fourier():
                    conv_some(6)
                    yield 0
                yield from attention()
                share[0] = 0.8
                direct.append(1)
                done2.extend(everything())
                yield from after_attention()

            weave(front(), back, 4)
            share[0] = 0.3
            done2.extend(everything())
            for n, (hi, lo, tk) in enumerate(((ath, atl, tat), (cvh, cvl, tcv))):
                run(chain(*[feats_out(hi, lo, 4, tk, evac_y(n, f)) for f in range(2)]))
            x_done = [[[], []], [[], []]]
            safe[0] = everything()
            n2 = Norm(4 + 2 * l)
            run(rows_out(mh2, ml2, tm2, add_to_x(0)))
            run(rows_held(mh2, ml2, tm2, add_to_x(512), tail_hooks(n2), True))
            share[0] = 0.8
            n2.scaled(1)
            n2.turned(1)
            share[0] = 0.8
            return ffn(False, n2.done, None if l else lambda: Norm(5), (1, 1, 0))

        for l in range(2):
            nm1 = layer(l, nm1)

        s_out = sem("s_out")
        for tt in range(2):
            t = sp.dma(sum(x_done[tt], []), s_out, 16 * (tt + 1),
                       lambda e, tt=tt: e.dma_start(out[tt * 128:(tt + 1) * 128, :], x[:, tt, :]))
        sp.wait([t])



def _pack(arrays):
    parts = []
    for name, layer, cs, k0, kk, _ in chunk_plan():
        w = arrays[name][layer]
        b = w[k0 * 128:(k0 + kk) * 128, :][:, np.asarray(cs)]
        parts.append(np.ascontiguousarray(b.reshape(kk, 128, len(cs)).transpose(1, 0, 2)).reshape(-1))
    return np.concatenate(parts)


def _small(a):
    f = np.float32
    sm = np.zeros((128, NSMALL), f)

    def put(name, v):
        o, n = SOFF[name]
        v = np.asarray(v)
        v = v.reshape(v.shape[0], -1)
        assert v.shape[1] == n, (name, v.shape)
        sm[:v.shape[0], o:o + n] = v

    def every(v):
        return np.broadcast_to(np.asarray(v).reshape(1, -1), (128, np.asarray(v).size))

    put("ident", np.eye(128, dtype=f))
    put("ones", np.ones((128, 128), f))
    put("mhalf", np.full((128, 16), -0.5, f))

    def rope(dim, theta):
        half = dim // 2
        inv = np.power(f(theta), -np.arange(half, dtype=f) / f(half)).astype(f)
        ang = (np.arange(S, dtype=f)[:, None] * inv[None, :]).astype(f).astype(np.float64)
        c, s = np.cos(ang).astype(f), np.sin(ang).astype(f)
        t = np.stack([np.concatenate([c, c], 1), np.concatenate([-s, s], 1)], 1)
        return t.reshape(2, 128, 2, dim).transpose(1, 0, 2, 3)

    put("ropen", rope(16, 500000.0))
    put("rope4", rope(8, 500000.0))
    ctab = np.ascontiguousarray(rope(128, 10000.0).reshape(128, 2, 256))
    seen = (np.arange(16)[None, :] * 16 + 31 <= np.arange(S)[:, None])
    put("madd", np.where(seen, 0.0, NEG).astype(f).reshape(2, 128, 16).transpose(1, 0, 2))
    put("m01", seen.astype(f).reshape(2, 128, 16).transpose(1, 0, 2))
    put("bm", (np.arange(120)[:, None] // 15 == np.arange(8)[None, :]).astype(f))
    put("w2k", a["cmp_w2_k"][0].reshape(2, 128, 64).transpose(1, 0, 2))
    put("w2v", a["cmp_w2_v"][0].reshape(2, 128, 64).transpose(1, 0, 2))
    put("pe", np.stack([a[n][0].reshape(16, 128).T for n in ("cmp_pe_k", "cmp_pe_v")], 1))
    fc = np.concatenate([a["ffn_conv_w"][0], a["ffn_conv_b"]], 0)
    put("fconv", fc.reshape(4, 2, NFT, 128).transpose(3, 2, 1, 0))
    put("lam", every(np.stack([a[n] for n in ("lambda_q1_2", "lambda_k1_2", "lambda_q2_2", "lambda_k2_2")], 1)))
    put("qkg", every(np.stack([a["qnorm_g_2"], a["knorm_g_2"]], 1)))
    put("subg", every(a["subln_g_2"]))
    put("cw", a["conv_w_2"].reshape(2, 31, 4, 128).transpose(3, 0, 2, 1))
    put("cvec", np.stack([a[n].reshape(2, 4, 128) for n in ("conv_b_2", "conv_ln_g_2", "conv_ln_b_2")], 1)
        .transpose(3, 0, 1, 2))
    put("bg", a["b_gate_2"].reshape(2, 24, 128).transpose(2, 0, 1))
    lg = np.log1p(-np.exp2(-5.0 - np.arange(4, dtype=np.float64)))
    j, i = np.arange(128)[:, None], np.arange(256)[None, :]
    full = np.concatenate([i - j, (i - j)[:, 0:128]], 1)[:, None, :]
    dec = np.where(full >= 0, np.exp(lg[None, :, None] * np.maximum(full, 0)), 0.0) * 128 ** -0.5
    n = np.arange(256)
    cs = 2 * np.pi * ((n[:, None] * n[None, :]) % 256) / 256
    cs = np.concatenate([np.cos(cs), np.sin(cs)], 1).astype(f).reshape(2, 128, 512).transpose(1, 0, 2)
    m = np.arange(128)
    cd = 2 * np.pi * ((m[:, None] * m[None, :]) % 128) / 128
    cd = (np.stack([np.cos(cd), -np.sin(cd)], 1) / math.sqrt(256 * 128)).astype(f)
    return sm, {"dec": dec.astype(f), "ctab": ctab, "cs": np.ascontiguousarray(cs), "cd": cd}


def kernel(**inputs):
    import concourse.bacc as _bacc
    from concourse import mybir as _mybir
    from concourse.bass_utils import run_bass_kernel_spmd as _run

    a = {k: np.asarray(v) for k, v in inputs.items()}
    sm, tabs = _small(a)
    rows = np.stack([a["norm_mix_w"][0], a["norm_ffn_w"][0], a["norm_final_w"],
                     a["norm1_g_2"][0], a["norm2_g_2"][0], a["norm1_g_2"][1], a["norm2_g_2"][1],
                     a["ret_gn_w"][0].reshape(-1)])
    arrays = {"in_w": _pack(a), "in_small": sm, "in_rows": rows,
              "in_x": np.ascontiguousarray(a["x"][0])}
    arrays.update({f"in_{k}": v for k, v in tabs.items()})
    nc = _bacc.Bacc("TRN2", target_bir_lowering=False, num_devices=1)
    d = {k: nc.dram_tensor(k, v.shape, _mybir.dt.from_np(v.dtype), kind="ExternalInput").ap()
         for k, v in arrays.items()}
    out = nc.dram_tensor("out_0", (S, D), _mybir.dt.float32, kind="ExternalOutput").ap()
    program(nc, d["in_w"], d["in_small"], {k: d[f"in_{k}"] for k in tabs}, d["in_rows"], d["in_x"], out)
    r = _run(nc, [arrays], core_ids=[0])
    return r.results[0]["out_0"].reshape(1, S, D)
```
